# Optimizing a Trainium2 kernel written in Bass

```python
import math, functools
import jax, jax.numpy as jnp
from jax import lax
import numpy as np

D_MODEL = 1024
BATCH = 1
SEQ = 1024
DEPTH = 1
DEC_BATCH = 8
DEC_SEQ = 1
PAST_LEN = 1024
PAGE_SIZE = 128

N_HEADS = 8
HEAD_DIM = 64
N_KV_HEADS = 2
HEADS_PER_GROUP = N_HEADS // N_KV_HEADS
ROT_DIM = HEAD_DIM // 4
ROPE_THETA = 500000.0
NSA_BLOCK = 64
NSA_TOP_N = 16
NSA_WINDOW = 512
PHI_HIDDEN = 2 * HEAD_DIM
NSA_Q_BLOCK = 32
WIN_Q_BLOCK = 128
D_CONV = 512
CONV_WIDTH = 3
D_FF = 2816
FFN_HALF = 0.5
NORM_EPS = 1e-6
NEG_INF = -1e30
Q_COLS = N_HEADS * HEAD_DIM
KV_COLS = 3 * 2 * N_KV_HEADS * HEAD_DIM
NSA_GATE_COLS = 3 * N_HEADS
CONV_COLS = 3 * D_CONV
MERGE_COLS = 2 * D_MODEL
IN_COLS = Q_COLS + KV_COLS + NSA_GATE_COLS + CONV_COLS + MERGE_COLS

kernel_name = 'hybrid_nsa_shortconv_macaron_step'

def rmsnorm(x, g):
    xf = x.astype(jnp.float32)
    y = xf * lax.rsqrt(jnp.mean(xf * xf, axis=-1, keepdims=True) + NORM_EPS)
    return y.astype(x.dtype) * g

def rope(x, pos):
    half = ROT_DIM // 2
    inv = jnp.power(ROPE_THETA, -jnp.arange(half, dtype=jnp.float32) * 2.0 / ROT_DIM)
    ang = pos.astype(jnp.float32)[:, None] * inv[None, :]
    ang = ang.reshape((1, pos.shape[0]) + (1,) * (x.ndim - 3) + (half,))
    cos = jnp.cos(ang).astype(x.dtype)
    sin = jnp.sin(ang).astype(x.dtype)
    x1 = x[..., :half]
    x2 = x[..., half:ROT_DIM]
    return jnp.concatenate([x1 * cos - x2 * sin, x2 * cos + x1 * sin, x[..., ROT_DIM:]], axis=-1)

def swiglu(a, w_gu, w_down):
    gu = a @ w_gu
    return (jax.nn.silu(gu[..., :D_FF]) * gu[..., D_FF:]) @ w_down

def project(a, pos, w_in):
    B, T, _ = a.shape
    z = a @ w_in
    o1 = Q_COLS
    o2 = o1 + KV_COLS
    o3 = o2 + NSA_GATE_COLS
    o4 = o3 + CONV_COLS
    q = rope(z[..., :o1].reshape(B, T, N_KV_HEADS, HEADS_PER_GROUP, HEAD_DIM), pos)
    kv = z[..., o1:o2].reshape(B, T, 3, 2, N_KV_HEADS, HEAD_DIM)
    kv = jnp.stack([rope(kv[:, :, :, 0], pos), kv[:, :, :, 1]], axis=3)
    nsa_g = jax.nn.sigmoid(z[..., o2:o3]).reshape(B, T, 3, N_KV_HEADS, HEADS_PER_GROUP)
    conv_h = z[..., o3:o3 + D_CONV]
    conv_b = z[..., o3 + D_CONV:o3 + 2 * D_CONV]
    conv_c = z[..., o3 + 2 * D_CONV:o4]
    merge_g = jax.nn.sigmoid(z[..., o4:]).reshape(B, T, 2, D_MODEL)
    return q, kv, nsa_g, conv_h, conv_b, conv_c, merge_g

def compress(xb, pe, w1, b1, w2):
    B, NB = xb.shape[:2]
    xb = xb.transpose(0, 1, 3, 2, 4) + pe
    h = jax.nn.silu(xb.reshape(B, NB, N_KV_HEADS, NSA_BLOCK * HEAD_DIM) @ w1 + b1)
    return h @ w2

def nsa_global(q, q_pos, cmp_kv, slc_kv, phi_pe, phi_w1, phi_b1, phi_w2):
    B, Tq = q.shape[:2]
    Tk = cmp_kv.shape[1]
    pad_k = (-Tk) % NSA_BLOCK
    kpad = ((0, 0), (0, pad_k), (0, 0), (0, 0), (0, 0))
    cmp_kv = jnp.pad(cmp_kv, kpad)
    slc_kv = jnp.pad(slc_kv, kpad)
    NB = (Tk + pad_k) // NSA_BLOCK
    cb = cmp_kv.reshape(B, NB, NSA_BLOCK, 2, N_KV_HEADS, HEAD_DIM)
    kc = compress(cb[:, :, :, 0], phi_pe[0], phi_w1[0], phi_b1[0], phi_w2[0])
    vc = compress(cb[:, :, :, 1], phi_pe[1], phi_w1[1], phi_b1[1], phi_w2[1])
    sb = slc_kv.reshape(B, NB, NSA_BLOCK, 2, N_KV_HEADS, HEAD_DIM).transpose(0, 4, 1, 2, 3, 5)
    n_sel = min(NSA_TOP_N, NB)
    qb = min(NSA_Q_BLOCK, Tq)
    nq = -(-Tq // qb)
    pad_q = nq * qb - Tq
    qs = jnp.pad(q, ((0, 0), (0, pad_q), (0, 0), (0, 0), (0, 0)))
    qs = qs.reshape(B, nq, qb, N_KV_HEADS, HEADS_PER_GROUP, HEAD_DIM).transpose(1, 0, 2, 3, 4, 5)
    ps = jnp.pad(q_pos, (0, pad_q), mode='edge').reshape(nq, qb)
    scale = HEAD_DIM ** -0.5
    blk = jnp.arange(NB, dtype=jnp.int32)
    offs = jnp.arange(NSA_BLOCK, dtype=jnp.int32)
    gather = jax.vmap(jax.vmap(lambda blocks, idx: blocks[idx]))

    def one_block(args):
        qq, pp = args
        s = jnp.einsum('btghd,bngd->bghtn', qq, kc).astype(jnp.float32) * scale
        cvalid = (blk[None, :] + 1) * NSA_BLOCK <= pp[:, None] + 1
        s = jnp.where(cvalid, s, NEG_INF)
        pc = jnp.where(cvalid, jax.nn.softmax(s, axis=-1), 0.0)
        o_cmp = jnp.einsum('bghtn,bngd->btghd', pc.astype(vc.dtype), vc)
        imp = pc.sum(axis=2)
        cur = (pp // NSA_BLOCK)[:, None]
        forced = (blk[None, :] == 0) | (blk[None, :] == cur) | (blk[None, :] == cur - 1)
        avail = blk[None, :] * NSA_BLOCK <= pp[:, None]
        imp = jnp.where(forced, HEADS_PER_GROUP + 1.0, imp)
        imp = jnp.where(avail, imp, -1.0)
        top_v, top_i = lax.top_k(imp, n_sel)
        g = gather(sb, top_i)
        s2 = jnp.einsum('btghd,bgtnld->bghtnl', qq, g[..., 0, :]).astype(jnp.float32) * scale
        kpos = top_i[..., None] * NSA_BLOCK + offs
        m2 = (top_v >= 0.0)[..., None] & (kpos <= pp[None, None, :, None, None])
        s2 = jnp.where(m2[:, :, None], s2, NEG_INF)
        p2 = jax.nn.softmax(s2.reshape(s2.shape[:4] + (n_sel * NSA_BLOCK,)), axis=-1).reshape(s2.shape)
        o_slc = jnp.einsum('bghtnl,bgtnld->btghd', p2.astype(g.dtype), g[..., 1, :])
        return o_cmp, o_slc

    o_cmp, o_slc = lax.map(one_block, (qs, ps))

    def unblock(o):
        o = o.transpose(1, 0, 2, 3, 4, 5).reshape(B, nq * qb, N_KV_HEADS, HEADS_PER_GROUP, HEAD_DIM)
        return o[:, :Tq]

    return unblock(o_cmp), unblock(o_slc)

def window_attn(qb, kb, vb, qpos, kpos):
    s = jnp.einsum('bntghd,bnkgd->bnghtk', qb, kb).astype(jnp.float32) * (HEAD_DIM ** -0.5)
    diff = qpos[:, :, None] - kpos[:, None, :]
    m = (diff >= 0) & (diff < NSA_WINDOW) & (kpos[:, None, :] >= 0)
    s = jnp.where(m[None, :, None, None], s, NEG_INF)
    p = jax.nn.softmax(s, axis=-1)
    return jnp.einsum('bnghtk,bnkgd->bntghd', p.astype(vb.dtype), vb)

def window_attn_banded(q, win_kv, pos):
    B, S = q.shape[:2]
    wb = WIN_Q_BLOCK if S % WIN_Q_BLOCK == 0 else S
    nb = S // wb
    wpad = jnp.pad(win_kv, ((0, 0), (NSA_WINDOW, 0), (0, 0), (0, 0), (0, 0)))
    idx = jnp.arange(nb, dtype=jnp.int32)[:, None] * wb + jnp.arange(NSA_WINDOW + wb, dtype=jnp.int32)[None, :]
    g = wpad[:, idx]
    kpos = idx - NSA_WINDOW
    o = window_attn(q.reshape(B, nb, wb, N_KV_HEADS, HEADS_PER_GROUP, HEAD_DIM),
                    g[:, :, :, 0], g[:, :, :, 1], pos.reshape(nb, wb), kpos)
    return o.reshape(B, S, N_KV_HEADS, HEADS_PER_GROUP, HEAD_DIM)

def token_mixer(a, pos, past, mix_w):
    w_in, phi_pe, phi_w1, phi_b1, phi_w2, w_attn_up, conv_w, w_conv_out, w_out = mix_w
    B, T, _ = a.shape
    q, kv, nsa_g, conv_h, conv_b, conv_c, merge_g = project(a, pos, w_in)
    cmp_new, slc_new, win_new = kv[:, :, 0], kv[:, :, 1], kv[:, :, 2]
    if past is None:
        cmp_full, slc_full = cmp_new, slc_new
        o_win = window_attn_banded(q, win_new, pos)
        win_keep = min(NSA_WINDOW, T)
        new_win = win_new[:, T - win_keep:]
        conv_buf = jnp.zeros((B, CONV_WIDTH - 1, D_CONV), a.dtype)
    else:
        cmp_past, slc_past, win_buf, conv_buf, past_len = past
        cmp_full = jnp.concatenate([cmp_past, cmp_new], axis=1)
        slc_full = jnp.concatenate([slc_past, slc_new], axis=1)
        nw = win_buf.shape[1]
        keys = jnp.concatenate([win_buf, win_new], axis=1)
        kpos = past_len - nw + jnp.arange(nw + T, dtype=jnp.int32)
        o_win = window_attn(q[:, None], keys[:, None, :, 0], keys[:, None, :, 1], pos[None], kpos[None])[:, 0]
        win_keep = min(NSA_WINDOW, past_len + T)
        new_win = keys[:, keys.shape[1] - win_keep:]
    o_cmp, o_slc = nsa_global(q, pos, cmp_full, slc_full, phi_pe, phi_w1, phi_b1, phi_w2)
    o_att = (nsa_g[:, :, 0, :, :, None] * o_cmp + nsa_g[:, :, 1, :, :, None] * o_slc
             + nsa_g[:, :, 2, :, :, None] * o_win)
    attn_out = o_att.reshape(B, T, Q_COLS) @ w_attn_up
    u = conv_c * conv_h
    u_ext = jnp.concatenate([conv_buf, u], axis=1)
    y = conv_w[0] * u_ext[:, 0:T]
    for j in range(1, CONV_WIDTH):
        y = y + conv_w[j] * u_ext[:, j:j + T]
    conv_out = (conv_b * y) @ w_conv_out
    new_conv = u_ext[:, u_ext.shape[1] - (CONV_WIDTH - 1):]
    merged = merge_g[:, :, 0] * attn_out + merge_g[:, :, 1] * conv_out
    return merged @ w_out, (cmp_new, slc_new, new_win, new_conv)

def decoder_layer(x, c, pos, past, mix_w, w_ada, b_ada, g_norm, w_ffn_gu, w_ffn_down):
    B, _, D = x.shape
    mod = (jax.nn.silu(c) @ w_ada + b_ada).reshape(B, 9, 1, D)
    a = rmsnorm(x, g_norm[0]) * (1.0 + mod[:, 1]) + mod[:, 0]
    x = x + FFN_HALF * mod[:, 2] * rmsnorm(swiglu(a, w_ffn_gu[0], w_ffn_down[0]), g_norm[1])
    a = rmsnorm(x, g_norm[2]) * (1.0 + mod[:, 4]) + mod[:, 3]
    m, states = token_mixer(a, pos, past, mix_w)
    x = x + mod[:, 5] * rmsnorm(m, g_norm[3])
    a = rmsnorm(x, g_norm[4]) * (1.0 + mod[:, 7]) + mod[:, 6]
    x = x + FFN_HALF * mod[:, 8] * rmsnorm(swiglu(a, w_ffn_gu[1], w_ffn_down[1]), g_norm[5])
    return x, states

def setup_inputs(seed: int = 0) -> dict:
    key = jax.random.key(seed)
    ks = jax.random.split(key, 24)
    n_pages = PAST_LEN // PAGE_SIZE
    n_phys = (DEC_BATCH * n_pages * 5) // 4
    win_keep = min(NSA_WINDOW, PAST_LEN)

    def nrm(k, shape, s):
        return jax.random.normal(k, shape, jnp.float32) * s

    page_table = jax.random.permutation(ks[8], n_phys)[:DEC_BATCH * n_pages].reshape(DEC_BATCH, n_pages).astype(jnp.int32)
    return {
        'x_prompt': nrm(ks[0], (BATCH, SEQ, D_MODEL), 1.0),
        'x_sample': nrm(ks[1], (DEC_BATCH, DEC_SEQ, D_MODEL), 1.0),
        'c_prompt': nrm(ks[2], (BATCH, D_MODEL), 1.0),
        'c_sample': nrm(ks[3], (DEC_BATCH, D_MODEL), 1.0),
        'cache_cmp_kv': nrm(ks[4], (DEPTH, n_phys, PAGE_SIZE, 2, N_KV_HEADS, HEAD_DIM), 1.0),
        'cache_slc_kv': nrm(ks[5], (DEPTH, n_phys, PAGE_SIZE, 2, N_KV_HEADS, HEAD_DIM), 1.0),
        'state_win_kv': nrm(ks[6], (DEPTH, DEC_BATCH, win_keep, 2, N_KV_HEADS, HEAD_DIM), 1.0),
        'state_conv': nrm(ks[7], (DEPTH, DEC_BATCH, CONV_WIDTH - 1, D_CONV), 1.0),
        'page_table': page_table,
        'w_ada': nrm(ks[9], (DEPTH, D_MODEL, 9 * D_MODEL), 0.5 * D_MODEL ** -0.5),
        'b_ada': nrm(ks[10], (DEPTH, 9 * D_MODEL), 0.02),
        'g_norm': 1.0 + nrm(ks[11], (DEPTH, 6, D_MODEL), 0.02),
        'w_ffn_gu': nrm(ks[12], (DEPTH, 2, D_MODEL, 2 * D_FF), D_MODEL ** -0.5),
        'w_ffn_down': nrm(ks[13], (DEPTH, 2, D_FF, D_MODEL), D_FF ** -0.5),
        'w_in': nrm(ks[14], (DEPTH, D_MODEL, IN_COLS), D_MODEL ** -0.5),
        'phi_pe': nrm(ks[15], (DEPTH, 2, NSA_BLOCK, HEAD_DIM), 0.02),
        'phi_w1': nrm(ks[16], (DEPTH, 2, NSA_BLOCK * HEAD_DIM, PHI_HIDDEN), (NSA_BLOCK * HEAD_DIM) ** -0.5),
        'phi_b1': nrm(ks[17], (DEPTH, 2, PHI_HIDDEN), 0.02),
        'phi_w2': nrm(ks[18], (DEPTH, 2, PHI_HIDDEN, HEAD_DIM), PHI_HIDDEN ** -0.5),
        'w_attn_up': nrm(ks[19], (DEPTH, Q_COLS, D_MODEL), Q_COLS ** -0.5),
        'conv_w': nrm(ks[20], (DEPTH, CONV_WIDTH, D_CONV), CONV_WIDTH ** -0.5),
        'w_conv_out': nrm(ks[21], (DEPTH, D_CONV, D_MODEL), D_CONV ** -0.5),
        'w_out': nrm(ks[22], (DEPTH, D_MODEL, D_MODEL), D_MODEL ** -0.5),
    }

def reference(x_prompt, x_sample, c_prompt, c_sample, cache_cmp_kv, cache_slc_kv, state_win_kv, state_conv,
              page_table, w_ada, b_ada, g_norm, w_ffn_gu, w_ffn_down, w_in, phi_pe, phi_w1, phi_b1, phi_w2,
              w_attn_up, conv_w, w_conv_out, w_out):
    n_dec = x_sample.shape[0]
    n_pages = page_table.shape[1]
    past_len = n_pages * PAGE_SIZE
    pos_p = jnp.arange(x_prompt.shape[1], dtype=jnp.int32)
    pos_s = past_len + jnp.arange(x_sample.shape[1], dtype=jnp.int32)
    h_p, h_s = x_prompt, x_sample
    st_p = [[], [], [], []]
    st_s = [[], [], [], []]
    for l in range(DEPTH):
        mix_w = (w_in[l], phi_pe[l], phi_w1[l], phi_b1[l], phi_w2[l], w_attn_up[l], conv_w[l], w_conv_out[l], w_out[l])
        h_p, sp = decoder_layer(h_p, c_prompt, pos_p, None, mix_w, w_ada[l], b_ada[l], g_norm[l], w_ffn_gu[l], w_ffn_down[l])
        cmp_past = cache_cmp_kv[l][page_table].reshape(n_dec, past_len, 2, N_KV_HEADS, HEAD_DIM)
        slc_past = cache_slc_kv[l][page_table].reshape(n_dec, past_len, 2, N_KV_HEADS, HEAD_DIM)
        past = (cmp_past, slc_past, state_win_kv[l], state_conv[l], past_len)
        h_s, ss = decoder_layer(h_s, c_sample, pos_s, past, mix_w, w_ada[l], b_ada[l], g_norm[l], w_ffn_gu[l], w_ffn_down[l])
        for i in range(4):
            st_p[i].append(sp[i])
            st_s[i].append(ss[i])
    cmp_kv_prompt = jnp.stack(st_p[0], axis=0)
    slc_kv_prompt = jnp.stack(st_p[1], axis=0)
    win_kv_prompt = jnp.stack(st_p[2], axis=0)
    conv_prompt = jnp.stack(st_p[3], axis=0)
    cmp_kv_sample = jnp.stack(st_s[0], axis=0)
    slc_kv_sample = jnp.stack(st_s[1], axis=0)
    win_kv_sample = jnp.stack(st_s[2], axis=0)
    conv_sample = jnp.stack(st_s[3], axis=0)
    return (h_p, h_s, cmp_kv_prompt, slc_kv_prompt, win_kv_prompt, conv_prompt,
            cmp_kv_sample, slc_kv_sample, win_kv_sample, conv_sample)


_drawn_inputs = setup_inputs


def setup_inputs(seed=0):
    import zlib

    import numpy as np

    out = dict(_drawn_inputs(seed))
    spreads = {}
    factors = {'cache_slc_kv': 7.41, 'phi_pe': 8.0, 'phi_b1': 8.0}
    for name, (base, spread) in spreads.items():
        noise = np.random.default_rng([zlib.crc32(name.encode()), seed]).standard_normal(out[name].shape)
        drawn = base * np.exp(spread * noise) if base else spread * noise
        out[name] = __import__('jax').numpy.asarray(drawn.astype(out[name].dtype))
    for name, factor in factors.items():
        out[name] = (out[name] * factor).astype(out[name].dtype)
    return out
```

```python
from contextlib import ExitStack

import numpy as np

import concourse.bass as bass
from concourse import mybir

ACT = mybir.ActivationFunctionType
ALU = mybir.AluOpType
F32 = mybir.dt.float32
F16 = mybir.dt.float16
BF16 = mybir.dt.bfloat16
I32 = mybir.dt.int32
AX_X = mybir.AxisListType.X

P = 128
D = 1024
KD = D // P
SEQ = 1024
NDEC = 8
T = SEQ + NDEC
NJ = 3
TJ = T // NJ
TT = SEQ // P
NSEQ = 1 + NDEC
DFF = 2816
KF = DFF // P
NH, HD, NG, HPG = 8, 64, 2, 4
PAST, PAGE = 1024, 128
NPAGE = PAST // PAGE
NPHYS = 80
BLK = 64
NB = SEQ // BLK
WIN = 512
HID = 128
DCONV = 512
KC = DCONV // P
QC, KVC, GC = NH * HD, 6 * NG * HD, 3 * NH
CONV0 = QC + KVC + GC
MERGE0 = CONV0 + 3 * DCONV
WS = 64.0
IWS = 1.0 / WS
SLAB = 11 * P
EPS = 1e-6
NEG = -1e30
NMOD = 9 * KD
NSTART = 2 * KD


def shape_constants():
    q = np.arange(P)[:, None]
    k = np.arange(P)[None, :]
    parts = {}
    parts["ident"] = (q == k).astype(np.float32)
    parts["mean"] = np.full((P, P), 1.0 / D, np.float32)
    pos = np.arange(SEQ).reshape(TT, P).T[:, :, None]
    parts["cmpok"] = ((np.arange(NB)[None, None, :] + 1) * BLK <= pos + 1).astype(np.float32).reshape(P, TT * NB)
    half = HD // 8
    inv = np.power(np.float32(500000.0), -np.arange(half, dtype=np.float32) * np.float32(2.0) / np.float32(2 * half))
    allpos = np.full((P, TT + 1), PAST, np.float32)
    allpos[:, :TT] = np.arange(SEQ, dtype=np.float32).reshape(TT, P).T
    ang = allpos[:, :, None] * inv[None, None, :].astype(np.float32)
    parts["cos"] = np.cos(ang).astype(np.float32).reshape(P, -1)
    parts["sin"] = np.sin(ang).astype(np.float32).reshape(P, -1)
    row = np.arange(P)[:, None]
    parts["seqmask"] = (row // NH == np.arange(NDEC)[None, :]).astype(np.float32)
    parts["headmask"] = (row // NB == np.arange(NH)[None, :]).astype(np.float32)
    parts["group"] = (row // HPG == np.arange(NDEC * NH)[None, :] // HPG).astype(np.float32)
    parts["spread"] = (row == np.arange(P)[None, :] % NB).astype(np.float32)
    parts["order"] = np.broadcast_to(np.arange(1, NB - 1, dtype=np.float32), (P, NB - 2))
    parts["seqrep"] = (row == np.arange(NDEC * NH)[None, :] // NH).astype(np.float32)
    parts["ownhead"] = (row % NH == np.arange(NH)[None, :]).astype(np.float32)
    parts["blockrow"] = ((row % 2) * 16 + np.arange(16)[None, :]).astype(np.float32)
    parts["eps"] = np.full((P, 1), EPS, np.float32)
    at, where = 0, {}
    for n, a in parts.items():
        where[n] = (at, at + a.shape[1])
        at += a.shape[1]
    return np.concatenate(list(parts.values()), axis=1).astype(np.float32), where


def mask_constants():
    q, k = np.arange(P)[:, None], np.arange(P)[None, :]
    return np.concatenate([np.where(k > q, NEG, 0.0), np.where(k <= q, NEG, 0.0)], axis=1).astype(np.float32)


def third(j):
    return j * TJ, (j + 1) * TJ


def build_program(nc, I, O):
    consts, CW = shape_constants()
    NCONST = consts.shape[1]

    cursor = [16512]

    def place(name, shape, dt, size=None):
        n = int(np.prod(shape[1:])) * (2 if dt in (F16, BF16) else 4)
        n = (n + 31) // 32 * 32
        t = nc.alloc_sbuf_tensor_at(name, shape, dt, offset=cursor[0])
        cursor[0] += n
        assert cursor[0] <= 229344, (name, cursor[0])
        return t

    cst = place("cst", [P, NCONST], F32)
    identh = place("identh", [P, P], F16)
    identb = place("identb", [P, P], BF16)
    maskb = place("maskb", [P, 2, P], BF16)
    x = place("x", [P, KD, T], F32)
    modv = place("modv", [P, NMOD, NSEQ], F32)
    scaleA = place("scaleA", [P, 3, KD, NSEQ], F32)
    gateC = place("gateC", [P, 3, KD, NSEQ], F32)
    par1 = place("par1", [P, 120], F32)
    par2 = place("par2", [P, 78], F32)
    csh = place("csh", [P, KD, NSEQ], F16)
    csl = place("csl", [P, KD, NSEQ], F16)
    rs_at = cursor[0]
    rs = place("rs", [P, NJ, TJ], F32)
    sq_at = cursor[0]
    sq = place("sq", [P, NJ, TJ], F32)
    tmp = place("tmp", [P, 2, TJ], F32)
    decd = place("decd", [P, 3, KD, NDEC], F32)
    stage = place("stage", [P, 2, SLAB], F32)
    whi = place("whi", [P, 4, SLAB], F16)
    wlo = place("wlo", [P, 4, SLAB], F16)
    a_at = cursor[0]
    ahi = place("ahi", [P, KD, T], F16)
    alo = place("alo", [P, KD, T], F16)
    y = nc.alloc_sbuf_tensor_at("y", [P, KD, T], F32, offset=a_at)
    free_at = cursor[0]

    hhi = place("hhi", [P, KF, T], F16)
    hlo = place("hlo", [P, KF, T], F16)
    sg = nc.alloc_sbuf_tensor_at("sg", [P, NJ, TJ], F32, offset=sq_at)
    h32 = nc.alloc_sbuf_tensor_at("h32", [P, NJ, TJ], F32, offset=rs_at)
    acc = nc.alloc_sbuf_tensor_at("acc", [P, NJ, TJ], F32, offset=rs_at)
    cursor[0] = free_at
    xrow = place("xrow", [P, 4, D], F32)
    crow = place("crow", [NSEQ, 2, D], F32)
    prow = place("prow", [P, 2, P], F32)
    mrow = place("mrow", [P, 2, P], F32)

    banks8 = nc.alloc_psum_tensor("banks8", [P, 8, 512], F32)
    bank = [banks8[:, n, :] for n in range(8)]

    def const(name, rows=P):
        a, b = CW[name]
        return cst[0:rows, a:b]

    sem = {}

    def S(name):
        if name not in sem:
            sem[name] = nc.alloc_semaphore(name)
        return sem[name]

    total = {}

    def count(name, n=1):
        total[name] = total.get(name, 0) + n
        return total[name]

    def at(name):
        return total.get(name, 0)

    stage_full = [S("stage_full0"), S("stage_full1")]
    slab_split, slab_used, slab_hi, slab_scaled = S("slab_split"), S("slab_used"), S("slab_hi"), S("slab_scaled")

    def slab_parts(u, kk, w=P):
        return (whi[:, u, 0:kk * w].rearrange("p (k n) -> p k n", k=kk),
                wlo[:, u, 0:kk * w].rearrange("p (k n) -> p k n", k=kk))

    def standing(eng, s, name):
        if not isinstance(s, int):
            eng.sem_inc(S(name), 1)

    def load_slab(sp, s, v, src, kk, w=P, first=False):
        if not first:
            sp.wait_ge(slab_split, s - 1)
            standing(sp, s, "loads_let_go")
        sp.dma_start(stage[:, v % 2, 0:kk * w].rearrange("p (k n) -> p k n", k=kk), src)\
          .then_inc(stage_full[v % 2], 16)

    def arrived(eng, s0, i4, v):
        eng.wait_ge(stage_full[v % 2], i4 * 8 + (s0 // 2 + v // 2 + 1) * 16)

    def split_slab(pool, s0, i4, v, n):
        s = i4 + (s0 + v)
        arrived(pool, s0, i4, v)
        pool.wait_ge(slab_used, s - 3)
        standing(pool, s, "splits_let_go")
        st, hi, lo = stage[:, v % 2, 0:n], whi[:, v % 4, 0:n], wlo[:, v % 4, 0:n]
        pool.tensor_scalar(st, st, WS, 1.0, ALU.mult, ALU.mult).then_inc(slab_scaled, 1)
        pool.wait_ge(slab_scaled, s + (1 - NSTART))
        standing(pool, s, "splits_let_go")
        pool.tensor_scalar(hi, st, 1.0, 1.0, ALU.mult, ALU.mult).then_inc(slab_hi, 1)
        pool.wait_ge(slab_hi, s + (1 - NSTART))
        pool.tensor_tensor(lo, st, hi, ALU.subtract).then_inc(slab_split, 1)

    def product(pe, out, w_hi, w_lo, a_hi, a_lo, start, stop):
        pe.matmul(out, w_hi, a_hi, start=start, stop=False)
        pe.matmul(out, w_hi, a_lo, start=False, stop=False)
        return pe.matmul(out, w_lo, a_hi, start=False, stop=stop)

    block_cm = nc.Block()
    block = block_cm.__enter__()

    wada = I["w_ada"][0]

    def ada_src(q):
        return wada[:, bass.ds(q * P, P)].rearrange("(k p) n -> p k n", p=P)

    x_prompt, x_sample = I["x_prompt"][0], I["x_sample"].rearrange("b o d -> (b o) d")

    @block.sync
    def _(sp):
        sp.dma_start(crow[0:1, 0, :], I["c_prompt"]).then_inc(S("c_in"), 16)
        sp.dma_start(crow[1:NSEQ, 0, :], I["c_sample"]).then_inc(S("c_in"), 16)
        sp.dma_start(cst[:], I["consts"]).then_inc(S("const_in"), 16)
        sp.dma_start(mrow[:].rearrange("p a n -> p (a n)"), I["masks"]).then_inc(S("mask_in"), 16)
        sp.dma_start(prow[0:72, 0, :], I["b_ada"][0].rearrange("(q p) -> q p", p=P)).then_inc(S("par_in"), 16)
        sp.dma_start(prow[72:120, 0, :], I["g_norm"][0].rearrange("n (c p) -> (n c) p", p=P)).then_inc(S("par_in"), 16)
        for s in range(2):
            load_slab(sp, s, s, ada_src(s), KD, first=True)
        sp.dma_start(prow[0:12, 1, :], I["conv_w"][0].rearrange("j (c p) -> (j c) p", p=P)).then_inc(S("par_in"), 16)
        sp.dma_start(prow[12:76, 1, :], I["phi_pe"][0].rearrange("v (m l) d -> (v m) (l d)", l=2)).then_inc(S("par_in"), 16)
        sp.dma_start(prow[76:78, 1, :], I["phi_b1"][0]).then_inc(S("par_in"), 16)
        for s in range(2, NSTART):
            load_slab(sp, s, s % 4, ada_src(s), KD)

    @block.scalar
    def _(act):
        for t in range(4):
            act.dma_start(xrow[:, t, :], x_prompt[t * P:(t + 1) * P, :]).then_inc(S(f"xrow_in{t}"), 16)
        act.wait_ge(S("c_in"), 32)
        act.activation(crow[:, 1, :], crow[:, 0, :], ACT.Silu).then_inc(S("c_silu"), 1)
        for t in range(TT + 1):
            for s in (2 * t, 2 * t + 1):
                if s < NSTART:
                    act.wait_ge(stage_full[s % 2], 16 * (s // 2 + 1))
                    if s >= 4:
                        act.wait_ge(slab_used, s - 3)
                    act.activation(whi[:, s % 4, 0:KD * P], stage[:, s % 2, 0:KD * P], ACT.Copy, scale=WS)\
                       .then_inc(S("start_hi"), 1)
            n = P if t < TT else NDEC
            act.wait_ge(S("xT_mm"), 2 * t + 2)
            act.activation(x[:, 4:8, t * P:t * P + n],
                           bank[2 * (t % 2) + 1].rearrange("p (c n) -> p c n", c=4)[:, :, 0:n], ACT.Copy)\
               .then_inc(S("xT_b"), 1)
            if t + 4 <= TT:
                act.wait_ge(S("xT_mm"), 2 * t + 2)
                if t + 4 < TT:
                    act.dma_start(xrow[:, t % 4, :], x_prompt[(t + 4) * P:(t + 5) * P, :]).then_inc(S(f"xrow_in{t % 4}"), 16)
                else:
                    act.dma_start(xrow[0:NDEC, t % 4, :], x_sample).then_inc(S(f"xrow_in{t % 4}"), 16)
            for s in (2 * t, 2 * t + 1):
                if s < NSTART:
                    act.wait_ge(slab_used, s + 1)
                    act.activation(modv[:, s, :], bank[6 + s % 2][:, 0:NSEQ], ACT.Identity,
                                   bias=par1[:, s:s + 1], scale=IWS).then_inc(S("mod_done"), 1)
    count("mod_done", NSTART)

    @block.tensor
    def _(pe):
        pe.wait_ge(S("const_in"), 16)
        pe.wait_ge(S("par_in"), 80)
        pe.transpose(bank[4][:, 0:120], prow[0:120, 0, :], const("ident", 120)[:, 0:120]).then_inc(S("parT"), 1)
        pe.transpose(bank[4][:, 128:128 + 78], prow[0:78, 1, :], const("ident", 78)[:, 0:78]).then_inc(S("parT"), 1)
        pe.wait_ge(S("c_silu"), 1)
        for k in range(KD):
            last = pe.transpose(bank[5][:, 16 * k:16 * k + NSEQ], crow[:, 1, k * P:(k + 1) * P],
                                const("ident", NSEQ)[:, 0:NSEQ])
        last.then_inc(S("cT"), 1)
        for t in range(TT + 1):
            n = P if t < TT else NDEC
            pe.wait_ge(S(f"xrow_in{t % 4}"), 16 * (t // 4 + 1))
            if t >= 2:
                pe.wait_ge(S("xT_a"), t - 1)
                pe.wait_ge(S("xT_b"), t - 1)
            for half in range(2):
                b = bank[2 * (t % 2) + half]
                for c in range(4):
                    k = 4 * half + c
                    last = pe.transpose(b[:, c * P:c * P + n], xrow[0:n, t % 4, k * P:(k + 1) * P],
                                        const("ident", n)[:, 0:n])
                last.then_inc(S("xT_mm"), 1)
            for s in (2 * t, 2 * t + 1):
                if s < NSTART:
                    if s == 0:
                        pe.wait_ge(S("cs_lo"), 1)
                    pe.wait_ge(slab_split, s + 1)
                    if s >= 2:
                        pe.wait_ge(S("mod_done"), s - 1)
                    w1, w2 = slab_parts(s % 4, KD)
                    for k in range(KD):
                        last = product(pe, bank[6 + s % 2][:, 0:NSEQ], w1[:, k, :], w2[:, k, :],
                                       csh[:, k, :], csl[:, k, :], k == 0, k == KD - 1)
                    last.then_inc(slab_used, 1)

    @block.vector
    def _(dve):
        dve.wait_ge(S("const_in"), 16)
        dve.tensor_copy(identh[:], const("ident")).then_inc(S("par"), 1)
        dve.tensor_copy(identb[:], const("ident")).then_inc(S("par"), 1)
        dve.wait_ge(S("mask_in"), 16)
        dve.tensor_copy(maskb[:], mrow[:]).then_inc(S("par"), 1)
        dve.wait_ge(S("parT"), 2)
        dve.tensor_copy(par1[:], bank[4][:, 0:120]).then_inc(S("par"), 1)
        dve.tensor_copy(par2[:], bank[4][:, 128:128 + 78]).then_inc(S("par"), 1)
        dve.wait_ge(S("cT"), 1)
        ct = bank[5][:, 0:16 * KD].rearrange("p (k n) -> p k n", n=16)[:, :, 0:NSEQ]
        dve.tensor_copy(csh[:], ct).then_inc(S("cs_hi"), 1)
        dve.wait_ge(S("cs_hi"), 1)
        dve.tensor_tensor(csl[:], ct, csh[:], ALU.subtract).then_inc(S("cs_lo"), 1)
        for t in range(TT + 1):
            n = P if t < TT else NDEC
            for s in (2 * t, 2 * t + 1):
                if s < NSTART:
                    dve.wait_ge(S("start_hi"), s + 1)
                    dve.scalar_tensor_tensor(out=wlo[:, s % 4, 0:KD * P], in0=stage[:, s % 2, 0:KD * P], scalar=WS,
                                             in1=whi[:, s % 4, 0:KD * P], op0=ALU.mult, op1=ALU.subtract)\
                       .then_inc(slab_split, 1)
            dve.wait_ge(S("xT_mm"), 2 * t + 1)
            dve.tensor_copy(x[:, 0:4, t * P:t * P + n],
                            bank[2 * (t % 2)].rearrange("p (c n) -> p c n", c=4)[:, :, 0:n])\
               .then_inc(S("xT_a"), 1)

    G = par1[:, 72:120].rearrange("p (n c) -> p n c", n=6)
    DC = SEQ - 2 * TJ

    def prompt_cols(j):
        a, b = third(j)
        return a, min(b, SEQ)

    def per_chunk(v):
        return v.unsqueeze(2).to_broadcast([P, KD, NSEQ])

    def boundary(post, pre, x_ready=None):
        base = {n: at(n) for n in ("acc_done", "y_mean", "rms_sqrt", "rms", "tmp_u", "x_new", "dec_u", "xsq",
                                   "xsq_used", "tmp_w", "a_full", "a_hi", "a_lo", "dec_n", "vec", "mod_done", "ysq")}
        ny = NJ if post is not None else 0
        vec = base["vec"]

        def b(name, n=0):
            return base[name] + n

        def y_order(j):
            return {0: 0, 1: 1, 2: 3 if pre is not None else 2}[j]

        def x_order(j):
            return {0: 2, 1: 4, 2: 5}[j] if post is not None else j

        @block.tensor
        def _(pe):
            pe.wait_ge(S("mod_done"), b("mod_done"))
            if post is not None:
                for j in range(NJ):
                    pe.wait_ge(S("acc_done"), b("acc_done", -NJ + j + 1))
                    if j == 2:
                        pe.wait_ge(S("rms_sqrt"), b("rms_sqrt", 1))
                    pe.matmul(bank[6 + j % 2][:, 0:TJ], const("mean"), acc[:, j, :], start=True, stop=True)\
                      .then_inc(S("y_mean"), 1)
                pe.wait_ge(S("ysq"), b("ysq"))
            if pre is not None:
                if post is None:
                    pe.wait_ge(S("xT_a"), TT + 1)
                    pe.wait_ge(S("xT_b"), TT + 1)
                for j in range(NJ):
                    for c in range(KD):
                        m = j * KD + c
                        pe.wait_ge(S("xsq"), b("xsq", m + 1))
                        pe.matmul(bank[3 + j][:, 0:TJ], const("mean"), sq[:, m % NJ, :],
                                  start=(c == 0), stop=(c == KD - 1)).then_inc(S("xsq_used"), 1)

        @block.scalar
        def _(act):
            def sqrt(j, source, sem_name, value):
                act.wait_ge(S(sem_name), value)
                act.activation(rs[:, j, :], source[:, 0:TJ], ACT.Sqrt, bias=const("eps")).then_inc(S("rms_sqrt"), 1)

            def squares(j):
                lo_, hi_ = third(j)
                for c in range(KD):
                    m = j * KD + c
                    if post is None:
                        x_ready(act, j)
                    else:
                        act.wait_ge(S("x_new"), b("x_new", m + 1))
                        if j == 2:
                            act.wait_ge(S("dec_u"), b("dec_u", 3))
                    act.wait_ge(S("xsq_used"), b("xsq_used", max(0, m - NJ + 1)))
                    act.activation(sq[:, m % NJ, :], x[:, c, lo_:hi_], ACT.Square).then_inc(S("xsq"), 1)
                sqrt(j, bank[3 + j], "xsq_used", b("xsq_used", (j + 1) * KD))

            def affine(j):
                lo_, hi_ = prompt_cols(j)
                w = hi_ - lo_
                for c in range(KD):
                    m = j * KD + c
                    act.wait_ge(S("tmp_w"), b("tmp_w", m + 1))
                    act.activation(tmp[:, m % 2, 0:w], tmp[:, m % 2, 0:w], ACT.Identity,
                                   bias=modv[:, 3 * pre * KD + c, 0:1], scale=scaleA[:, pre, c, 0:1])\
                       .then_inc(S("a_full"), 1)
                    act.wait_ge(S("a_full"), b("a_full", m + 1))
                    act.activation(ahi[:, c, lo_:hi_], tmp[:, m % 2, 0:w], ACT.Copy).then_inc(S("a_hi"), 1)

            if post is not None:
                for j in range(NJ):
                    sqrt(j, bank[6 + j % 2], "y_mean", b("y_mean", j + 1))
            if pre is not None:
                act.wait_ge(S("vec"), vec + (1 if post is not None else 0) + 2)
                squares(0)
                squares(1)
                affine(0)
                squares(2)
                affine(1)
                affine(2)

        @block.vector
        def _(dve):
            def inverse(j, k):
                dve.wait_ge(S("rms_sqrt"), b("rms_sqrt", (j if k < 0 else ny + j) + 1))
                dve.reciprocal(rs[:, j, :], rs[:, j, :]).then_inc(S("rms"), 1)

            def add(j):
                dve.wait_ge(S("rms"), b("rms", y_order(j) + 1))
                lo_, hi_ = prompt_cols(j)
                w = hi_ - lo_

                def finish(m):
                    dve.wait_ge(S("tmp_u"), b("tmp_u", m + 1))
                    xc = x[:, m % KD, lo_:hi_]
                    dve.tensor_tensor(xc, xc, tmp[:, m % 2, 0:w], ALU.add).then_inc(S("x_new"), 1)
                for c in range(KD):
                    m = j * KD + c
                    if c >= 2:
                        finish(m - 2)
                        dve.wait_ge(S("x_new"), b("x_new", m - 1))
                    dve.scalar_tensor_tensor(out=tmp[:, m % 2, 0:w], in0=y[:, c, lo_:hi_],
                                             scalar=gateC[:, post, c, 0:1], in1=rs[:, j, 0:w],
                                             op0=ALU.mult, op1=ALU.mult).then_inc(S("tmp_u"), 1)
                finish(j * KD + KD - 2)
                finish(j * KD + KD - 1)
                dve.wait_ge(S("x_new"), b("x_new", (j + 1) * KD))
                if j == 2:
                    rsd = rs[:, 2, DC:TJ].unsqueeze(1).to_broadcast([P, KD, NDEC])
                    dve.tensor_tensor(decd[:, 0], y[:, :, SEQ:T], rsd, ALU.mult).then_inc(S("dec_u"), 1)
                    dve.wait_ge(S("dec_u"), b("dec_u", 1))
                    dve.tensor_tensor(decd[:, 1], decd[:, 0], gateC[:, post, :, 1:NSEQ], ALU.mult)\
                       .then_inc(S("dec_u"), 1)
                    dve.wait_ge(S("dec_u"), b("dec_u", 2))
                    dve.tensor_tensor(x[:, :, SEQ:T], x[:, :, SEQ:T], decd[:, 1], ALU.add).then_inc(S("dec_u"), 1)
                    dve.wait_ge(S("dec_u"), b("dec_u", 3))

            def apply(j):
                dve.wait_ge(S("rms"), b("rms", x_order(j) + 1))
                lo_, hi_ = prompt_cols(j)
                w = hi_ - lo_

                def low(m):
                    dve.wait_ge(S("a_hi"), b("a_hi", m + 1))
                    dve.tensor_tensor(alo[:, m % KD, lo_:hi_], tmp[:, m % 2, 0:w], ahi[:, m % KD, lo_:hi_],
                                      ALU.subtract).then_inc(S("a_lo"), 1)
                for c in range(KD):
                    m = j * KD + c
                    if c >= 2:
                        low(m - 2)
                        dve.wait_ge(S("a_lo"), b("a_lo", m - 1))
                    dve.tensor_tensor(tmp[:, m % 2, 0:w], x[:, c, lo_:hi_], rs[:, j, 0:w], ALU.mult)\
                       .then_inc(S("tmp_w"), 1)
                low(j * KD + KD - 2)
                low(j * KD + KD - 1)
                dve.wait_ge(S("a_lo"), b("a_lo", (j + 1) * KD))
                if j == 2:
                    rsd = rs[:, 2, DC:TJ].unsqueeze(1).to_broadcast([P, KD, NDEC])
                    dve.tensor_tensor(decd[:, 0], x[:, :, SEQ:T], rsd, ALU.mult).then_inc(S("dec_n"), 1)
                    dve.wait_ge(S("dec_n"), b("dec_n", 1))
                    dve.tensor_tensor(decd[:, 1], decd[:, 0], scaleA[:, pre, :, 1:NSEQ], ALU.mult)\
                       .then_inc(S("dec_n"), 1)
                    dve.wait_ge(S("dec_n"), b("dec_n", 2))
                    dve.tensor_tensor(decd[:, 2], decd[:, 1], modv[:, 3 * pre * KD:(3 * pre + 1) * KD, 1:NSEQ],
                                      ALU.add).then_inc(S("dec_n"), 1)
                    dve.wait_ge(S("dec_n"), b("dec_n", 3))
                    dve.tensor_copy(ahi[:, :, SEQ:T], decd[:, 2]).then_inc(S("dec_n"), 1)
                    dve.wait_ge(S("dec_n"), b("dec_n", 4))
                    dve.tensor_tensor(alo[:, :, SEQ:T], decd[:, 2], ahi[:, :, SEQ:T], ALU.subtract)\
                       .then_inc(S("a_lo"), 1)

            n = vec
            if post is not None:
                dve.wait_ge(S("mod_done"), (3 * post + 3) * KD)
                dve.scalar_tensor_tensor(out=gateC[:, post], in0=modv[:, (3 * post + 2) * KD:(3 * post + 3) * KD, :],
                                         scalar=0.5 if post != 1 else 1.0, in1=per_chunk(G[:, 2 * post + 1, :]),
                                         op0=ALU.mult, op1=ALU.mult).then_inc(S("vec"), 1)
                n += 1
            if pre is not None:
                dve.wait_ge(S("par"), 5)
                dve.wait_ge(S("mod_done"), (3 * pre + 2) * KD)
                dve.tensor_scalar(scaleA[:, pre], modv[:, (3 * pre + 1) * KD:(3 * pre + 2) * KD, :], 1.0, None,
                                  ALU.add).then_inc(S("vec"), 1)
                dve.wait_ge(S("vec"), n + 1)
                dve.tensor_tensor(scaleA[:, pre], scaleA[:, pre], per_chunk(G[:, 2 * pre, :]), ALU.mult)\
                   .then_inc(S("vec"), 1)
                n += 2
            dve.wait_ge(S("vec"), n)
            if post is not None:
                inverse(0, -1)
                add(0)
                inverse(1, -1)
                add(1)
                if pre is not None:
                    inverse(0, 0)
                    apply(0)
                inverse(2, -1)
                add(2)
                if pre is not None:
                    inverse(1, 0)
                    apply(1)
                    inverse(2, 0)
                    apply(2)
            else:
                for j in range(NJ):
                    inverse(j, 0)
                    apply(j)

        if post is not None:
            count("y_mean", NJ)
            count("tmp_u", NJ * KD)
            count("x_new", NJ * KD)
            count("dec_u", 3)
            count("vec", 1)
        if pre is not None:
            for name in ("xsq", "xsq_used", "tmp_w", "a_full", "a_hi"):
                count(name, NJ * KD)
            count("a_lo", NJ * KD + 1)
            count("dec_n", 4)
            count("vec", 2)
        for name in ("rms_sqrt", "rms"):
            count(name, ny + (NJ if pre is not None else 0))
        return [b("a_lo", KD), b("a_lo", 2 * KD), b("a_lo", 3 * KD + 1)]

    def ffn(f, a_ready, with_ada):
        wgu, wdn = I["w_ffn_gu"][0, f], I["w_ffn_down"][0, f]
        s0 = at("slab")
        per = 8 if with_ada else 4
        q0 = NSTART
        silu0, h0, hh0, hl0, g0, acc0 = (at(n) for n in ("silu", "h", "h_hi", "h_lo", "group", "acc_done"))
        ysq0, y0 = at("ysq"), at("y")

        def gu_src(k, up):
            return wgu[:, bass.ds(k * P + up * DFF, P)].rearrange("(k p) n -> p k n", p=P)

        def dn_src(c, half):
            return wdn[half * 11 * P:(half + 1) * 11 * P, bass.ds(c * P, P)].rearrange("(k p) n -> p k n", p=P)

        def plan():
            out, ada = [], 0
            for u in range(2):
                for kind in ("gate", "up"):
                    out.append((kind, u, None))
                    if with_ada:
                        out.append(("ada", u, ada))
                        ada += 1
            return out

        PLAN = plan()
        NIT = KF // 2
        s1 = s0 + NIT * per
        nd = [3, 1] if with_ada else [4]
        dper = [8, 4] if with_ada else [4]
        q1 = q0 + 4 * NIT

        def dplan(part):
            out = []
            for u in range(2):
                out += [("down", u, 0), ("down", u, 1)]
                if dper[part] == 8:
                    out += [("ada", u, 2 * u), ("ada", u, 2 * u + 1)]
            return out

        def down_parts():
            c, s, q = 0, s1, q1
            for part, n in enumerate(nd):
                yield part, n, c, s, q
                c, s, q = c + 2 * n, s + n * dper[part], q + 4 * n * (dper[part] == 8)

        @block.sync
        def _(sp):
            with sp.Fori(0, NIT) as i:
                for v, (kind, u, ada) in enumerate(PLAN):
                    if kind == "ada":
                        load_slab(sp, i * per + (s0 + v), v % 4, ada_src(i * 4 + (q0 + ada)), KD)
                    else:
                        load_slab(sp, i * per + (s0 + v), v % 4, gu_src(i * 2 + u, kind == "up"), KD)
            for part, n, c0, s2, q2 in down_parts():
                with sp.Fori(0, n) as i:
                    for v, (kind, u, x_) in enumerate(dplan(part)):
                        if kind == "ada":
                            load_slab(sp, i * dper[part] + (s2 + v), v % 4, ada_src(i * 4 + (q2 + x_)), KD)
                        else:
                            load_slab(sp, i * dper[part] + (s2 + v), v % 4, dn_src(i * 2 + (c0 + u), x_), 11)

        @block.gpsimd
        def _(pool):
            if s0 == NSTART:
                pool.wait_ge(slab_used, NSTART)
                pool.wait_ge(stage_full[1], 16 * (NSTART // 2 + 1))
            with pool.Fori(0, NIT) as i:
                for v in range(per):
                    split_slab(pool, s0, i * per, v, KD * P)
            for part, n, c0, s2, q2 in down_parts():
                with pool.Fori(0, n) as i:
                    for v, (kind, u, x_) in enumerate(dplan(part)):
                        split_slab(pool, s2, i * dper[part], v, KD * P if kind == "ada" else SLAB)

        def ada_product(pe, s, v, q, slot):
            pe.wait_ge(slab_split, s + 1)
            pe.wait_ge(S("mod_done"), q - 1)
            w1, w2 = slab_parts(v % 4, KD)
            o = bank[6 + slot % 2][:, 0:NSEQ]
            for k in range(KD):
                last = product(pe, o, w1[:, k, :], w2[:, k, :], csh[:, k, :], csl[:, k, :], k == 0, k == KD - 1)
            last.then_inc(slab_used, 1)

        def ada_value(act, s, q, slot):
            act.wait_ge(slab_used, s + 1)
            act.activation(modv[:, bass.ds(q, 1), :], bank[6 + slot % 2][:, 0:NSEQ].unsqueeze(1), ACT.Identity,
                           bias=par1[:, bass.ds(q, 1)], scale=IWS).then_inc(S("mod_done"), 1)

        @block.tensor
        def _(pe):
            with pe.Fori(0, NIT) as i:
                for v, (kind, u, ada) in enumerate(PLAN):
                    s = i * per + (s0 + v)
                    if kind == "ada":
                        ada_product(pe, s, v, i * 4 + (q0 + ada), ada % 4)
                        continue
                    w1, w2 = slab_parts(v % 4, KD)
                    pe.wait_ge(slab_split, s + 1)
                    for j in range(NJ):
                        a, b = third(j)
                        pe.wait_ge(S("a_lo"), a_ready[j])
                        pe.wait_ge(S("silu" if kind == "gate" else "h"),
                                   i * 6 + (3 * u + j + 1 + (silu0 if kind == "gate" else h0)))
                        o = bank[j + 3 * (kind == "up")][:, 0:TJ]
                        for k in range(KD):
                            last = product(pe, o, w1[:, k, :], w2[:, k, :], ahi[:, k, a:b], alo[:, k, a:b],
                                           k == 0, k == KD - 1)
                        last.then_inc(S("group") if j < 2 else slab_used, 1)
            for part, n, c0, s2, q2 in down_parts():
                with pe.Fori(0, n) as i:
                    for v, (kind, u, x_) in enumerate(dplan(part)):
                        s = i * dper[part] + (s2 + v)
                        if kind == "ada":
                            ada_product(pe, s, v, i * 4 + (q2 + x_), x_ % 4)
                            continue
                        if x_ == 0:
                            continue
                        halves = [slab_parts((v - 1) % 4, 11), slab_parts(v % 4, 11)]
                        pe.wait_ge(slab_split, s + 1)
                        pe.wait_ge(S("silu"), silu0 + 3 + NJ * KF)
                        pe.wait_ge(S("h"), h0 + 3 + NJ * KF)
                        for j in range(NJ):
                            a, b = third(j)
                            pe.wait_ge(S("ysq"), i * 6 + (ysq0 + 3 * (c0 + u) + j + 1))
                            pe.wait_ge(S("h_lo"), hl0 + 3 + NJ * (KF - 1) + j + 1)
                            o = bank[3 * u + j][:, 0:TJ]
                            for k in range(KF):
                                w1, w2 = halves[k // 11]
                                last = product(pe, o, w1[:, k % 11, :], w2[:, k % 11, :], hhi[:, k, a:b],
                                               hlo[:, k, a:b], k == 0, k == KF - 1)
                                if j == NJ - 1 and k == 10:
                                    last.then_inc(slab_used, 1)
                            last.then_inc(S("group") if j < 2 else slab_used, 1)

        @block.scalar
        def _(act):
            act.sem_inc(S("silu"), 3)
            with act.Fori(0, NIT) as i:
                for v, (kind, u, ada) in enumerate(PLAN):
                    s = i * per + (s0 + v)
                    if kind == "ada":
                        ada_value(act, s, i * 4 + (q0 + ada), ada % 4)
                        continue
                    for j in range(NJ):
                        a, b = third(j)
                        if kind == "gate":
                            if j < 2:
                                act.wait_ge(S("group"), i * 8 + (g0 + 4 * u + j + 1))
                            else:
                                act.wait_ge(slab_used, s + 1)
                            act.wait_ge(S("h"), i * 6 + (h0 + 3 * u + j + 1))
                            act.activation(sg[:, j, :], bank[j][:, 0:TJ], ACT.Silu, scale=IWS).then_inc(S("silu"), 1)
                        else:
                            act.wait_ge(S("h"), i * 6 + (h0 + 3 + 3 * u + j + 1))
                            act.activation(hhi[:, bass.ds(i * 2 + u, 1), a:b], h32[:, j, :].unsqueeze(1), ACT.Copy)\
                               .then_inc(S("h_hi"), 1)
            act.sem_inc(S("ysq"), 6)
            for part, n, c0, s2, q2 in down_parts():
                with act.Fori(0, n) as i:
                    for v, (kind, u, x_) in enumerate(dplan(part)):
                        s = i * dper[part] + (s2 + v)
                        if kind == "ada":
                            ada_value(act, s, i * 4 + (q2 + x_), x_ % 4)
                            continue
                        if x_ == 0:
                            continue
                        for j in range(NJ):
                            a, b = third(j)
                            if j < 2:
                                act.wait_ge(S("group"), i * 4 + (g0 + 4 * KF + 2 * (c0 + u) + j + 1))
                            else:
                                act.wait_ge(slab_used, s + 1)
                            act.activation(y[:, bass.ds(i * 2 + (c0 + u), 1), a:b], bank[3 * u + j][:, 0:TJ].unsqueeze(1),
                                           ACT.Copy, scale=IWS).then_inc(S("y"), 1)
                            act.wait_ge(S("acc_done"), i * 6 + (acc0 + 3 * (c0 + u) + j + 1))
                            act.activation(sq[:, j, :], bank[3 * u + j][:, 0:TJ], ACT.Square, scale=IWS)\
                               .then_inc(S("ysq"), 1)

        @block.vector
        def _(dve):
            dve.sem_inc(S("h"), 3)
            dve.sem_inc(S("h_lo"), 3)
            with dve.Fori(0, NIT) as i:
                for v, (kind, u, ada) in enumerate(PLAN):
                    if kind != "up":
                        continue
                    s = i * per + (s0 + v)
                    for j in range(NJ):
                        if j < 2:
                            dve.wait_ge(S("group"), i * 8 + (g0 + 4 * u + 2 + j + 1))
                        else:
                            dve.wait_ge(slab_used, s + 1)
                        dve.wait_ge(S("silu"), i * 6 + (silu0 + 3 + 3 * u + j + 1))
                        dve.wait_ge(S("h_lo"), i * 6 + (hl0 + 3 * u + j + 1))
                        dve.scalar_tensor_tensor(out=h32[:, j, :], in0=bank[3 + j][:, 0:TJ], scalar=IWS,
                                                 in1=sg[:, j, :], op0=ALU.mult, op1=ALU.mult).then_inc(S("h"), 1)
                    for j in range(NJ):
                        a, b = third(j)
                        dve.wait_ge(S("h_hi"), i * 6 + (hh0 + 3 * u + j + 1))
                        dve.tensor_tensor(hlo[:, bass.ds(i * 2 + u, 1), a:b], h32[:, j, :].unsqueeze(1),
                                          hhi[:, bass.ds(i * 2 + u, 1), a:b], ALU.subtract).then_inc(S("h_lo"), 1)
            dve.wait_ge(S("h_lo"), hl0 + 3 + NJ * KF)
            for j in range(NJ):
                dve.memset(acc[:, j, :], 0.0).then_inc(S("acc_done"), 1)
            for part, n, c0, s2, q2 in down_parts():
                with dve.Fori(0, n) as i:
                    for u in range(2):
                        for j in range(NJ):
                            m = 3 * (c0 + u) + j
                            dve.wait_ge(S("ysq"), i * 6 + (ysq0 + 6 + m + 1))
                            dve.wait_ge(S("acc_done"), i * 6 + (acc0 + m + 1))
                            dve.tensor_tensor(acc[:, j, :], acc[:, j, :], sq[:, j, :], ALU.add)\
                               .then_inc(S("acc_done"), 1)

        count("slab", NIT * per + sum(a * b for a, b in zip(nd, dper)))
        count("silu", 3 + NJ * KF)
        count("h", 3 + NJ * KF)
        count("h_hi", NJ * KF)
        count("h_lo", 3 + NJ * KF)
        count("group", 4 * KF + 2 * KD)
        count("ysq", 6 + NJ * KD)
        count("y", NJ * KD)
        count("acc_done", NJ + NJ * KD)
        if with_ada:
            count("mod_done", NMOD - NSTART)

    def write_out(ready):
        o_prompt, o_sample = O["y_prompt"][0], O["y_sample"].rearrange("b o d -> (b o) d")

        @block.tensor
        def _(pe):
            ready(pe)
            for t in range(TT + 1):
                n = P if t < TT else NDEC
                if t >= 2:
                    pe.wait_ge(S("row_a"), t - 1)
                    pe.wait_ge(S("row_b"), t - 1)
                for half in range(2):
                    for c in range(4):
                        last = pe.transpose(bank[2 * (t % 2) + half][0:n, c * P:(c + 1) * P],
                                            x[:, 4 * half + c, t * P:t * P + n], const("ident"))
                    last.then_inc(S("row_mm"), 1)

        @block.vector
        def _(dve):
            for t in range(TT + 1):
                n = P if t < TT else NDEC
                dve.wait_ge(S("row_mm"), 2 * t + 1)
                if t >= 4:
                    dve.wait_ge(S(f"row_out{t % 4}"), 16 * (t // 4))
                dve.tensor_copy(xrow[0:n, t % 4, 0:512], bank[2 * (t % 2)][0:n, :]).then_inc(S("row_a"), 1)

        @block.scalar
        def _(act):
            for t in range(TT + 1):
                n = P if t < TT else NDEC
                act.wait_ge(S("row_mm"), 2 * t + 2)
                if t >= 4:
                    act.wait_ge(S(f"row_out{t % 4}"), 16 * (t // 4))
                act.activation(xrow[0:n, t % 4, 512:D], bank[2 * (t % 2) + 1][0:n, :], ACT.Copy).then_inc(S("row_b"), 1)

        @block.sync
        def _(sp):
            for t in range(TT + 1):
                sp.wait_ge(S("row_a"), t + 1)
                sp.wait_ge(S("row_b"), t + 1)
                if t < TT:
                    sp.dma_start(o_prompt[t * P:(t + 1) * P, :], xrow[:, t % 4, :]).then_inc(S(f"row_out{t % 4}"), 16)
                else:
                    sp.dma_start(o_sample, xrow[0:NDEC, t % 4, :]).then_inc(S(f"row_out{t % 4}"), 16)
            for q in range(4):
                sp.wait_ge(S(f"row_out{q}"), 16 * (3 if q == 0 else 2))

    def mixer(a_ready):
        w_in = I["w_in"][0]
        sa = at("slab")
        sphi = sa + 11
        sw2 = sphi + 8
        sconv = sw2 + 1
        smerge = sconv + 3 * KC
        sout = smerge + 4 * KD
        assert sa % 4 == 0 and smerge % 4 == 0 and (sout + KD) % 4 == 0
        count("slab", sout + KD - sa)
        R = NDEC * NH

        cursor[0] = free_at
        oahi = place("oahi", [P, KC, T], F16)
        oalo = place("oalo", [P, KC, T], F16)
        mix_at = cursor[0]
        gs = place("gs", [P, TT + 1, GC], F32)
        qst_at = cursor[0]
        qst = place("qst", [P, NH, SEQ], F16)
        kst = place("kst", [P, 2, NG, 2, SEQ], F16)
        vst_at = cursor[0]
        vst = place("vst", [P, 2, TT + 1, P], F32)
        zd = place("zd", [NDEC, 6, P], F32)
        qd = place("qd", [P, NDEC, NH], F32)
        knt = place("knt", [P, 2, NDEC], F32)
        vbd = place("vbd", [P, NH, HD], F32)
        kcst = place("kcst", [P, NG, 2, NB], F16)
        kcd = place("kcd", [P, NDEC * NB], F32)
        vcd = place("vcd", [P, P], F32)
        gdec = place("gdec", [R, 3], F32)
        ptf = place("ptf", [P, 1], F32)
        pti = place("pti", [P, 1], I32)
        rowid = place("rowid", [P, 16], I32)
        mixwork = cursor[0]
        zs = place("zs", [P, 2, TT + 1, P], F32)
        rot = place("rot", [P, 4, (TT + 1) * 16], F32)

        def split_const(pool, s, n):
            split_slab(pool, s - s % 4, 0, s % 4, n)

        def load_const(sp, s, src, kk, w=P):
            load_slab(sp, s, s % 4, src, kk, w)

        def cols(c0, w):
            return w_in[:, c0:c0 + w].rearrange("(k p) n -> p k n", p=P)

        KINDS = ["q", "q", "q", "q", "cmp_k", "cmp_v", "slc_k", "slc_v", "win_k", "win_v", "gate"]
        DEST = {0: 0, 1: 1, 2: 0, 3: 1, 4: 0, 5: 1, 6: 0, 8: 1}
        width = [GC if kind == "gate" else P for kind in KINDS]
        outs = {4: ("cmp", 0), 5: ("cmp", 1), 6: ("slc", 0), 7: ("slc", 1), 8: ("win", 0), 9: ("win", 1)}

        @block.sync
        def _(sp):
            for n in range(11):
                load_const(sp, sa + n, cols(n * P, width[n]), KD, width[n])
            sp.dma_start(O["win_kv_sample"][0][:, 0:WIN - 1], I["state_win_kv"][0][:, 1:WIN]).then_inc(S("win_shift"), 16)

        @block.gpsimd
        def _(pool):
            for n in range(11):
                split_const(pool, sa + n, KD * width[n])

        @block.vector
        def _(dve):
            dve.memset(zs[:, :, TT, :], 0.0).then_inc(S("z_clear"), 1)
            dve.memset(qd[:], 0.0).then_inc(S("z_clear"), 1)

        @block.tensor
        def _(pe):
            for j in range(NJ):
                pe.wait_ge(S("a_lo"), a_ready[j])
            pe.wait_ge(S("rms_sqrt"), at("rms_sqrt"))

        roped, evac, zdec, out_sems = {}, {}, {}, []

        def dest(n, ts):
            if n in (7, 9):
                return vst[:, (n - 7) // 2, ts, :]
            return gs[:, ts, :] if n == 10 else zs[:, DEST[n], ts, :]

        def project(n):
            s, w = sa + n, width[n]

            @block.tensor
            def _(pe):
                w1, w2 = slab_parts(s % 4, KD, w)
                pe.wait_ge(slab_split, s + 1)
                if n >= 2:
                    pe.wait_ge(S("z_row"), evac[n - 2])
                for part, tiles in enumerate((range(0, 4), range(4, 8), range(8, 9))):
                    for t in tiles:
                        a, b = t * P, min(T, (t + 1) * P)
                        o = bank[3 * (n % 2) + part][0:b - a, (t % 4) * P:(t % 4) * P + w]
                        for k in range(KD):
                            last = product(pe, o, ahi[:, k, a:b], alo[:, k, a:b], w1[:, k, :], w2[:, k, :],
                                           k == 0, k == KD - 1)
                    if part < 2:
                        last.then_inc(S("z_mm"), 1)
                        count("z_mm")
                    else:
                        last.then_inc(slab_used, 1)

            @block.scalar
            def _(act):
                for part in range(3):
                    rows = NDEC if part == 2 else P
                    ts = slice(4 * part, 4 * part + 4) if part < 2 else slice(8, 9)
                    if part == 0:
                        if n in DEST:
                            if n - 2 in DEST:
                                act.wait_ge(S("z_used"), used[n - 2])
                            if n - 2 in zdec:
                                act.wait_ge(S("z_dec"), zdec[n - 2])
                            for name in slot_out.get(DEST[n], []):
                                act.wait_ge(S(name), 16)
                            act.wait_ge(S("z_clear"), 2)
                    if part < 2:
                        act.wait_ge(S("z_mm"), at("z_mm") - 1 + part)
                    else:
                        act.wait_ge(slab_used, s + 1)
                    nt = 4 if part < 2 else 1
                    src = bank[3 * (n % 2) + part][0:rows, 0:nt * P].rearrange("p (t n) -> p t n", n=P)[:, :, 0:w]
                    act.activation(dest(n, ts)[0:rows], src, ACT.Sigmoid if n == 10 else ACT.Copy,
                                   scale=IWS / 8 if KINDS[n] == "q" else IWS).then_inc(S("z_row"), 1)
                    evac[n] = count("z_row")

            if n in DEST and n != 5:
                z = zs[:, DEST[n]].rearrange("p t (h d) -> p t h d", h=2)
                x1, x2 = z[:, :, :, 0:8], z[:, :, :, 8:16]
                cosb, sinb = (const(m).rearrange("p (t r) -> p t r", t=TT + 1).unsqueeze(2)
                              .to_broadcast([P, TT + 1, 2, 8]) for m in ("cos", "sin"))
                r = [rot[:, m, :].rearrange("p (t h r) -> p t h r", t=TT + 1, h=2) for m in range(4)]

                @block.vector
                def _(dve):
                    dve.wait_ge(S("z_row"), evac[n])
                    if at("rope"):
                        dve.wait_ge(S("rope"), at("rope"))
                    for m, (xx, cs) in enumerate(((x1, cosb), (x2, sinb), (x2, cosb), (x1, sinb))):
                        dve.tensor_tensor(r[m], xx, cs, ALU.mult).then_inc(S("rope"), 1)
                        count("rope")
                    dve.wait_ge(S("rope"), at("rope"))
                    dve.tensor_tensor(x1, r[0], r[1], ALU.subtract).then_inc(S("rope"), 1)
                    dve.tensor_tensor(x2, r[2], r[3], ALU.add).then_inc(S("rope"), 1)
                    roped[n] = count("rope", 2)
                    if n in ZD:
                        dve.wait_ge(S("rope"), roped[n])
                        dve.tensor_copy(zd[:, ZD[n], :], zs[0:NDEC, DEST[n], TT, :]).then_inc(S("z_dec"), 1)
                        zdec[n] = count("z_dec")
            if n in outs:
                name, kv = outs[n]

                @block.scalar
                def _(act):
                    if n in roped:
                        act.wait_ge(S("rope"), roped[n])
                    else:
                        act.wait_ge(S("z_row"), evac[n])
                    t0 = 4 if name == "win" else 0
                    o = O[f"{name}_kv_prompt"][0, 0].rearrange("(t p) v g d -> p t v (g d)", p=P)
                    act.dma_start(o[:, :, kv, :], dest(n, slice(t0, TT))).then_inc(S(f"out_p{n}"), 16)
                    o = O[f"{name}_kv_sample"][0][:, WIN - 1 if name == "win" else 0, kv].rearrange("b g d -> b (g d)")
                    act.dma_start(o, dest(n, slice(TT, TT + 1))[0:NDEC, 0, :]).then_inc(S(f"out_s{n}"), 16)
                    out_sems.extend([f"out_p{n}", f"out_s{n}"])
                    if n in DEST:
                        slot_out[DEST[n]] = [f"out_p{n}", f"out_s{n}"]

        ZD = {0: 0, 1: 1, 2: 2, 3: 3, 6: 4, 8: 5}
        used, slot_out, tsplit = {}, {}, {}

        def transposed(n):
            if n not in DEST:
                return
            if n in (4, 5):
                used[n] = at("z_used")
                return
            for half in range(2):
                b = bank[6 + half]
                sl = slice(half * 512, half * 512 + 512)

                @block.tensor
                def _(pe):
                    pe.wait_ge(S("rope"), roped[n])
                    if tsplit.get(half):
                        pe.wait_ge(S("zT_lo"), tsplit[half])
                    for t in range(4):
                        last = pe.transpose(b[:, t * P:(t + 1) * P], zs[:, DEST[n], 4 * half + t, :], const("ident"))
                    last.then_inc(S("z_used"), 1)
                    used[n] = count("z_used")
                for r in range(2):
                    rows, other = slice(64 * r, 64 * r + 64), slice(64 - 64 * r, 128 - 64 * r)
                    if n < 4:
                        hi, lo = qst[rows, 2 * n + r, sl], qst[other, 2 * n + r, sl]
                    else:
                        hi, lo = kst[rows, (n - 6) // 2, r, 0, sl], kst[rows, (n - 6) // 2, r, 1, sl]

                    @block.scalar
                    def _(act):
                        act.wait_ge(S("z_used"), used[n])
                        act.activation(hi, b[rows, :], ACT.Copy).then_inc(S("zT_hi"), 1)
                        count("zT_hi")

                    @block.vector
                    def _(dve):
                        dve.wait_ge(S("zT_hi"), at("zT_hi"))
                        dve.tensor_tensor(lo, b[rows, :], hi, ALU.subtract).then_inc(S("zT_lo"), 1)
                        tsplit[half] = count("zT_lo")
            if n >= 6:
                @block.vector
                def _(dve):
                    dve.wait_ge(S("zT_lo"), at("zT_lo"))
                    for r in range(2):
                        rows, other = slice(64 * r, 64 * r + 64), slice(64 - 64 * r, 128 - 64 * r)
                        for part in range(2):
                            dve.tensor_copy(kst[other, (n - 6) // 2, r, part, :], kst[rows, (n - 6) // 2, r, part, :])\
                               .then_inc(S("k_twice"), 1)
                            count("k_twice")

        for n in range(12):
            if n < 11:
                project(n)
            if n >= 1:
                transposed(n - 1)
        z_end = {m: at(m) for m in ("z_row", "zT_lo", "zT_hi", "k_twice", "z_used", "rope", "z_dec")}

        @block.tensor
        def _(pe):
            pe.wait_ge(S("z_dec"), at("z_dec"))
            pe.wait_ge(S("zT_lo"), at("zT_lo"))
            pe.wait_ge(S("z_row"), at("z_row"))
            for m in range(6):
                last = pe.transpose(bank[6][:, 16 * m:16 * m + NDEC], zd[:, m, :], const("ident", NDEC)[:, 0:NDEC])
            last.then_inc(S("dT_mm"), 1)
            pe.matmul(bank[7][0:R, 0:GC], const("seqrep", NDEC)[:, 0:R], gs[0:NDEC, TT, :], start=True, stop=True)\
              .then_inc(S("dT_mm"), 1)

        @block.vector
        def _(dve):
            dve.wait_ge(S("dT_mm"), 2)
            for h in range(NH):
                src = bank[6][64 * (h % 2):64 * (h % 2) + 64, 16 * (h // 2):16 * (h // 2) + NDEC]
                g = h // HPG
                dve.tensor_copy(qd[64 * g:64 * g + 64, :, h], src).then_inc(S("dec_q"), 1)
            for br in range(2):
                dve.tensor_copy(knt[:, br, :], bank[6][:, 64 + 16 * br:64 + 16 * br + NDEC]).then_inc(S("dec_q"), 1)
            g3 = rot[0:R, 0, 0:GC].rearrange("p (b h) -> p b h", h=NH)
            dve.wait_ge(S("rope"), at("rope"))
            dve.tensor_tensor(g3, bank[7][0:R, 0:GC].rearrange("p (b h) -> p b h", h=NH),
                              const("ownhead", R).unsqueeze(1).to_broadcast([R, 3, NH]), ALU.mult)\
               .then_inc(S("dec_q"), 1)
            dve.wait_ge(S("dec_q"), 11)
            dve.reduce_sum(gdec[:], g3, AX_X).then_inc(S("dec_q"), 1)
            dve.wait_ge(S("dec_q"), 12)
        count("dec_q", 12)

        NBK = NDEC * NB + NB
        NL = 4
        NLC = BLK // NL
        cx = nc.alloc_sbuf_tensor_at("cx", [P, 2, NL * 2 * P], F32, offset=free_at)
        cxs = nc.alloc_sbuf_tensor_at("cxs", [P, 2, NL * 2 * P], F32, offset=free_at + 2 * NL * 2 * P * 4)
        cursor[0] = mixwork
        cxp = place("cxp", [NB, 2, NL * 2 * P], F32)
        cxps = place("cxps", [NB, 2, NL * 2 * P], F32)
        xth = place("xth", [P, 2, NG * NBK], F16)
        xtl = place("xtl", [P, 2, NG * NBK], F16)
        hid = place("hid", [P, 2, NG * NBK], F32)
        hidh = place("hidh", [P, 2, NG * NBK], F16)
        hidl = place("hidl", [P, 2, NG * NBK], F16)
        vcp = place("vcp", [NB, P], F32)

        @block.sync
        def _(sp):
            for half in range(2):
                sp.dma_start(pti[half:P:2, :], I["page_table"].rearrange("b (n o) -> (b n) o", o=1))\
                  .then_inc(S("pages_in"), 16)
            for n in range(8):
                v, m = n % 2, n // 2
                load_const(sp, sphi + n,
                           I["phi_w1"][0, v, m * 8 * P:(m + 1) * 8 * P, :].rearrange("(k p) n -> p k n", p=P), 8)
            load_const(sp, sw2, I["phi_w2"][0].rearrange("v p d -> p v d"), 2, HD)

        @block.vector
        def _(dve):
            dve.wait_ge(S("pages_in"), 32)
            dve.tensor_copy(ptf[:], pti[:]).then_inc(S("rowid"), 1)
            dve.wait_ge(S("rowid"), 1)
            dve.tensor_scalar(ptf[:], ptf[:], 2.0 * NLC, None, ALU.mult).then_inc(S("rowid"), 1)
            dve.wait_ge(S("rowid"), 2)
            dve.tensor_scalar(rowid[:], const("blockrow"), ptf[:, 0:1], None, ALU.add).then_inc(S("rowid"), 1)

        cache_rows = I["cache_cmp_kv"][0].rearrange("r (a l) v g d -> (r a) (l v g d)", l=NL)
        new_rows = O["cmp_kv_prompt"][0, 0].rearrange("(n a l) v g d -> n a (l v g d)", a=NLC, l=NL)
        chunks = [(lc, v, m) for lc in range(NLC) for v in range(2) for m in range(2)]

        def gather(lc):
            @block.gpsimd
            def _(pool):
                if lc == 0:
                    pool.wait_ge(S("rowid"), 3)
                    pool.wait_ge(S("dec_q"), 12)
                if lc >= 2:
                    pool.wait_ge(S("cx_used"), lc - 1)
                pool.indirect_dma_start(cx[:, lc % 2, :], None, cache_rows,
                                        bass.IndirectOffsetOnAxis(ap=rowid[:, lc:lc + 1], axis=0))\
                    .then_inc(S(f"cx_in{lc % 2}"), 16)

            @block.scalar
            def _(act):
                if lc == 0:
                    for n in (4, 5, 6, 8):
                        act.wait_ge(S(f"out_p{n}"), 16)
                        act.wait_ge(S(f"out_s{n}"), 16)
                    act.wait_ge(S("dec_q"), 12)
                if lc >= 2:
                    act.wait_ge(S("cxp_used"), lc - 1)
                act.dma_start(cxp[:, lc % 2, :], new_rows[:, lc, :]).then_inc(S(f"cxp_in{lc % 2}"), 16)

        def permute(lc):
            for src, dst, eng, n, full, used_sem, ready_sem in (
                    (cx, cxs, block.vector, P, "cx_in", "cx_used", "cx_side"),
                    (cxp, cxps, block.scalar, NB, "cxp_in", "cxp_used", "cxp_side")):
                a = src[:, lc % 2, :].rearrange("p (m l x d) -> p m x l d", m=NL // 2, l=2, d=HD)
                b = dst[:, lc % 2, :].rearrange("p (m x l d) -> p m x l d", m=NL // 2, l=2, d=HD)

                @eng
                def _(e):
                    e.wait_ge(S(f"{full}{lc % 2}"), 16 * (lc // 2 + 1))
                    if lc >= 2:
                        e.wait_ge(S("xt_mm"), 4 * (lc - 1))
                    for m in range(NL // 2):
                        op = e.tensor_copy(b[:, m], a[:, m]) if n == P else \
                            e.activation(b[:, m], a[:, m], ACT.Copy)
                        op.then_inc(S(used_sem if m else ready_sem), 1)

        for lc in range(2):
            gather(lc)
        permute(0)

        @block.gpsimd
        def _(pool):
            for n in range(4):
                split_const(pool, sphi + n, KD * P)

        @block.tensor
        def _(pe):
            pe.wait_ge(S("dec_q"), 12)

        for u in range(len(chunks) + 1):
            if u < len(chunks):
                lc, v, m = chunks[u]
                if v == 0 and m == 0 and lc + 1 < NLC:
                    permute(lc + 1)
                    if lc + 2 < NLC:
                        gather(lc + 2)
                    if lc % 4 == 3 and lc < 11:
                        @block.gpsimd
                        def _(pool):
                            split_const(pool, sphi + 4 + lc // 2 - 1, KD * P)
                            split_const(pool, sphi + 4 + lc // 2, KD * P)

                @block.tensor
                def _(pe):
                    if v == 0 and m == 0:
                        pe.wait_ge(S("cx_used"), lc + 1)
                        pe.wait_ge(S("cxp_used"), lc + 1)
                    if u >= 2:
                        pe.wait_ge(S("xt_lo"), u - 1)
                    for g in range(NG):
                        for src, n, c0 in ((cxs, P, 0), (cxps, NB, P)):
                            at_ = ((m * 2 + v) * NG + g) * P
                            last = pe.transpose(bank[u % 2][:, g * NBK + c0:g * NBK + c0 + n],
                                                src[:, lc % 2, at_:at_ + P], const("ident", n)[:, 0:n])
                    last.then_inc(S("xt_mm"), 1)
                bias = par2[:, 12 + 32 * v + 2 * lc + m:13 + 32 * v + 2 * lc + m]

                @block.scalar
                def _(act):
                    act.wait_ge(S("xt_mm"), u + 1)
                    if u >= 2:
                        act.wait_ge(S("x_mm"), u - 1)
                    act.activation(xth[:, u % 2, :], bank[u % 2][:, 0:NG * NBK], ACT.Identity, bias=bias)\
                       .then_inc(S("xt_hi"), 1)

                @block.vector
                def _(dve):
                    dve.wait_ge(S("xt_hi"), u + 1)
                    dve.scalar_tensor_tensor(out=xtl[:, u % 2, :], in0=bank[u % 2][:, 0:NG * NBK], scalar=bias,
                                             in1=xth[:, u % 2, :], op0=ALU.add, op1=ALU.subtract)\
                       .then_inc(S("xt_lo"), 1)
            if u >= 1:
                lc, v, m = chunks[u - 1]

                @block.tensor
                def _(pe):
                    s = sphi + 2 * (lc // 4) + v
                    kc = 2 * (lc % 4) + m
                    w1, w2 = slab_parts(s % 4, KD)
                    pe.wait_ge(slab_split, s + 1)
                    pe.wait_ge(S("xt_lo"), u)
                    last = product(pe, bank[2 + v][:, 0:NG * NBK], w1[:, kc, :], w2[:, kc, :], xth[:, (u - 1) % 2, :],
                                   xtl[:, (u - 1) % 2, :], lc == 0 and m == 0, lc == NLC - 1 and m == 1)
                    last.then_inc(S("x_mm"), 1)
                    if kc == 7:
                        pe.wait_ge(S("x_mm"), u)
                        pe.sem_inc(slab_used, 1)

        @block.gpsimd
        def _(pool):
            split_const(pool, sw2, P)

        @block.scalar
        def _(act):
            act.wait_ge(S("x_mm"), 64)
            for v in range(2):
                act.activation(hid[:, v, :], bank[2 + v][:, 0:NG * NBK], ACT.Silu, bias=par2[:, 76 + v:77 + v],
                               scale=IWS).then_inc(S("hid"), 1)
            act.wait_ge(S("hid"), 2)
            act.activation(hidh[:], hid[:], ACT.Copy).then_inc(S("hid_hi"), 1)

        @block.vector
        def _(dve):
            dve.wait_ge(S("hid_hi"), 1)
            dve.tensor_tensor(hidl[:], hid[:], hidh[:], ALU.subtract).then_inc(S("hid_lo"), 1)

        @block.tensor
        def _(pe):
            w1, w2 = slab_parts(sw2 % 4, 2, HD)
            pe.wait_ge(slab_split, sw2 + 1)
            pe.wait_ge(S("hid_lo"), 1)
            product(pe, bank[4][0:HD, 0:NG * NBK], w1[:, 0, :], w2[:, 0, :], hidh[:, 0, :], hidl[:, 0, :], True, True)\
                .then_inc(S("kc_mm"), 1)
            for g in range(NG):
                for n, c0, o in ((P, g * NBK, 0), (NB, g * NBK + P, 256)):
                    last = product(pe, bank[5][0:n, o + g * HD:o + (g + 1) * HD], hidh[:, 1, c0:c0 + n],
                                   hidl[:, 1, c0:c0 + n], w1[:, 1, :], w2[:, 1, :], True, True)
            last.then_inc(slab_used, 1)

        @block.scalar
        def _(act):
            act.wait_ge(S("kc_mm"), 1)
            for g in range(NG):
                act.activation(kcst[0:HD, g, 0, :], bank[4][0:HD, g * NBK + P:(g + 1) * NBK], ACT.Copy, scale=IWS)\
                   .then_inc(S("kc_hi"), 1)
            for g in range(NG):
                act.activation(kcd[64 * g:64 * g + 64, :], bank[4][0:HD, g * NBK:g * NBK + P], ACT.Copy, scale=IWS)\
                   .then_inc(S("kc_hi"), 1)

        @block.vector
        def _(dve):
            dve.wait_ge(S("kc_hi"), 4)
            for g in range(NG):
                dve.scalar_tensor_tensor(out=kcst[0:HD, g, 1, :], in0=bank[4][0:HD, g * NBK + P:(g + 1) * NBK],
                                         scalar=IWS, in1=kcst[0:HD, g, 0, :], op0=ALU.mult, op1=ALU.subtract)\
                   .then_inc(S("kc_lo"), 1)
            dve.wait_ge(slab_used, sw2 + 1)
            dve.tensor_scalar(vcd[:], bank[5][:, 0:P], IWS, None, ALU.mult).then_inc(S("kc_lo"), 1)
            dve.tensor_scalar(vcp[:], bank[5][0:NB, 256:256 + P], IWS, None, ALU.mult).then_inc(S("kc_lo"), 1)
            dve.wait_ge(S("kc_lo"), 4)
            dve.tensor_copy(kcst[HD:P], kcst[0:HD]).then_inc(S("kc_lo"), 1)

        @block.tensor
        def _(pe):
            pe.wait_ge(S("kc_lo"), 4)
            pe.matmul(bank[0][:, 0:P], const("spread", NB), vcp[:], start=True, stop=True).then_inc(S("vbd_mm"), 1)

        @block.vector
        def _(dve):
            dve.wait_ge(S("vbd_mm"), 1)
            for h in range(NH):
                g = h // HPG
                dve.tensor_scalar(vbd[:, h, :], bank[0][:, g * HD:(g + 1) * HD], const("headmask")[:, h:h + 1], None,
                                  ALU.mult).then_inc(S("vbd"), 1)
        pe_after = {}

        cursor[0] = mixwork
        pr = place("pr", [P, 2, SEQ], F32)
        pt = place("pt", [P, 2, TT, P], F32)
        pct = place("pct", [P, 2, P], F32)
        cneg = place("cneg", [P, TT, NB], F32)
        stat = place("stat", [P, 2, 2], F32)
        cstat = place("cstat", [P, 2, NH], F32)
        cp = nc.alloc_sbuf_tensor_at("cp", [P, NH, NB], F32, offset=cursor[0])
        cursor[0] += NH * NB * 4
        dwork_at = cursor[0]
        units = []
        for t in range(TT):
            units.append(("cmp", t, 0))
            for h in range(NH):
                units += [("slc", t, h), ("win", t, h)]
        U = len(units)
        psum = banks8[:].rearrange("p b n -> p (b n)")

        def blocks(kind, t):
            return list(range(t + 1)) if kind == "slc" else list(range(max(0, t - WIN // P), t + 1))

        @block.vector
        def _(dve):
            dve.tensor_scalar(cneg[:].rearrange("p t n -> p (t n)"), const("cmpok"), -NEG, NEG, ALU.mult, ALU.add)\
               .then_inc(S("cneg"), 1)
            dve.wait_ge(S("cneg"), 1)

        @block.tensor
        def _(pe):
            for name in ("vbd", "kc_lo", "kc_hi", "zT_lo", "k_twice"):
                pe.wait_ge(S(name), {"vbd": NH, "kc_lo": 5, "kc_hi": 4}.get(name, at(name)))
            for name, v in pe_after.items():
                pe.wait_ge(S(name), v)

        exp_at, scaled, t_mm, t_ev, pv, o_lo = {}, {}, {}, {}, {}, {}
        bank_ev = {4: [], 5: []}

        for u in range(U + 2):
            if u < U:
                kind, t, h = units[u]
                sl = u % 2
                q0 = t * P
                base_col = sl * 1024
                g, br = h // HPG, 0 if kind == "slc" else 1
                ks = blocks(kind, t)
                n = len(ks) * P

                @block.tensor
                def _(pe):
                    if u >= 2:
                        pe.wait_ge(S("s_read"), exp_at[u - 2])
                    if kind == "cmp":
                        for hh in range(NH):
                            o = psum[:, base_col + hh * NB:base_col + (hh + 1) * NB]
                            for part in range(2):
                                last = pe.matmul(o, qst[:, hh, q0:q0 + P], kcst[:, hh // HPG, part, :],
                                                 start=part == 0, stop=part == 1)
                    else:
                        for c in range(0, len(ks), 4):
                            kk = ks[c:c + 4]
                            o = psum[:, base_col + c * P:base_col + c * P + len(kk) * P]
                            masks = [(i, 0) for i, k in enumerate(kk) if k == t] + \
                                    [(i, 1) for i, k in enumerate(kk) if kind == "win" and k == t - WIN // P]
                            for part in range(2):
                                last = pe.matmul(o, qst[:, h, q0:q0 + P],
                                                 kst[:, br, g, part, kk[0] * P:(kk[-1] + 1) * P],
                                                 start=part == 0, stop=part == 1 and not masks)
                            for i, m in masks:
                                last = pe.matmul(o[:, i * P:(i + 1) * P], identb[:], maskb[:, m, :], start=False,
                                                 stop=(i, m) == masks[-1])
                    last.then_inc(S("s_mm"), 1)

                if kind == "cmp":
                    okt = const("cmpok").rearrange("p (t n) -> p t n", n=NB)[:, t, :].unsqueeze(1).to_broadcast([P, NH, NB])
                    neg = cneg[:, t, :].unsqueeze(1).to_broadcast([P, NH, NB])
                    s3 = psum[:, base_col:base_col + NH * NB].rearrange("p (h n) -> p h n", n=NB)
                    p3 = pr[:, sl, 0:NH * NB].rearrange("p (h n) -> p h n", n=NB)

                    def wide(v):
                        return v.unsqueeze(2).to_broadcast([P, NH, NB])

                    @block.vector
                    def _(dve):
                        dve.wait_ge(S("s_mm"), u + 1)
                        dve.wait_ge(S("cm"), at("cm"))
                        dve.tensor_tensor(cp[:], s3, neg, ALU.add).then_inc(S("s_read"), 1)
                        dve.wait_ge(S("s_read"), at("s_read") + 1)
                        dve.reduce_max(cstat[:, 0, :], cp[:], AX_X).then_inc(S("cm"), 1)
                        dve.wait_ge(S("cm"), count("cm"))
                        dve.tensor_tensor(cp[:], cp[:], wide(cstat[:, 0, :]), ALU.subtract).then_inc(S("cm"), 1)
                    exp_at[u] = count("s_read")
                    cm1 = count("cm")

                    @block.scalar
                    def _(act):
                        act.wait_ge(S("cm"), cm1)
                        act.activation(cp[:], cp[:], ACT.Exp).then_inc(S("c_exp"), 1)

                    @block.vector
                    def _(dve):
                        dve.wait_ge(S("c_exp"), t + 1)
                        if u >= 2:
                            dve.wait_ge(S("t_mm"), t_mm[u - 2])
                        dve.tensor_tensor(cp[:], cp[:], okt, ALU.mult).then_inc(S("cm"), 1)
                        dve.wait_ge(S("cm"), count("cm"))
                        dve.reduce_sum(cstat[:, 1, :], cp[:], AX_X).then_inc(S("cm"), 1)
                        dve.wait_ge(S("cm"), count("cm"))
                        dve.tensor_scalar(cstat[:, 1, :], cstat[:, 1, :], 1e-30, None, ALU.max).then_inc(S("cm"), 1)
                        dve.wait_ge(S("cm"), count("cm"))
                        dve.reciprocal(cstat[:, 1, :], cstat[:, 1, :]).then_inc(S("cm"), 1)
                        dve.wait_ge(S("cm"), count("cm"))
                        dve.tensor_tensor(cstat[:, 1, :], cstat[:, 1, :], gs[:, t, 0:NH], ALU.mult).then_inc(S("cm"), 1)
                        dve.wait_ge(S("cm"), count("cm"))
                        dve.tensor_tensor(p3, cp[:], wide(cstat[:, 1, :]), ALU.mult).then_inc(S("p_scaled"), 1)
                        scaled[u] = count("p_scaled")
                        dve.wait_ge(S("p_scaled"), scaled[u])
                else:
                    @block.vector
                    def _(dve):
                        dve.wait_ge(S("s_mm"), u + 1)
                        if u >= 2:
                            dve.wait_ge(S("p_scaled"), scaled[u - 2])
                        dve.reduce_max(stat[:, sl, 0:1], psum[:, base_col:base_col + n], AX_X, negate=True)\
                           .then_inc(S("s_max"), 1)
                        count("s_max")

                    @block.scalar
                    def _(act):
                        act.wait_ge(S("s_max"), at("s_max"))
                        if u >= 2:
                            act.wait_ge(S("t_mm"), t_mm[u - 2])
                        act.wait_ge(S("p_sum"), at("p_sum"))
                        act.activation(pr[:, sl, 0:n], psum[:, base_col:base_col + n], ACT.Exp, bias=stat[:, sl, 0:1],
                                       accum_out=stat[:, sl, 1:2]).then_inc(S("p_exp"), 1)
                        count("p_exp")

                    @block.vector
                    def _(dve):
                        dve.wait_ge(S("p_exp"), at("p_exp"))
                        dve.reciprocal(stat[:, sl, 1:2], stat[:, sl, 1:2]).then_inc(S("s_read"), 1)
                        exp_at[u] = count("s_read")
                        dve.wait_ge(S("s_read"), exp_at[u])
                        col = (1 + br) * NH + h
                        dve.tensor_scalar(pr[:, sl, 0:n], pr[:, sl, 0:n], stat[:, sl, 1:2], gs[:, t, col:col + 1],
                                          ALU.mult, ALU.mult).then_inc(S("p_scaled"), 1)
                        scaled[u] = count("p_scaled")

            if 1 <= u <= U:
                v = u - 1
                kind, t, h = units[v]
                sl = v % 2
                nblk = 1 if kind == "cmp" else len(blocks(kind, t))
                for c in range(0, nblk, 4):
                    m = min(4, nblk - c)
                    b = 4 + c // 4

                    @block.tensor
                    def _(pe):
                        pe.wait_ge(S("p_scaled"), scaled[v])
                        if bank_ev[b]:
                            pe.wait_ge(S("t_ev"), bank_ev[b][-1])
                        for i in range(m):
                            last = pe.transpose(bank[b][:, i * P:(i + 1) * P], pr[:, sl, (c + i) * P:(c + i + 1) * P],
                                                const("ident"))
                        last.then_inc(S("t_mm"), 1)
                        t_mm[v] = count("t_mm")

                    @block.scalar
                    def _(act):
                        act.wait_ge(S("t_mm"), t_mm[v])
                        if kind == "cmp":
                            if t >= 2:
                                act.wait_ge(S("o_mm"), (t - 1) * NH // 2)
                            act.activation(pct[:, t % 2, :], bank[b][:, 0:P], ACT.Copy).then_inc(S("t_ev"), 1)
                        else:
                            if v - 2 in pv:
                                act.wait_ge(S("pv"), pv[v - 2])
                            act.activation(pt[:, sl, c:c + m, :].rearrange("p m q -> p (m q)"), bank[b][:, 0:m * P],
                                           ACT.Copy).then_inc(S("t_ev"), 1)
                        t_ev[v] = count("t_ev")
                        bank_ev[b].append(t_ev[v])

            if u >= 2:
                v = u - 2
                kind, t, h = units[v]
                sl = v % 2
                if kind != "cmp":
                    g, br = h // HPG, 0 if kind == "slc" else 1
                    ks = blocks(kind, t)
                    pair = t * NH // 2 + h // 2
                    o = bank[6 + pair % 2][64 * (h % 2):64 * (h % 2) + 64, 0:P]

                    @block.tensor
                    def _(pe):
                        pe.wait_ge(S("t_ev"), t_ev[v])
                        if kind == "slc":
                            if h % 2 == 0 and pair >= 2:
                                pe.wait_ge(S("o_lo"), pair - 1)
                            pe.matmul(o, vbd[:, h, :], pct[:, t % 2, :], start=True, stop=False)
                        for i, k in enumerate(ks):
                            last = pe.matmul(o, vst[:, br, k, g * HD:(g + 1) * HD], pt[:, sl, i, :], start=False,
                                             stop=kind == "win" and i == len(ks) - 1)
                        pv_end = kind == "win" and h % 2 == 1
                        last.then_inc(S("o_mm" if pv_end else "pv"), 1)
                        if not pv_end:
                            pv[v] = count("pv")
                        else:
                            pv[v] = at("pv")
                    if kind == "win" and h % 2 == 1:
                        @block.scalar
                        def _(act):
                            act.wait_ge(S("o_mm"), pair + 1)
                            act.activation(oahi[:, h // 2, t * P:(t + 1) * P], bank[6 + pair % 2][:, 0:P], ACT.Copy)\
                               .then_inc(S("o_hi"), 1)

                        @block.vector
                        def _(dve):
                            dve.wait_ge(S("o_hi"), pair + 1)
                            dve.tensor_tensor(oalo[:, h // 2, t * P:(t + 1) * P], bank[6 + pair % 2][:, 0:P],
                                              oahi[:, h // 2, t * P:(t + 1) * P], ALU.subtract).then_inc(S("o_lo"), 1)
        at_s_mm = U

        cursor[0] = qst_at
        NKB = NPAGE + WIN // P
        ring = place("ring", [P, 2, NKB, P], F32)
        ktr = place("ktr", [P, 2, NKB, P], F32)
        qpad = place("qpad", [P, NDEC, R], F32)
        dprod = place("dprod", [P, R], F32)
        assert cursor[0] <= vst_at
        cursor[0] = dwork_at
        ptrow = place("ptrow", [1, NDEC * NPAGE], I32)
        cursor[0] = mixwork
        sds = place("sds", [R, PAST + 1], F32)
        sdw = place("sdw", [R, WIN + 1], F32)
        sdc = place("sdc", [R, 4, NB], F32)
        dst = place("dst", [R, 16], F32)
        pdiag = place("pdiag", [R, NDEC, NB], F32)
        ptd = place("ptd", [P, NKB + 1, R], F32)
        osb = place("osb", [NH, NDEC, P], F32)
        newp = place("newp", [R, 2, R], F32)
        newr = place("newr", [NDEC, 2, R], F32)
        ot = place("ot", [P, R], F32)
        oth = place("oth", [P, R], F16)
        otl = place("otl", [P, R], F16)
        assert cursor[0] <= dwork_at
        rounds = 2 * NDEC
        s_mm_end, o_end = at_s_mm, TT * NH // 2

        @block.sync
        def _(sp):
            sp.wait_ge(S("s_mm"), 1)
            sp.dma_start(ptrow[:], I["page_table"].rearrange("(o b) n -> o (b n)", o=1)).then_inc(S("ptrow_in"), 16)
            sp.wait_ge(S("ptrow_in"), 16)
            sp.wait_ge(S("s_mm"), s_mm_end)
            for r in range(rounds):
                kv, b = r // NDEC, r % NDEC
                if r >= 2:
                    sp.wait_ge(S("ring_used"), r - 1)
                for n in range(NPAGE):
                    page = sp.value_load(ptrow[0:1, b * NPAGE + n:b * NPAGE + n + 1], min_val=0, max_val=NPHYS - 1)
                    sp.dma_start(ring[:, r % 2, n:n + 1, :],
                                 I["cache_slc_kv"][0][bass.ds(page, 1), :, kv].rearrange("a p g d -> p a (g d)"))\
                      .then_inc(S(f"ring_in{r % 2}"), 16)
                sp.dma_start(ring[:, r % 2, NPAGE:NKB, :],
                             I["state_win_kv"][0][b, :, kv].rearrange("(c p) g d -> p c (g d)", p=P))\
                  .then_inc(S(f"ring_in{r % 2}"), 16)

        full = 16 * (NPAGE + 1)

        @block.vector
        def _(dve):
            dve.wait_ge(S("s_mm"), s_mm_end)
            dve.wait_ge(S("p_scaled"), at("p_scaled"))
            dve.wait_ge(S("o_lo"), o_end)
            dve.wait_ge(S("pv"), at("pv"))
            dve.wait_ge(S("t_ev"), at("t_ev"))
            dve.memset(qpad[:], 0.0).then_inc(S("dq"), 1)
            dve.wait_ge(S("dq"), 1)
            for b in range(NDEC):
                dve.tensor_copy(qpad[:, b, b * NH:(b + 1) * NH], qd[:, b, :]).then_inc(S("dq"), 1)
            dve.tensor_tensor(dprod[:].rearrange("p (b h) -> p b h", h=NH), qd[:],
                              knt[:, 0, :].unsqueeze(2).to_broadcast([P, NDEC, NH]), ALU.mult).then_inc(S("dq"), 1)

        @block.tensor
        def _(pe):
            pe.wait_ge(S("o_lo"), o_end)
            pe.wait_ge(S("t_ev"), at("t_ev"))
            pe.wait_ge(S("s_read"), at("s_read"))
            pe.wait_ge(S("dq"), 10)
            for b in range(NDEC):
                last = pe.matmul(bank[6][0:R, 0:NB], qpad[:, b, :], kcd[:, b * NB:(b + 1) * NB], start=b == 0,
                                 stop=b == NDEC - 1)
            last.then_inc(S("dc_mm"), 1)
            pe.matmul(bank[7][0:R, 0:1], dprod[:], const("mean")[:, 0:1], start=True, stop=True).then_inc(S("dn_mm"), 1)

        def d(i, n=1):
            return dst[:, i:i + n]

        @block.vector
        def _(dve):
            dve.wait_ge(S("dn_mm"), 1)
            dve.tensor_scalar(sds[:, PAST:PAST + 1], bank[7][0:R, 0:1], float(D), None, ALU.mult).then_inc(S("dq"), 1)
            dve.tensor_tensor(dprod[:].rearrange("p (b h) -> p b h", h=NH), qd[:],
                              knt[:, 1, :].unsqueeze(2).to_broadcast([P, NDEC, NH]), ALU.mult).then_inc(S("dq"), 1)
            dve.wait_ge(S("dc_mm"), 1)
            dve.tensor_copy(sdc[:, 0, :], bank[6][0:R, 0:NB]).then_inc(S("dc"), 1)
            dve.wait_ge(S("dc"), 1)
            dve.reduce_max(d(0), sdc[:, 0, :], AX_X, negate=True).then_inc(S("dc"), 1)

        @block.tensor
        def _(pe):
            pe.wait_ge(S("dq"), 12)
            pe.matmul(bank[7][0:R, 0:1], dprod[:], const("mean")[:, 0:1], start=True, stop=True).then_inc(S("dn_mm"), 1)

        @block.scalar
        def _(act):
            act.wait_ge(S("dc"), 2)
            act.activation(sdc[:, 1, :], sdc[:, 0, :], ACT.Exp, bias=d(0), accum_out=d(1)).then_inc(S("dc_exp"), 1)

        @block.vector
        def _(dve):
            dve.wait_ge(S("dn_mm"), 2)
            dve.tensor_scalar(sdw[:, WIN:WIN + 1], bank[7][0:R, 0:1], float(D), None, ALU.mult).then_inc(S("dq"), 1)
            dve.wait_ge(S("dc_exp"), 1)
            dve.reciprocal(d(1), d(1)).then_inc(S("dc"), 1)
            dve.wait_ge(S("dc"), 3)
            dve.tensor_scalar(sdc[:, 1, :], sdc[:, 1, :], d(1), None, ALU.mult).then_inc(S("dc"), 1)

        @block.tensor
        def _(pe):
            pe.wait_ge(S("dc"), 4)
            pe.wait_ge(S("dq"), 13)
            pe.matmul(bank[7][0:R, 0:NB], const("group", R)[:, 0:R], sdc[:, 1, :], start=True, stop=True)\
              .then_inc(S("imp_mm"), 1)

        @block.vector
        def _(dve):
            order = const("order", R)
            other = slice(1, NB - 1)
            dve.wait_ge(S("imp_mm"), 1)
            dve.tensor_copy(sdc[:, 2, :], bank[7][0:R, 0:NB]).then_inc(S("dc"), 1)
            dve.wait_ge(S("dc"), 5)
            dve.tensor_reduce(d(2), sdc[:, 2, other], AX_X, ALU.min).then_inc(S("dc"), 1)
            dve.wait_ge(S("dc"), 6)
            dve.tensor_scalar(sdc[:, 3, other], sdc[:, 2, other], d(2), None, ALU.is_le).then_inc(S("dc"), 1)
            dve.wait_ge(S("dc"), 7)
            dve.tensor_tensor(sdc[:, 3, other], sdc[:, 3, other], order, ALU.mult).then_inc(S("dc"), 1)
            dve.wait_ge(S("dc"), 8)
            dve.reduce_max(d(3), sdc[:, 3, other], AX_X).then_inc(S("dc"), 1)
            dve.wait_ge(S("dc"), 9)
            dve.tensor_scalar(sdc[:, 3, other], order, d(3), NEG, ALU.is_equal, ALU.mult).then_inc(S("dc"), 1)
            dve.tensor_scalar(sdc[:, 1, :], sdc[:, 1, :], gdec[:, 0:1], None, ALU.mult).then_inc(S("dc"), 1)
            dve.wait_ge(S("dc"), 11)
            dve.tensor_tensor(pdiag[:], sdc[:, 1, :].unsqueeze(1).to_broadcast([R, NDEC, NB]),
                              const("seqmask", R).unsqueeze(2).to_broadcast([R, NDEC, NB]), ALU.mult)\
               .then_inc(S("dc"), 1)

        for r in range(NDEC + 1):
            if r < NDEC:
                @block.tensor
                def _(pe):
                    pe.wait_ge(S(f"ring_in{r % 2}"), full * (r // 2 + 1))
                    for c in range(3):
                        if r >= 1:
                            pe.wait_ge(S("kt_b") if c == 2 else S("kt_a"), r if c == 2 else 2 * r - 1 + c)
                        for i in range(4):
                            last = pe.transpose(bank[3 + c][:, i * P:(i + 1) * P], ring[:, r % 2, 4 * c + i, :],
                                                const("ident"))
                        last.then_inc(S("ring_used" if c == 2 else "kt_mm"), 1)

                @block.scalar
                def _(act):
                    for c in range(2):
                        act.wait_ge(S("kt_mm"), 2 * r + c + 1)
                        if r >= 2:
                            act.wait_ge(S("ds_mm"), r - 1)
                        act.activation(ktr[:, r % 2, 4 * c:4 * c + 4, :].rearrange("p c n -> p (c n)"), bank[3 + c],
                                       ACT.Copy).then_inc(S("kt_a"), 1)

                @block.vector
                def _(dve):
                    dve.wait_ge(S("ring_used"), r + 1)
                    if r >= 2:
                        dve.wait_ge(S("ds_mm"), r - 1)
                    dve.tensor_copy(ktr[:, r % 2, 8:12, :].rearrange("p c n -> p (c n)"), bank[5]).then_inc(S("kt_b"), 1)
            if r >= 1:
                @block.tensor
                def _(pe):
                    b = r - 1
                    pe.wait_ge(S("kt_a"), 2 * b + 2)
                    pe.wait_ge(S("kt_b"), b + 1)
                    for c in range(3):
                        last = pe.matmul(bank[c][0:R, :], qpad[:, b, :],
                                         ktr[:, b % 2, 4 * c:4 * c + 4, :].rearrange("p c n -> p (c n)"),
                                         start=b == 0, stop=b == NDEC - 1)
                    last.then_inc(S("ds_mm"), 1)

        @block.vector
        def _(dve):
            dve.wait_ge(S("ds_mm"), NDEC)
            dve.wait_ge(S("dc"), 12)
            dve.tensor_copy(sds[:, 0:PAST], psum[0:R, 0:PAST]).then_inc(S("dx"), 1)
            dve.tensor_copy(sdw[:, 0:WIN], bank[2][0:R, :]).then_inc(S("dx"), 1)
            dve.wait_ge(S("dx"), 2)
            kept = sds[:, BLK:BLK * (NB - 1)].rearrange("p (n l) -> p n l", l=BLK)
            dve.tensor_tensor(kept, kept, sdc[:, 3, 1:NB - 1].unsqueeze(2).to_broadcast([R, NB - 2, BLK]), ALU.add)\
               .then_inc(S("dx"), 1)
            dve.memset(sdw[:, 0:1], NEG).then_inc(S("dx"), 1)
            dve.wait_ge(S("dx"), 4)
            dve.reduce_max(d(4), sds[:], AX_X, negate=True).then_inc(S("dx"), 1)
            dve.reduce_max(d(5), sdw[:], AX_X, negate=True).then_inc(S("dx"), 1)

        @block.scalar
        def _(act):
            act.wait_ge(S("dx"), 6)
            act.activation(sds[:], sds[:], ACT.Exp, bias=d(4), accum_out=d(6)).then_inc(S("dx_exp"), 1)
            act.activation(sdw[:], sdw[:], ACT.Exp, bias=d(5), accum_out=d(7)).then_inc(S("dx_exp"), 1)

        @block.vector
        def _(dve):
            dve.wait_ge(S("dx_exp"), 2)
            dve.reciprocal(d(6, 2), d(6, 2)).then_inc(S("dx"), 1)
            dve.wait_ge(S("dx"), 7)
            dve.tensor_scalar(sds[:], sds[:], d(6), gdec[:, 1:2], ALU.mult, ALU.mult).then_inc(S("dx"), 1)
            dve.tensor_scalar(sdw[:], sdw[:], d(7), gdec[:, 2:3], ALU.mult, ALU.mult).then_inc(S("dx"), 1)
            dve.wait_ge(S("dx"), 9)
            for br, col in ((0, sds[:, PAST:PAST + 1]), (1, sdw[:, WIN:WIN + 1])):
                dve.tensor_scalar(newp[:, br, :], const("ident", R)[:, 0:R], col, None, ALU.mult).then_inc(S("dx"), 1)

        @block.tensor
        def _(pe):
            pe.wait_ge(S("dx"), 9)
            pe.wait_ge(S("kt_a"), 2 * NDEC)
            pe.wait_ge(S("kt_b"), NDEC)
            for i in range(NPAGE):
                last = pe.transpose(bank[3][:, i * R:(i + 1) * R], sds[:, i * P:(i + 1) * P], const("ident", R)[:, 0:R])
            last.then_inc(S("dp_mm"), 1)
            for i in range(WIN // P):
                pe.transpose(bank[4][:, i * R:(i + 1) * R], sdw[:, i * P:(i + 1) * P], const("ident", R)[:, 0:R])
            pe.transpose(bank[4][:, 4 * R:5 * R], pdiag[:].rearrange("p b n -> p (b n)"), const("ident", R)[:, 0:R])\
              .then_inc(S("dp_mm"), 1)
            pe.wait_ge(S("dx"), 11)
            for br in range(2):
                last = pe.matmul(bank[5][0:NDEC, br * R:(br + 1) * R], const("seqmask", R), newp[:, br, :],
                                 start=True, stop=True)
            last.then_inc(S("dp_mm"), 1)

        @block.vector
        def _(dve):
            dve.wait_ge(S("dp_mm"), 1)
            dve.tensor_copy(ptd[:, 0:NPAGE, :].rearrange("p c n -> p (c n)"), bank[3]).then_inc(S("dp"), 1)
            dve.wait_ge(S("dp_mm"), 2)
            dve.tensor_copy(ptd[:, NPAGE:NKB + 1, :].rearrange("p c n -> p (c n)"), bank[4][:, 0:5 * R])\
               .then_inc(S("dp"), 1)
            dve.wait_ge(S("dp_mm"), 3)
            dve.tensor_copy(newr[:].rearrange("p c n -> p (c n)"), bank[5][0:NDEC, 0:2 * R]).then_inc(S("dp"), 1)

        @block.tensor
        def _(pe):
            pe.wait_ge(S("dp"), 3)
            for r in range(NDEC, rounds):
                b = r - NDEC
                pe.wait_ge(S(f"ring_in{r % 2}"), full * (r // 2 + 1))
                for i in range(NKB):
                    last = pe.matmul(psum[0:NH, b * P:(b + 1) * P], ptd[:, i, b * NH:(b + 1) * NH], ring[:, r % 2, i, :],
                                     start=i == 0, stop=i == NKB - 1)
                last.then_inc(S("ring_used"), 1)

        @block.vector
        def _(dve):
            dve.wait_ge(S("ring_used"), rounds)
            dve.tensor_copy(osb[:].rearrange("p b n -> p (b n)"), psum[0:NH, 0:NDEC * P]).then_inc(S("dp"), 1)

        @block.tensor
        def _(pe):
            o = bank[2][:, 0:R]
            pe.matmul(o, vcd[:], ptd[:, NKB, :], start=True, stop=False)
            for br in range(2):
                pe.matmul(o, vst[0:NDEC, br, TT, :], newr[:, br, :], start=False, stop=False)
            pe.wait_ge(S("dp"), 4)
            for b in range(NDEC):
                last = pe.matmul(o[:, b * NH:(b + 1) * NH], osb[:, b, :], const("ident", NH)[:, 0:NH], start=False,
                                 stop=b == NDEC - 1)
            last.then_inc(S("dp_mm"), 1)

        @block.vector
        def _(dve):
            dve.wait_ge(S("dp_mm"), 4)
            dve.tensor_copy(oth[:], bank[2][:, 0:R]).then_inc(S("dp"), 1)
            dve.wait_ge(S("dp"), 5)
            dve.tensor_tensor(otl[:], bank[2][:, 0:R], oth[:], ALU.subtract).then_inc(S("dp"), 1)
            dve.wait_ge(S("dp"), 6)
            for dst_, src in ((oahi, oth), (oalo, otl)):
                for h in range(NH):
                    g, to = h // HPG, 64 * (h % 2)
                    dve.tensor_copy(dst_[to:to + 64, h // 2, SEQ:T],
                                    src[64 * g:64 * g + 64, :].rearrange("p (b h) -> p b h", h=NH)[:, :, h])\
                       .then_inc(S("dp"), 1)

        cursor[0] = qst_at
        cihi = place("cihi", [P, KC, T], F16)
        cilo = place("cilo", [P, KC, T], F16)
        mhi = place("mhi", [P, KD, T], F16)
        mlo = place("mlo", [P, KD, T], F16)
        late_at = cursor[0]
        hc = place("hc", [P, T], F32)
        uc = place("uc", [P, 2, T + 2], F32)
        yc = place("yc", [P, T], F32)
        ci = hc
        srow = place("srow", [2 * NDEC, DCONV], F32)
        stc = place("stc", [P, KC, 2 * NDEC], F32)
        tail = place("tail", [2, DCONV], F32)
        ulast = place("ulast", [NDEC, DCONV], F32)
        o_ready = at("o_lo")

        @block.sync
        def _(sp):
            for n in range(3 * KC):
                c, kind = n // 3, n % 3
                col = CONV0 + (0, 2 * DCONV, DCONV)[kind] + c * P
                load_const(sp, sconv + n, cols(col, P), KD)
                if n == 1:
                    sp.wait_ge(S("dp"), 22)
                    sp.dma_start(srow[:], I["state_conv"][0].rearrange("b j n -> (b j) n")).then_inc(S("srow_in"), 16)
                    sp.dma_start(O["conv_sample"][0][:, 0, :], I["state_conv"][0][:, 1, :]).then_inc(S("conv_shift"), 16)

        @block.gpsimd
        def _(pool):
            for n in range(3 * KC):
                split_const(pool, sconv + n, KD * P)

        @block.vector
        def _(dve):
            dve.wait_ge(S("dp"), 22)
            dve.memset(uc[:, :, 0:2], 0.0).then_inc(S("u_clear"), 1)

        @block.tensor
        def _(pe):
            pe.wait_ge(S("dp"), 6)
            pe.wait_ge(S("srow_in"), 16)
            for c in range(KC):
                last = pe.transpose(bank[6][:, c * 2 * NDEC:(c + 1) * 2 * NDEC], srow[:, c * P:(c + 1) * P],
                                    const("ident", 2 * NDEC)[:, 0:2 * NDEC])
            last.then_inc(S("stc_mm"), 1)

        @block.vector
        def _(dve):
            dve.wait_ge(S("stc_mm"), 1)
            dve.tensor_copy(stc[:].rearrange("p c n -> p (c n)"), bank[6][:, 0:KC * 2 * NDEC]).then_inc(S("stc"), 1)
            dve.wait_ge(S("stc"), 1)

        W = par2[:, 0:3 * KC].rearrange("p (j c) -> p j c", j=3)
        for n in range(3 * KC):
            c, kind = n // 3, n % 3
            s = sconv + n

            @block.tensor
            def _(pe):
                w1, w2 = slab_parts(s % 4, KD)
                pe.wait_ge(slab_split, s + 1)
                for j in range(NJ):
                    a, b = third(j)
                    if n >= 2:
                        m = n - 2
                        name, v = {0: ("hc", m // 3 * 3 + j + 1), 1: ("uc", m // 3 * 3 + j + 1),
                                   2: ("ci", m // 3 * 3 + j + 1)}[m % 3]
                        pe.wait_ge(S(name), v)
                    for k in range(KD):
                        last = product(pe, bank[3 * (n % 2) + j][:, 0:TJ], w1[:, k, :], w2[:, k, :], ahi[:, k, a:b],
                                       alo[:, k, a:b], k == 0, k == KD - 1)
                    last.then_inc(S("cv_mm") if j < 2 else slab_used, 1)

            def arrived_third(eng, j):
                eng.wait_ge(S("cv_mm") if j < 2 else slab_used, 2 * n + j + 1 if j < 2 else s + 1)

            if kind == 0:
                @block.scalar
                def _(act):
                    for j in range(NJ):
                        a, b = third(j)
                        arrived_third(act, j)
                        if c == 0:
                            act.wait_ge(S("u_clear"), 1)
                        if c >= 1:
                            act.wait_ge(S("ci_lo"), (c - 1) * 3 + j + 1)
                        act.activation(hc[:, a:b], bank[3 * (n % 2) + j][:, 0:TJ], ACT.Copy, scale=IWS)\
                           .then_inc(S("hc"), 1)
            elif kind == 1:
                @block.vector
                def _(dve):
                    for j in range(NJ):
                        a, b = third(j)
                        arrived_third(dve, j)
                        dve.wait_ge(S("hc"), 3 * c + j + 1)
                        if c >= 2:
                            dve.wait_ge(S("tail_mm"), c - 1)
                        dve.scalar_tensor_tensor(out=uc[:, c % 2, 2 + a:2 + b], in0=bank[3 * (n % 2) + j][:, 0:TJ],
                                                 scalar=IWS, in1=hc[:, a:b], op0=ALU.mult, op1=ALU.mult)\
                           .then_inc(S("uc"), 1)
                    dve.wait_ge(S("uc"), 3 * c + 3)
                    if c >= 1:
                        dve.wait_ge(S("ci"), 3 * c)
                    sd = stc[:, c, :].rearrange("p (b j) -> p j b", j=2)
                    u = uc[:, c % 2, :]
                    dve.tensor_scalar(yc[:, 0:SEQ], u[:, 2:2 + SEQ], W[:, 2, c:c + 1], None, ALU.mult)\
                       .then_inc(S("taps"), 1)
                    dve.tensor_scalar(yc[:, SEQ:T], u[:, 2 + SEQ:2 + T], W[:, 2, c:c + 1], None, ALU.mult)\
                       .then_inc(S("taps"), 1)
                    dve.wait_ge(S("taps"), 6 * c + 2)
                    dve.scalar_tensor_tensor(out=yc[:, 0:SEQ], in0=u[:, 1:1 + SEQ], scalar=W[:, 1, c:c + 1],
                                             in1=yc[:, 0:SEQ], op0=ALU.mult, op1=ALU.add).then_inc(S("taps"), 1)
                    dve.scalar_tensor_tensor(out=yc[:, SEQ:T], in0=sd[:, 1, :], scalar=W[:, 1, c:c + 1],
                                             in1=yc[:, SEQ:T], op0=ALU.mult, op1=ALU.add).then_inc(S("taps"), 1)
                    dve.wait_ge(S("taps"), 6 * c + 4)
                    dve.scalar_tensor_tensor(out=yc[:, 0:SEQ], in0=u[:, 0:SEQ], scalar=W[:, 0, c:c + 1],
                                             in1=yc[:, 0:SEQ], op0=ALU.mult, op1=ALU.add).then_inc(S("taps"), 1)
                    dve.scalar_tensor_tensor(out=yc[:, SEQ:T], in0=sd[:, 0, :], scalar=W[:, 0, c:c + 1],
                                             in1=yc[:, SEQ:T], op0=ALU.mult, op1=ALU.add).then_inc(S("taps"), 1)
                    dve.wait_ge(S("taps"), 6 * c + 6)
            else:
                @block.tensor
                def _(pe):
                    pe.wait_ge(S("uc"), 3 * c + 3)
                    if c == 0:
                        pe.wait_ge(S("stc"), 1)
                    pe.transpose(bank[6][0:2, c * P:(c + 1) * P], uc[:, c % 2, SEQ:SEQ + 2], const("ident"))
                    pe.transpose(bank[7][0:NDEC, c * P:(c + 1) * P], uc[:, c % 2, 2 + SEQ:2 + T], const("ident"))\
                      .then_inc(S("tail_mm"), 1)

                @block.vector
                def _(dve):
                    for j in range(NJ):
                        a, b = third(j)
                        arrived_third(dve, j)
                        if c >= 1:
                            dve.wait_ge(S("ci_lo"), 3 * c - 2 + j)
                        dve.scalar_tensor_tensor(out=ci[:, a:b], in0=bank[3 * (n % 2) + j][:, 0:TJ], scalar=IWS,
                                                 in1=yc[:, a:b], op0=ALU.mult, op1=ALU.mult).then_inc(S("ci"), 1)

                @block.scalar
                def _(act):
                    for j in range(NJ):
                        a, b = third(j)
                        act.wait_ge(S("ci"), 3 * c + j + 1)
                        act.activation(cihi[:, c, a:b], ci[:, a:b], ACT.Copy).then_inc(S("ci_hi"), 1)

                @block.vector
                def _(dve):
                    for j in range(NJ):
                        a, b = third(j)
                        dve.wait_ge(S("ci_hi"), 3 * c + j + 1)
                        dve.tensor_tensor(cilo[:, c, a:b], ci[:, a:b], cihi[:, c, a:b], ALU.subtract)\
                           .then_inc(S("ci_lo"), 1)

        @block.vector
        def _(dve):
            dve.wait_ge(S("tail_mm"), KC)
            dve.tensor_copy(tail[:], bank[6][0:2, :]).then_inc(S("tail"), 1)
            dve.tensor_copy(ulast[:], bank[7][0:NDEC, :]).then_inc(S("tail"), 1)

        @block.scalar
        def _(act):
            act.wait_ge(S("tail"), 2)
            act.dma_start(O["conv_prompt"][0, 0], tail[:]).then_inc(S("conv_out_p"), 16)
            act.dma_start(O["conv_sample"][0][:, 1, :], ulast[:]).then_inc(S("conv_out_s"), 16)
        out_sems.extend(["win_shift", "conv_shift", "conv_out_p", "conv_out_s"])

        cursor[0] = late_at + 0
        sgm = place("sgm", [P, NJ, TJ], F32)
        mm = place("mm", [P, 2, NJ, TJ], F32)
        assert cursor[0] <= late_at + 4 * (4 * T + 4)

        @block.sync
        def _(sp):
            with sp.Fori(0, KD) as i:
                for v in range(4):
                    if v % 2 == 0:
                        src = w_in[:, bass.ds(i * P + (MERGE0 + v // 2 * D), P)].rearrange("(k p) n -> p k n", p=P)
                        load_slab(sp, i * 4 + (smerge + v), v, src, KD)
                    else:
                        w = (I["w_attn_up"] if v == 1 else I["w_conv_out"])[0]
                        load_slab(sp, i * 4 + (smerge + v), v,
                                  w[:, bass.ds(i * P, P)].rearrange("(k p) n -> p k n", p=P), KC)
            with sp.Fori(0, KD // 4) as i:
                for v in range(4):
                    load_slab(sp, i * 4 + (sout + v), v,
                              I["w_out"][0][:, bass.ds(i * (4 * P) + v * P, P)].rearrange("(k p) n -> p k n", p=P), KD)

        @block.gpsimd
        def _(pool):
            with pool.Fori(0, KD) as i:
                for v in range(4):
                    split_slab(pool, smerge, i * 4, v, (KD if v % 2 == 0 else KC) * P)
            with pool.Fori(0, KD // 4) as i:
                for v in range(4):
                    split_slab(pool, sout, i * 4, v, KD * P)

        ysq0, y0, acc0, group0 = at("ysq"), at("y"), at("acc_done"), at("group")

        @block.tensor
        def _(pe):
            pe.wait_ge(S("uc"), 3 * KC)
            pe.wait_ge(S("dp"), 22)
            pe.wait_ge(S("o_lo"), o_ready)
            pe.wait_ge(S("ci_lo"), 3 * KC)
            with pe.Fori(0, KD) as i:
                for v in range(4):
                    s = i * 4 + (smerge + v)
                    nk = KD if v % 2 == 0 else KC
                    x1, x2 = ((ahi, alo), (oahi, oalo), (ahi, alo), (cihi, cilo))[v]
                    w1, w2 = slab_parts(v, nk)
                    pe.wait_ge(slab_split, s + 1)
                    for j in range(NJ):
                        a, b = third(j)
                        pe.wait_ge(S("mg_sig" if v % 2 == 0 else "mg_mul"), i * 6 + (v // 2 * 3 + j + 1))
                        for k in range(nk):
                            last = product(pe, bank[j + 3 * (v % 2)][:, 0:TJ], w1[:, k, :], w2[:, k, :], x1[:, k, a:b],
                                           x2[:, k, a:b], k == 0, k == nk - 1)
                        last.then_inc(S("mg_mm") if j < 2 else slab_used, 1)
            pe.wait_ge(S("mg_sig"), 3 + 6 * KD)
            pe.wait_ge(S("mg_mul"), 3 + 6 * KD)
            with pe.Fori(0, KD // 4) as i:
                for v in range(4):
                    s = i * 4 + (sout + v)
                    w1, w2 = slab_parts(v, KD)
                    pe.wait_ge(slab_split, s + 1)
                    for j in range(NJ):
                        a, b = third(j)
                        pe.wait_ge(S("mg_lo"), 3 + NJ * (KD - 1) + j + 1)
                        pe.wait_ge(S("ysq"), i * 12 + (ysq0 + 3 * v + j + 1))
                        for k in range(KD):
                            last = product(pe, bank[3 * (v % 2) + j][:, 0:TJ], w1[:, k, :], w2[:, k, :], mhi[:, k, a:b],
                                           mlo[:, k, a:b], k == 0, k == KD - 1)
                        last.then_inc(S("group") if j < 2 else slab_used, 1)

        @block.scalar
        def _(act):
            act.wait_ge(S("ci_lo"), 3 * KC)
            act.sem_inc(S("mg_sig"), 3)
            with act.Fori(0, KD) as i:
                for half in range(2):
                    for j in range(NJ):
                        a, b = third(j)
                        if j < 2:
                            act.wait_ge(S("mg_mm"), i * 8 + (4 * half + j + 1))
                        else:
                            act.wait_ge(slab_used, i * 4 + (smerge + 2 * half + 1))
                        act.wait_ge(S("mg_mul"), i * 6 + (3 * half + j + 1))
                        act.activation(sgm[:, j, :], bank[j][:, 0:TJ], ACT.Sigmoid, scale=IWS).then_inc(S("mg_sig"), 1)
                for j in range(NJ):
                    a, b = third(j)
                    act.wait_ge(S("mg_add"), i * 3 + (j + 1))
                    act.activation(mhi[:, bass.ds(i, 1), a:b], mm[:, 0, j, :].unsqueeze(1), ACT.Copy)\
                       .then_inc(S("mg_hi"), 1)
            act.sem_inc(S("ysq"), 6)
            with act.Fori(0, KD // 4) as i:
                for v in range(4):
                    for j in range(NJ):
                        a, b = third(j)
                        if j < 2:
                            act.wait_ge(S("group"), i * 8 + (group0 + 2 * v + j + 1))
                        else:
                            act.wait_ge(slab_used, i * 4 + (sout + v + 1))
                        act.activation(y[:, bass.ds(i * 4 + v, 1), a:b], bank[3 * (v % 2) + j][:, 0:TJ].unsqueeze(1),
                                       ACT.Copy, scale=IWS).then_inc(S("y"), 1)
                        act.wait_ge(S("acc_done"), i * 12 + (acc0 + 3 * v + j + 1))
                        act.activation(sq[:, j, :], bank[3 * (v % 2) + j][:, 0:TJ], ACT.Square, scale=IWS)\
                           .then_inc(S("ysq"), 1)

        @block.vector
        def _(dve):
            dve.wait_ge(S("ci_lo"), 3 * KC)
            dve.sem_inc(S("mg_mul"), 3)
            dve.sem_inc(S("mg_lo"), 3)
            with dve.Fori(0, KD) as i:
                for half in range(2):
                    for j in range(NJ):
                        if j < 2:
                            dve.wait_ge(S("mg_mm"), i * 8 + (4 * half + 2 + j + 1))
                        else:
                            dve.wait_ge(slab_used, i * 4 + (smerge + 2 * half + 2))
                        dve.wait_ge(S("mg_sig"), i * 6 + (3 + 3 * half + j + 1))
                        dve.wait_ge(S("mg_lo"), i * 3 + (j + 1))
                        dve.scalar_tensor_tensor(out=mm[:, half, j, :], in0=bank[3 + j][:, 0:TJ], scalar=IWS,
                                                 in1=sgm[:, j, :], op0=ALU.mult, op1=ALU.mult).then_inc(S("mg_mul"), 1)
                for j in range(NJ):
                    dve.wait_ge(S("mg_mul"), i * 6 + (3 + 3 + j + 1))
                    dve.tensor_tensor(mm[:, 0, j, :], mm[:, 0, j, :], mm[:, 1, j, :], ALU.add).then_inc(S("mg_add"), 1)
                for j in range(NJ):
                    a, b = third(j)
                    dve.wait_ge(S("mg_hi"), i * 3 + (j + 1))
                    dve.tensor_tensor(mlo[:, bass.ds(i, 1), a:b], mm[:, 0, j, :].unsqueeze(1),
                                      mhi[:, bass.ds(i, 1), a:b], ALU.subtract).then_inc(S("mg_lo"), 1)
            dve.wait_ge(S("conv_out_p"), 16)
            dve.wait_ge(S("conv_out_s"), 16)
            for j in range(NJ):
                dve.memset(acc[:, j, :], 0.0).then_inc(S("acc_done"), 1)
            with dve.Fori(0, KD // 4) as i:
                for v in range(4):
                    for j in range(NJ):
                        m = 3 * v + j
                        dve.wait_ge(S("ysq"), i * 12 + (ysq0 + 6 + m + 1))
                        dve.wait_ge(S("acc_done"), i * 12 + (acc0 + m + 1))
                        dve.tensor_tensor(acc[:, j, :], acc[:, j, :], sq[:, j, :], ALU.add).then_inc(S("acc_done"), 1)

        count("group", 2 * KD)
        count("ysq", 6 + NJ * KD)
        count("y", NJ * KD)
        count("acc_done", NJ + NJ * KD)
        return out_sems

    total["slab"] = NSTART

    def x_loaded(eng, j):
        eng.wait_ge(S("xT_a"), min(TT + 1, (third(j)[1] - 1) // P + 1))
        eng.wait_ge(S("xT_b"), min(TT + 1, (third(j)[1] - 1) // P + 1))

    a_ready = boundary(None, 0, x_loaded)
    ffn(0, a_ready, True)
    a_ready = boundary(0, 1)
    out_sems = mixer(a_ready)
    a_ready = boundary(1, 2)
    ffn(1, a_ready, False)
    boundary(2, None)

    @block.sync
    def _(sp):
        for name in out_sems:
            sp.wait_ge(S(name), 16)
    last = at("x_new"), at("dec_u")

    def all_x(pe):
        pe.wait_ge(S("x_new"), last[0])
        pe.wait_ge(S("dec_u"), last[1])
    write_out(all_x)
    block_cm.__exit__(None, None, None)


_INS = ["x_prompt", "x_sample", "c_prompt", "c_sample", "cache_cmp_kv", "cache_slc_kv", "state_win_kv", "state_conv",
        "page_table", "w_ada", "b_ada", "g_norm", "w_ffn_gu", "w_ffn_down", "w_in", "phi_pe", "phi_w1", "phi_b1",
        "phi_w2", "w_attn_up", "conv_w", "w_conv_out", "w_out"]
_OUTS = [("y_prompt", (1, SEQ, D)), ("y_sample", (NDEC, 1, D)),
         ("cmp_kv_prompt", (1, 1, SEQ, 2, NG, HD)), ("slc_kv_prompt", (1, 1, SEQ, 2, NG, HD)),
         ("win_kv_prompt", (1, 1, WIN, 2, NG, HD)), ("conv_prompt", (1, 1, 2, DCONV)),
         ("cmp_kv_sample", (1, NDEC, 1, 2, NG, HD)), ("slc_kv_sample", (1, NDEC, 1, 2, NG, HD)),
         ("win_kv_sample", (1, NDEC, WIN, 2, NG, HD)), ("conv_sample", (1, NDEC, 2, DCONV))]


def kernel(**inputs):
    import numpy as _np
    import concourse.bacc as _bacc
    from concourse import mybir as _mybir
    from concourse.bass_utils import run_bass_kernel_spmd as _run

    nc = _bacc.Bacc("TRN2", target_bir_lowering=False, num_devices=1)
    arrays, ins, outs = {}, {}, {}
    made = {"consts": shape_constants()[0], "masks": mask_constants()}
    for name in _INS + list(made):
        a = made[name] if name in made else _np.ascontiguousarray(inputs[name])
        arrays[f"in_{name}_dram"] = a
        ins[name] = nc.dram_tensor(f"in_{name}_dram", a.shape, _mybir.dt.from_np(a.dtype), kind="ExternalInput").ap()
    for name, shape in _OUTS:
        outs[name] = nc.dram_tensor(f"out_{name}_dram", shape, _mybir.dt.float32, kind="ExternalOutput").ap()
    build_program(nc, ins, outs)
    r = _run(nc, [arrays], core_ids=[0])
    return tuple(r.results[0][f"out_{name}_dram"] for name, _ in _OUTS)
```

```python
from contextlib import ExitStack

import numpy as np

import concourse.bass as bass
from concourse import mybir

ACT = mybir.ActivationFunctionType
ALU = mybir.AluOpType
F32 = mybir.dt.float32
F16 = mybir.dt.float16
BF16 = mybir.dt.bfloat16
I32 = mybir.dt.int32
AX_X = mybir.AxisListType.X

P = 128
D = 1024
KD = D // P
SEQ = 1024
NDEC = 8
T = SEQ + NDEC
NJ = 3
TJ = T // NJ
TT = SEQ // P
NSEQ = 1 + NDEC
DFF = 2816
KF = DFF // P
NH, HD, NG, HPG = 8, 64, 2, 4
PAST, PAGE = 1024, 128
NPAGE = PAST // PAGE
NPHYS = 80
BLK = 64
NB = SEQ // BLK
WIN = 512
HID = 128
DCONV = 512
KC = DCONV // P
QC, KVC, GC = NH * HD, 6 * NG * HD, 3 * NH
CONV0 = QC + KVC + GC
MERGE0 = CONV0 + 3 * DCONV
WS = 64.0
IWS = 1.0 / WS
SLAB = 11 * P
EPS = 1e-6
NEG = -1e30
NMOD = 9 * KD
NSTART = 2 * KD


def shape_constants():
    q = np.arange(P)[:, None]
    k = np.arange(P)[None, :]
    parts = {}
    parts["ident"] = (q == k).astype(np.float32)
    parts["mean"] = np.full((P, P), 1.0 / D, np.float32)
    pos = np.arange(SEQ).reshape(TT, P).T[:, :, None]
    parts["cmpok"] = ((np.arange(NB)[None, None, :] + 1) * BLK <= pos + 1).astype(np.float32).reshape(P, TT * NB)
    half = HD // 8
    inv = np.power(np.float32(500000.0), -np.arange(half, dtype=np.float32) * np.float32(2.0) / np.float32(2 * half))
    allpos = np.full((P, TT + 1), PAST, np.float32)
    allpos[:, :TT] = np.arange(SEQ, dtype=np.float32).reshape(TT, P).T
    ang = allpos[:, :, None] * inv[None, None, :].astype(np.float32)
    parts["cos"] = np.cos(ang).astype(np.float32).reshape(P, -1)
    parts["sin"] = np.sin(ang).astype(np.float32).reshape(P, -1)
    row = np.arange(P)[:, None]
    parts["seqmask"] = (row // NH == np.arange(NDEC)[None, :]).astype(np.float32)
    parts["headmask"] = (row // NB == np.arange(NH)[None, :]).astype(np.float32)
    parts["group"] = (row // HPG == np.arange(NDEC * NH)[None, :] // HPG).astype(np.float32)
    parts["spread"] = (row == np.arange(P)[None, :] % NB).astype(np.float32)
    parts["order"] = np.broadcast_to(np.arange(1, NB - 1, dtype=np.float32), (P, NB - 2))
    parts["seqrep"] = (row == np.arange(NDEC * NH)[None, :] // NH).astype(np.float32)
    parts["ownhead"] = (row % NH == np.arange(NH)[None, :]).astype(np.float32)
    parts["blockrow"] = ((row % 2) * 16 + np.arange(16)[None, :]).astype(np.float32)
    parts["eps"] = np.full((P, 1), EPS, np.float32)
    at, where = 0, {}
    for n, a in parts.items():
        where[n] = (at, at + a.shape[1])
        at += a.shape[1]
    return np.concatenate(list(parts.values()), axis=1).astype(np.float32), where


def mask_constants():
    q, k = np.arange(P)[:, None], np.arange(P)[None, :]
    return np.concatenate([np.where(k > q, NEG, 0.0), np.where(k <= q, NEG, 0.0)], axis=1).astype(np.float32)


def third(j):
    return j * TJ, (j + 1) * TJ


def build_program(nc, I, O):
    consts, CW = shape_constants()
    NCONST = consts.shape[1]

    cursor = [16512]

    def place(name, shape, dt, size=None):
        n = int(np.prod(shape[1:])) * (2 if dt in (F16, BF16) else 4)
        n = (n + 31) // 32 * 32
        t = nc.alloc_sbuf_tensor_at(name, shape, dt, offset=cursor[0])
        cursor[0] += n
        assert cursor[0] <= 229344, (name, cursor[0])
        return t

    cst = place("cst", [P, NCONST], F32)
    identb = place("identb", [P, P], BF16)
    maskb = place("maskb", [P, 2, P], BF16)
    x = place("x", [P, KD, T], F32)
    mod0 = place("mod0", [P, NSTART, NSEQ], F32)
    mods = place("mods", [P, NMOD - NSTART, 2, NSEQ], F32)
    scaleA = place("scaleA", [P, 3, KD, NSEQ], F32)
    gateC = place("gateC", [P, 3, KD, NSEQ], F32)
    par1 = place("par1", [P, 120], F32)
    par2 = place("par2", [P, 78], F32)
    cshl = place("cshl", [P, KD, 2, NSEQ], F16)
    csh, csl = cshl[:, :, 0, :], cshl[:, :, 1, :]
    rs_at = cursor[0]
    rs = place("rs", [P, NJ, TJ], F32)
    sq_at = cursor[0]
    sq = place("sq", [P, NJ, TJ], F32)
    cursor[0] = sq_at
    pair = place("pair", [P, 2, 2, TJ], F32)
    decd = place("decd", [P, 2, KD, NDEC], F32)
    stage = place("stage", [P, 2, SLAB], F32)
    whi = place("whi", [P, 4, SLAB], F16)
    wlo = place("wlo", [P, 4, SLAB], F16)
    a_at = cursor[0]
    ahi = place("ahi", [P, KD, T], F16)
    alo = place("alo", [P, KD, T], F16)
    y = nc.alloc_sbuf_tensor_at("y", [P, KD, T], F32, offset=a_at)
    free_at = cursor[0]

    hhi = place("hhi", [P, KF, T], F16)
    hlo = place("hlo", [P, KF, T], F16)
    sg = nc.alloc_sbuf_tensor_at("sg", [P, NJ, TJ], F32, offset=sq_at)
    h32 = nc.alloc_sbuf_tensor_at("h32", [P, NJ, TJ], F32, offset=rs_at)
    acc = nc.alloc_sbuf_tensor_at("acc", [P, NJ, TJ], F32, offset=rs_at)
    sqx = nc.alloc_sbuf_tensor_at("sqx", [P, 2, KD, TJ], F32, offset=free_at)
    cursor[0] = free_at
    xrow = place("xrow", [P, 4, D], F32)
    crow = place("crow", [NSEQ, 2, D], F32)
    first = place("first", [P, NSTART // 4, KD, 4 * P], F32)
    cs32 = place("cs32", [P, KD, NSEQ], F32)
    prow = nc.alloc_sbuf_tensor_at("prow", [P, 2, P], F32, offset=sq_at)
    mrow = nc.alloc_sbuf_tensor_at("mrow", [P, 2, P], F32, offset=sq_at + 2 * P * 4)

    banks8 = nc.alloc_psum_tensor("banks8", [P, 8, 512], F32)
    bank = [banks8[:, n, :] for n in range(8)]

    def mod(q0, n=KD):
        return mod0[:, q0:q0 + n, :] if q0 < NSTART else mods[:, q0 - NSTART:q0 - NSTART + n, 0, :]

    def const(name, rows=P):
        a, b = CW[name]
        return cst[0:rows, a:b]

    sem = {}

    def S(name):
        if name not in sem:
            sem[name] = nc.alloc_semaphore(name)
        return sem[name]

    total = {}

    def count(name, n=1):
        total[name] = total.get(name, 0) + n
        return total[name]

    def at(name):
        return total.get(name, 0)

    stage_full = [S("stage_full0"), S("stage_full1")]
    slab_split, slab_used, slab_hi, slab_scaled = S("slab_split"), S("slab_used"), S("slab_hi"), S("slab_scaled")

    def slab_parts(u, kk, w=P):
        return (whi[:, u, 0:kk * w].rearrange("p (k n) -> p k n", k=kk),
                wlo[:, u, 0:kk * w].rearrange("p (k n) -> p k n", k=kk))

    def standing(eng, s, name):
        if not isinstance(s, int):
            eng.sem_inc(S(name), 1)

    def load_slab(sp, s, v, src, kk, w=P):
        if not isinstance(s, int) or s >= NSTART + 2:
            sp.wait_ge(slab_split, s - 1)
            standing(sp, s, "loads_let_go")
        sp.dma_start(stage[:, v % 2, 0:kk * w].rearrange("p (k n) -> p k n", k=kk), src)\
          .then_inc(stage_full[v % 2], 16)

    def arrived(eng, s0, i4, v):
        eng.wait_ge(stage_full[v % 2], i4 * 8 + (s0 // 2 + v // 2 + 1) * 16)

    def split_slab(pool, s0, i4, v, n):
        s = i4 + (s0 + v)
        arrived(pool, s0, i4, v)
        pool.wait_ge(slab_used, s - 3)
        standing(pool, s, "splits_let_go")
        st, hi, lo = stage[:, v % 2, 0:n], whi[:, v % 4, 0:n], wlo[:, v % 4, 0:n]
        pool.tensor_scalar(st, st, WS, 1.0, ALU.mult, ALU.mult).then_inc(slab_scaled, 1)
        pool.wait_ge(slab_scaled, s + (1 - NSTART))
        standing(pool, s, "splits_let_go")
        pool.tensor_scalar(hi, st, 1.0, 1.0, ALU.mult, ALU.mult).then_inc(slab_hi, 1)
        pool.wait_ge(slab_hi, s + (1 - NSTART))
        pool.tensor_tensor(lo, st, hi, ALU.subtract).then_inc(slab_split, 1)

    def product(pe, out, w_hi, w_lo, a_hi, a_lo, start, stop):
        pe.matmul(out, w_hi, a_hi, start=start, stop=False)
        pe.matmul(out, w_hi, a_lo, start=False, stop=False)
        return pe.matmul(out, w_lo, a_hi, start=False, stop=stop)

    block_cm = nc.Block()
    block = block_cm.__enter__()

    wada = I["w_ada"][0]
    GROUP_AFTER = [3, 6]
    EARLY = len(GROUP_AFTER)

    def ada_src(q):
        return wada[:, bass.ds(q * P, P)].rearrange("(k p) n -> p k n", p=P)

    x_prompt, x_sample = I["x_prompt"][0], I["x_sample"].rearrange("b o d -> (b o) d")

    @block.sync
    def _(sp):
        sp.dma_start(crow[0:1, 0, :], I["c_prompt"]).then_inc(S("c_in"), 16)
        sp.dma_start(crow[1:NSEQ, 0, :], I["c_sample"]).then_inc(S("c_in"), 16)
        sp.dma_start(cst[:], I["consts"]).then_inc(S("const_in"), 16)
        sp.dma_start(mrow[:].rearrange("p a n -> p (a n)"), I["masks"]).then_inc(S("mask_in"), 16)
        sp.dma_start(prow[0:72, 0, :], I["b_ada"][0].rearrange("(q p) -> q p", p=P)).then_inc(S("par_in"), 16)
        sp.dma_start(prow[72:120, 0, :], I["g_norm"][0].rearrange("n (c p) -> (n c) p", p=P)).then_inc(S("par_in"), 16)
        sp.dma_start(prow[0:12, 1, :], I["conv_w"][0].rearrange("j (c p) -> (j c) p", p=P)).then_inc(S("par_in"), 16)
        sp.dma_start(prow[12:76, 1, :], I["phi_pe"][0].rearrange("v (m l) d -> (v m) (l d)", l=2)).then_inc(S("par_in"), 16)
        sp.dma_start(prow[76:78, 1, :], I["phi_b1"][0]).then_inc(S("par_in"), 16)
        for g in range(NSTART // 4):
            if g == EARLY:
                sp.wait_ge(S("rows_dma2"), 32)
            sp.dma_start(first[:, g], wada[:, g * 4 * P:(g + 1) * 4 * P].rearrange("(k p) n -> p k n", p=P))\
              .then_inc(S(f"first_in{g}"), 16)
            if g == 1:
                for q in range(2):
                    sp.sem_inc(stage_full[q], 16 * (NSTART // 2))

    modrow = y[0:NSEQ, :, TJ:TJ + NSTART * P // KD]

    def first_row(act, g):
        act.wait_ge(S("first_mm"), g + 1)
        act.activation(modrow[:, 2 * g:2 * g + 2, :],
                       bank[6 + g % 2][0:NSEQ, :].rearrange("p (c n) -> p c n", c=2), ACT.Copy)\
           .then_inc(S("first_row"), 1)

    @block.scalar
    def _(act):
        for t in range(4):
            act.dma_start(xrow[:, t, :], x_prompt[t * P:(t + 1) * P, :]).then_inc(S(f"rows_dma{t}"), 16)
        act.wait_ge(S("c_in"), 32)
        act.activation(crow[:, 1, :], crow[:, 0, :], ACT.Silu).then_inc(S("c_silu"), 1)
        for t in range(TT + 1):
            n = P if t < TT else NDEC
            act.wait_ge(S("rows_mm"), 2 * t + 2)
            act.activation(x[:, 4:8, t * P:t * P + n],
                           bank[2 * (t % 2) + 1].rearrange("p (c n) -> p c n", c=4)[:, :, 0:n], ACT.Copy)\
               .then_inc(S("rows_b"), 1)
            if t + 4 <= TT:
                act.wait_ge(S("rows_mm"), 2 * t + 2)
                if t + 4 < TT:
                    act.dma_start(xrow[:, t % 4, :], x_prompt[(t + 4) * P:(t + 5) * P, :]).then_inc(S(f"rows_dma{t % 4}"), 16)
                else:
                    act.dma_start(xrow[0:NDEC, t % 4, :], x_sample).then_inc(S(f"rows_dma{t % 4}"), 16)
            if t - 1 in GROUP_AFTER:
                first_row(act, GROUP_AFTER.index(t - 1))
    count("mod_done", NSTART)

    def first_mods_act(act):
        for g in range(EARLY, NSTART // 4):
            first_row(act, g)
        act.wait_ge(S("first_mods"), 2)
        act.sem_inc(S("mod_done"), NSTART)

    def first_mods_dve(dve):
        dve.wait_ge(S("first_mm"), NSTART // 4 + 1)
        dve.tensor_tensor(mod0[:], bank[0][:, 0:16 * NSTART].rearrange("p (q n) -> p q n", n=16)[:, :, 0:NSEQ],
                          par1[:, 0:NSTART].unsqueeze(2).to_broadcast([P, NSTART, NSEQ]), ALU.add)\
           .then_inc(S("first_mods"), 1)
        dve.wait_ge(S("first_mods"), 1)
        dve.tensor_scalar(par1[:, 0:NMOD], par1[:, 0:NMOD], 0.5, None, ALU.mult).then_inc(S("first_mods"), 1)
        dve.wait_ge(S("first_mods"), 2)

    def first_group(pe, g):
        if g == 0:
            pe.wait_ge(S("cs_lo"), 1)
            pe.sem_inc(slab_used, NSTART)
        pe.wait_ge(S(f"first_in{g}"), 16)
        if g >= 2:
            pe.wait_ge(S("first_row"), g - 1)
        for k in range(KD):
            last = pe.matmul(bank[6 + g % 2][0:NSEQ, :], cs32[:, k, :], first[:, g, k, :], start=k == 0,
                             stop=k == KD - 1)
        last.then_inc(S("first_mm"), 1)

    def first_mods_pe(pe):
        for g in range(EARLY, NSTART // 4):
            first_group(pe, g)
        pe.wait_ge(S("first_row"), NSTART // 4)
        for q in range(NSTART):
            last = pe.transpose(bank[0][:, 16 * q:16 * q + NSEQ], modrow[:, q // 2, (q % 2) * P:(q % 2 + 1) * P],
                                const("ident", NSEQ)[:, 0:NSEQ])
        last.then_inc(S("first_mm"), 1)

    @block.tensor
    def _(pe):
        pe.wait_ge(S("const_in"), 16)
        pe.wait_ge(S("par_in"), 80)
        pe.transpose(bank[4][:, 0:120], prow[0:120, 0, :], const("ident", 120)[:, 0:120]).then_inc(S("parT"), 1)
        pe.transpose(bank[4][:, 128:128 + 78], prow[0:78, 1, :], const("ident", 78)[:, 0:78]).then_inc(S("parT"), 1)
        pe.wait_ge(S("c_silu"), 1)
        for k in range(KD):
            last = pe.transpose(bank[5][:, 16 * k:16 * k + NSEQ], crow[:, 1, k * P:(k + 1) * P],
                                const("ident", NSEQ)[:, 0:NSEQ])
        last.then_inc(S("cT"), 1)
        for t in range(TT + 1):
            n = P if t < TT else NDEC
            pe.wait_ge(S(f"rows_dma{t % 4}"), 16 * (t // 4 + 1))
            if t >= 2:
                pe.wait_ge(S("rows_a"), t - 1)
                pe.wait_ge(S("rows_b"), t - 1)
            for half in range(2):
                b = bank[2 * (t % 2) + half]
                for c in range(4):
                    k = 4 * half + c
                    last = pe.transpose(b[:, c * P:c * P + n], xrow[0:n, t % 4, k * P:(k + 1) * P],
                                        const("ident", n)[:, 0:n])
                last.then_inc(S("rows_mm"), 1)
            if t in GROUP_AFTER:
                first_group(pe, GROUP_AFTER.index(t))

    @block.vector
    def _(dve):
        dve.wait_ge(S("const_in"), 16)
        dve.tensor_copy(identb[:], const("ident")).then_inc(S("par"), 1)
        dve.wait_ge(S("mask_in"), 16)
        dve.tensor_copy(maskb[:], mrow[:]).then_inc(S("par"), 1)
        dve.wait_ge(S("parT"), 2)
        dve.tensor_copy(par1[:], bank[4][:, 0:120]).then_inc(S("par"), 1)
        dve.tensor_copy(par2[:], bank[4][:, 128:128 + 78]).then_inc(S("par"), 1)
        dve.wait_ge(S("cT"), 1)
        ct = bank[5][:, 0:16 * KD].rearrange("p (k n) -> p k n", n=16)[:, :, 0:NSEQ]
        dve.tensor_copy(cs32[:], ct).then_inc(S("cs_hi"), 1)
        dve.tensor_copy(csh, ct).then_inc(S("cs_hi"), 1)
        dve.wait_ge(S("cs_hi"), 2)
        dve.tensor_tensor(csl, ct, csh, ALU.subtract).then_inc(S("cs_lo"), 1)
        for t in range(TT + 1):
            n = P if t < TT else NDEC
            dve.wait_ge(S("rows_mm"), 2 * t + 1)
            dve.tensor_copy(x[:, 0:4, t * P:t * P + n],
                            bank[2 * (t % 2)].rearrange("p (c n) -> p c n", c=4)[:, :, 0:n])\
               .then_inc(S("rows_a"), 1)

    G = par1[:, 72:120].rearrange("p (n c) -> p n c", n=6)
    DC = SEQ - 2 * TJ

    def prompt_cols(j):
        a, b = third(j)
        return a, min(b, SEQ)

    def per_chunk(v):
        return v.unsqueeze(2).to_broadcast([P, KD, NSEQ])

    def sum_shares(dve, q0, q1):
        dve.tensor_tensor(mod(q0, q1 - q0), mod(q0, q1 - q0), mods[:, q0 - NSTART:q1 - NSTART, 1, :], ALU.add).then_inc(S("vec"), 1)
        dve.wait_ge(S("vec"), count("vec"))

    def gate_values(post):
        @block.vector
        def _(dve):
            dve.wait_ge(S("par"), 4)
            dve.wait_ge(S("mod_done"), (3 * post + 3) * KD)
            sum_shares(dve, (3 * post + 2) * KD, (3 * post + 3) * KD)
            dve.scalar_tensor_tensor(out=gateC[:, post], in0=mod((3 * post + 2) * KD),
                                     scalar=(0.5 if post != 1 else 1.0) * IWS, in1=per_chunk(G[:, 2 * post + 1, :]),
                                     op0=ALU.mult, op1=ALU.mult).then_inc(S("vec"), 1)
        return count("vec")

    def y_chunk(act, post, vec, c, j, src):
        a, b = third(j)
        pb = min(b, SEQ)
        if post is not None:
            act.wait_ge(S("vec"), vec)
        out = y[:, bass.ds(c, 1), a:pb]
        op = act.activation(out, src[:, 0:pb - a].unsqueeze(1), ACT.Copy, scale=gateC[:, post, bass.ds(c, 1), 0:1])
        if pb < b:
            op.then_inc(S("y_part"), 1)
            op = act.activation(y[:, bass.ds(c, 1), pb:b], src[:, pb - a:b - a].unsqueeze(1), ACT.Copy)
        op.then_inc(S("y"), 1)

    def y_mean(pe, j, acc_value):
        pe.wait_ge(S("acc_done"), acc_value)
        if j == 0:
            pe.wait_ge(S("mod_done"), at("mod_done"))
        if j == 2:
            pe.wait_ge(S("rms_sqrt"), at("rms_sqrt") + 1)
        pe.matmul(bank[6 + j % 2][:, 0:TJ], const("mean"), acc[:, j, :], start=True, stop=True)\
          .then_inc(S("y_mean"), 1)

    def boundary(post, pre, x_ready=None, tail=None):
        if pre:
            @block.vector
            def _(dve):
                dve.wait_ge(S("mod_done"), (3 * pre + 2) * KD)
                sum_shares(dve, 3 * pre * KD, (3 * pre + 2) * KD)

        base = {n: at(n) for n in ("y_mean", "rms_sqrt", "rms", "y_scaled", "x_new", "x_new_b", "xsq", "x_mean",
                                   "dec_u", "tmp_w", "a_full", "a_hi", "a_lo", "dec_n", "vec", "ysq")}
        ny = NJ if post is not None else 0

        def b(name, n=0):
            return base[name] + n

        CB = 5

        def squares_of(j):
            return sqx[:, j - 1] if j > 0 else y[:, :, 0:TJ]

        def x_mean(pe, j):
            for c in range(KD):
                if c % 4 == 0:
                    pe.wait_ge(S("xsq"), b("xsq", 2 * j + c // 4 + 1))
                last = pe.matmul(bank[3 + j][:, 0:TJ], const("mean"), squares_of(j)[:, c, :],
                                 start=(c == 0), stop=(c == KD - 1))
            last.then_inc(S("x_mean"), 1)

        @block.tensor
        def _(pe):
            if pre is not None:
                if post is None:
                    pe.wait_ge(S("rows_a"), TT + 1)
                    pe.wait_ge(S("rows_b"), TT + 1)
                else:
                    pe.wait_ge(S("ysq"), b("ysq") - 1)
                x_mean(pe, 0)
                if post is not None:
                    y_mean(pe, 2, tail["acc"])
                    pe.wait_ge(S("ysq"), b("ysq"))
                else:
                    first_mods_pe(pe)
                x_mean(pe, 1)
            elif post is not None:
                y_mean(pe, 2, tail["acc"])

        @block.scalar
        def _(act):
            def sqrt(j, source, sem_name, value):
                act.wait_ge(S(sem_name), value)
                act.activation(rs[:, j, :], source[:, 0:TJ], ACT.Sqrt, bias=const("eps")).then_inc(S("rms_sqrt"), 1)

            def squares(j, between=None):
                lo_, hi_ = third(j)
                if post is None:
                    x_ready(act, j)
                else:
                    act.wait_ge(S("x_new"), b("x_new", j + 1))
                    act.wait_ge(S("x_new_b"), b("x_new_b", j + 1))
                for half in range(2):
                    chunks_ = slice(4 * half, 4 * half + 4)
                    act.activation(squares_of(j)[:, chunks_, :], x[:, chunks_, lo_:hi_],
                                   ACT.Square).then_inc(S("xsq"), 1)
                if between:
                    between(act)

            def root_x(j):
                sqrt(j, bank[3 + j], "x_mean", b("x_mean", j + 1))

            def affine(j):
                lo_, hi_ = prompt_cols(j)
                w = hi_ - lo_
                act.wait_ge(S("x_mean"), b("x_mean", 1))
                if post is not None:
                    act.wait_ge(S("x_new"), b("x_new", 2 if j == 0 else 3))
                    act.wait_ge(S("x_new_b"), b("x_new_b", 2 if j == 0 else 3))
                for q in range(KD // 2):
                    m = j * KD // 2 + q
                    act.wait_ge(S("tmp_w"), b("tmp_w", m + 1))
                    for c in (2 * q, 2 * q + 1):
                        t_ = pair[:, m % 2, c % 2, 0:w]
                        act.activation(t_, t_, ACT.Identity, bias=mod(3 * pre * KD)[:, c, 0:1],
                                       scale=scaleA[:, pre, c, 0:1]).then_inc(S("a_full"), 1)
                    act.wait_ge(S("a_full"), b("a_full", 2 * m + 2))
                    act.activation(ahi[:, 2 * q:2 * q + 2, lo_:hi_], pair[:, m % 2, :, 0:w], ACT.Copy)\
                       .then_inc(S("a_hi"), 1)

            if post is not None:
                for j in range(2):
                    sqrt(j, bank[6 + j % 2], "y_mean", b("y_mean", j + 1))
            if pre is not None:
                if post is not None:
                    act.wait_ge(S("vec"), b("vec", 2))
                    squares(0, tail["act"])
                    root_x(0)
                    sqrt(2, bank[6], "y_mean", b("y_mean", 3))
                    squares(1)
                    affine(0)
                    root_x(1)
                    squares(2)
                    affine(1)
                    root_x(2)
                    affine(2)
                else:
                    squares(0)
                    squares(1)
                    root_x(0)
                    squares(2)
                    first_mods_act(act)
                    act.wait_ge(S("vec"), b("vec", 2))
                    affine(0)
                    root_x(1)
                    affine(1)
                    root_x(2)
                    affine(2)
            elif post is not None:
                tail["act"](act)
                sqrt(2, bank[6], "y_mean", b("y_mean", 3))

        if post is not None:
            @block.gpsimd
            def _(pool):
                for j in range(NJ):
                    lo_, hi_ = third(j)
                    if pre is not None and j != 1:
                        for v in (j, j + 1):
                            split_slab(pool, at("slab"), 0, v, KD * P)
                    pool.wait_ge(S("y_scaled"), b("y_scaled", j + 1))
                    xc = x[:, CB:KD, lo_:hi_]
                    pool.tensor_tensor(xc, xc, y[:, CB:KD, lo_:hi_], ALU.add).then_inc(S("x_new_b"), 1)

        @block.vector
        def _(dve):
            def inverse(j, k):
                dve.wait_ge(S("rms_sqrt"), b("rms_sqrt", k + 1))
                dve.reciprocal(rs[:, j, :], rs[:, j, :]).then_inc(S("rms"), 1)
                dve.wait_ge(S("rms"), b("rms", k + 1))

            def across(j, w=TJ):
                return rs[:, j, 0:w].unsqueeze(1).to_broadcast([P, KD, w])

            def add(j):
                lo_, hi_ = third(j)
                yt = y[:, :, lo_:hi_]
                if j == 2:
                    dve.wait_ge(S("y"), at("y"))
                    yd = y[:, :, SEQ:T]
                    dve.tensor_tensor(yd, yd, gateC[:, post, :, 1:NSEQ], ALU.mult).then_inc(S("dec_u"), 1)
                    dve.wait_ge(S("dec_u"), b("dec_u", 1))
                dve.wait_ge(S("y"), at("y") - 2 + j)
                dve.tensor_tensor(yt, yt, across(j), ALU.mult).then_inc(S("y_scaled"), 1)
                dve.wait_ge(S("y_scaled"), b("y_scaled", j + 1))
                xc = x[:, 0:CB, lo_:hi_]
                dve.tensor_tensor(xc, xc, y[:, 0:CB, lo_:hi_], ALU.add).then_inc(S("x_new"), 1)

            def apply(j):
                lo_, hi_ = prompt_cols(j)
                w = hi_ - lo_

                def low(q):
                    m = j * KD // 2 + q
                    dve.wait_ge(S("a_hi"), b("a_hi", m + 1))
                    dve.tensor_tensor(alo[:, 2 * q:2 * q + 2, lo_:hi_], pair[:, m % 2, :, 0:w],
                                      ahi[:, 2 * q:2 * q + 2, lo_:hi_], ALU.subtract).then_inc(S("a_lo"), 1)
                if post is not None:
                    dve.wait_ge(S("x_new"), b("x_new", j + 1))
                    dve.wait_ge(S("x_new_b"), b("x_new_b", j + 1))
                for q in range(KD // 2):
                    m = j * KD // 2 + q
                    if q >= 2:
                        low(q - 2)
                        dve.wait_ge(S("a_lo"), b("a_lo", m - 1))
                    dve.tensor_tensor(pair[:, m % 2, :, 0:w], x[:, 2 * q:2 * q + 2, lo_:hi_],
                                      rs[:, j, 0:w].unsqueeze(1).to_broadcast([P, 2, w]), ALU.mult)\
                       .then_inc(S("tmp_w"), 1)
                low(KD // 2 - 2)
                low(KD // 2 - 1)
                dve.wait_ge(S("a_lo"), b("a_lo", (j + 1) * KD // 2))
                if j == 2:
                    rsd = rs[:, 2, DC:TJ].unsqueeze(1).to_broadcast([P, KD, NDEC])
                    dve.tensor_tensor(decd[:, 0], x[:, :, SEQ:T], rsd, ALU.mult).then_inc(S("dec_n"), 1)
                    dve.wait_ge(S("dec_n"), b("dec_n", 1))
                    dve.tensor_tensor(decd[:, 1], decd[:, 0], scaleA[:, pre, :, 1:NSEQ], ALU.mult)\
                       .then_inc(S("dec_n"), 1)
                    dve.wait_ge(S("dec_n"), b("dec_n", 2))
                    dve.tensor_tensor(decd[:, 0], decd[:, 1], mod(3 * pre * KD)[:, :, 1:NSEQ],
                                      ALU.add).then_inc(S("dec_n"), 1)
                    dve.wait_ge(S("dec_n"), b("dec_n", 3))
                    dve.tensor_copy(ahi[:, :, SEQ:T], decd[:, 0]).then_inc(S("dec_n"), 1)
                    dve.wait_ge(S("dec_n"), b("dec_n", 4))
                    dve.tensor_tensor(alo[:, :, SEQ:T], decd[:, 0], ahi[:, :, SEQ:T], ALU.subtract)\
                       .then_inc(S("a_lo"), 1)

            if post is None:
                inverse(0, 0)
                first_mods_dve(dve)
            if pre is not None:
                dve.wait_ge(S("par"), 4)
                dve.wait_ge(S("mod_done"), (3 * pre + 2) * KD)
                dve.tensor_scalar(scaleA[:, pre], mod((3 * pre + 1) * KD), 1.0, None,
                                  ALU.add).then_inc(S("vec"), 1)
                dve.wait_ge(S("vec"), b("vec", 1))
                dve.tensor_tensor(scaleA[:, pre], scaleA[:, pre], per_chunk(G[:, 2 * pre, :]), ALU.mult)\
                   .then_inc(S("vec"), 1)
                dve.wait_ge(S("vec"), b("vec", 2))
            if post is not None:
                inverse(0, 0)
                add(0)
                inverse(1, 1)
                add(1)
                tail["dve"](dve)
                if pre is None:
                    inverse(2, 2)
                    add(2)
            if pre is not None:
                if post is None:
                    for j in range(NJ):
                        if j > 0:
                            inverse(j, j)
                        apply(j)
                else:
                    inverse(0, 2)
                    apply(0)
                    inverse(2, 3)
                    add(2)
                    inverse(1, 4)
                    apply(1)
                    inverse(2, 5)
                    apply(2)
        if post is not None:
            count("y_mean", NJ)
            for name in ("y_scaled", "x_new", "x_new_b"):
                count(name, NJ)
            count("dec_u", 1)
        if pre is not None:
            count("xsq", 2 * NJ)
            count("x_mean", NJ)
            count("a_full", NJ * KD)
            for name in ("tmp_w", "a_hi"):
                count(name, NJ * KD // 2)
            count("a_lo", NJ * KD // 2 + 1)
            count("dec_n", 4)
            count("vec", 2)
        for name in ("rms_sqrt", "rms"):
            count(name, ny + (NJ if pre is not None else 0))
        return [b("a_lo", KD // 2), b("a_lo", KD), b("a_lo", 3 * KD // 2 + 1)], lambda pe: x_mean(pe, 2)

    def ada_product(pe, slot, q, b, back):
        pe.wait_ge(S("mod_done"), q - (back - 1))
        w1, w2 = slab_parts(slot, KD)
        o = bank[b][:, 0:2 * NSEQ]
        for k in range(KD):
            both = cshl[:, k].rearrange("p v n -> p (v n)")
            pe.matmul(o, w1[:, k, :], both, start=k == 0, stop=False)
            last = pe.matmul(o, w2[:, k, :], both, start=False, stop=k == KD - 1)
        last.then_inc(slab_used, 1)

    def ada_value(act, s, q, b):
        act.wait_ge(slab_used, s + 1)
        act.activation(mods[:, bass.ds(q + -NSTART, 1)].rearrange("p q v n -> p q (v n)"),
                       bank[b][:, 0:2 * NSEQ].unsqueeze(1), ACT.Identity,
                       bias=par1[:, bass.ds(q, 1)], scale=IWS).then_inc(S("mod_done"), 1)

    def lin(i, k, c):
        return i * k + c if isinstance(i, int) else i[0] * k + (c + i[1] * k)

    def looped(eng, body, n, first=0, last=0):
        for i in range(first):
            body(i)
        with eng.Fori(0, n - first - last) as i:
            body((i, first))
        for i in range(n - last, n):
            body(i)

    def ffn(f, post, a_ready, with_ada):
        wgu, wdn = I["w_ffn_gu"][0, f], I["w_ffn_down"][0, f]
        a_ready, late = a_ready
        late_after = 0 if with_ada else 3
        s_first = at("slab")
        per = 8 if with_ada else 4
        NIT = KF // 2
        s0 = s_first - (per - 4)
        s1 = s0 + NIT * per
        q0 = NSTART - 4
        silu0, h0, hh0, hl0, g0, acc0 = (at(n) for n in ("silu", "h", "h_hi", "h_lo", "group", "acc_done"))
        ysq0 = at("ysq")

        def gu_src(k, up):
            return wgu[:, bass.ds(k * P + up * DFF, P)].rearrange("(k p) n -> p k n", p=P)

        def dn_src(c, half):
            return wdn[half * 11 * P:(half + 1) * 11 * P, bass.ds(c * P, P)].rearrange("(k p) n -> p k n", p=P)

        def plan(i):
            out, ada = [], 0
            for u in range(2):
                for kind in ("gate", "up"):
                    out.append((kind, u, None))
                    if with_ada and i != 0:
                        out.append(("ada", u, ada))
                        ada += 1
            return out

        def place_of(i, u, j):
            return 2 * j + u if i == 0 else 3 * u + j

        roots = at("rms_sqrt")

        def slab(i, v):
            return s_first + v if i == 0 else lin(i, per, s0 + v)

        DOWN = [(u, half) for u in range(2) for half in range(2)]

        @block.sync
        def _(sp):
            def pair_of_chunks(i):
                for v, (kind, u, ada) in enumerate(plan(i)):
                    src = ada_src(lin(i, 4, q0 + ada)) if kind == "ada" else gu_src(lin(i, 2, u), kind == "up")
                    load_slab(sp, slab(i, v), v % 4, src, KD)

            looped(sp, pair_of_chunks, NIT, first=1)
            with sp.Fori(0, KD // 2) as i:
                for v, (u, half) in enumerate(DOWN):
                    load_slab(sp, i * 4 + (s1 + v), v, dn_src(i * 2 + u, half), 11)

        @block.gpsimd
        def _(pool):
            if s_first == NSTART:
                pool.sem_inc(slab_split, NSTART)
                for v in range(4):
                    split_slab(pool, s_first, 0, v, KD * P)
            with pool.Fori(0, NIT - 1) as i:
                for v in range(per):
                    split_slab(pool, s_first + 4, i * per, v, KD * P)
            with pool.Fori(0, KD // 2) as i:
                for v in range(4):
                    split_slab(pool, s1, i * 4, v, SLAB)

        @block.tensor
        def _(pe):
            def group(i, v, kind, u, j):
                a, b = third(j)
                w1, w2 = slab_parts(v % 4, KD)
                if v > 0 or j == 2 or i != 0:
                    pe.wait_ge(S("a_lo"), a_ready[j])
                m = place_of(i, u, j)
                if i == 0 and kind == "up":
                    pe.wait_ge(S("rms_sqrt"), roots - (m < 2))
                if i != 0 or m >= 3:
                    pe.wait_ge(S("silu" if kind == "gate" else "h"),
                               lin(i, 6, m + 1 + (silu0 if kind == "gate" else h0)))
                o = bank[m % 3 + 3 * (kind == "up")][:, 0:TJ]
                for k in range(KD):
                    if i == 0 and v == 0 and j < 2:
                        pe.wait_ge(S("a_lo"), a_ready[j] - KD // 2 + k // 2 + 1)
                    last = product(pe, o, w1[:, k, :], w2[:, k, :], ahi[:, k, a:b], alo[:, k, a:b],
                                   k == 0, k == KD - 1)
                last.then_inc(S("group") if j < 2 else slab_used, 1)

            def pair_of_chunks(i):
                if i == 0:
                    for j in range(NJ):
                        for v, (kind, u, ada) in enumerate(plan(0)):
                            pe.wait_ge(slab_split, s_first + v + 1)
                            group(0, v, kind, u, j)
                            if j == 0 and v == late_after:
                                late(pe)
                    return
                for v, (kind, u, ada) in enumerate(plan(i)):
                    pe.wait_ge(slab_split, lin(i, per, s0 + v + 1))
                    if kind == "ada":
                        ada_product(pe, v % 4, lin(i, 4, q0 + ada), 6 + ada % 2, 2)
                    else:
                        for j in range(NJ):
                            group(i, v, kind, u, j)

            looped(pe, pair_of_chunks, NIT, first=1)

            def output_chunks(i):
                for u in range(2):
                    halves = [slab_parts(2 * u, 11), slab_parts(2 * u + 1, 11)]
                    pe.wait_ge(slab_split, lin(i, 4, s1 + 2 * u + 2))
                    pe.wait_ge(S("silu"), silu0 + 3 + NJ * KF)
                    pe.wait_ge(S("h"), h0 + 3 + NJ * KF)
                    tail = i == KD // 2 - 1 and u == 1
                    for j in range(NJ):
                        a, b = third(j)
                        pe.wait_ge(S("ysq"), lin(i, 6, ysq0 + 3 * u + j + 1))
                        pe.wait_ge(S("h_lo"), hl0 + 3 + NJ * (KF - 1) + j + 1)
                        o = bank[3 * u + j][:, 0:TJ]
                        for k in range(KF):
                            w1, w2 = halves[k // 11]
                            last = product(pe, o, w1[:, k % 11, :], w2[:, k % 11, :], hhi[:, k, a:b],
                                           hlo[:, k, a:b], k == 0, k == KF - 1)
                            if j == NJ - 1 and k == 10:
                                last.then_inc(slab_used, 1)
                                if tail:
                                    y_mean(pe, 1, acc0 + NJ * KD + 2)
                        last.then_inc(S("group") if j < 2 else slab_used, 1)
                        if tail and j == 1:
                            y_mean(pe, 0, acc0 + NJ * KD + 1)

            looped(pe, output_chunks, KD // 2, last=1)

        vec = None

        @block.scalar
        def _(act):
            act.sem_inc(S("silu"), 3)

            def take(i, u, kind, j):
                a, b = third(j)
                m = place_of(i, u, j)
                if kind == "gate":
                    act.wait_ge(S("h"), lin(i, 6, h0 + m + 1))
                    act.activation(sg[:, m % 3, :], bank[m % 3][:, 0:TJ], ACT.Silu, scale=IWS).then_inc(S("silu"), 1)
                else:
                    act.wait_ge(S("h"), lin(i, 6, h0 + 3 + m + 1))
                    act.activation(hhi[:, bass.ds(lin(i, 2, u), 1), a:b], h32[:, m % 3, :].unsqueeze(1), ACT.Copy)\
                       .then_inc(S("h_hi"), 1)

            def pair_of_chunks(i):
                if i == 0:
                    for j in range(NJ):
                        for v, (kind, u, ada) in enumerate(plan(0)):
                            if kind == "gate":
                                act.wait_ge(S("group") if j < 2 else slab_used, g0 + 4 * j + v + 1 if j < 2
                                            else s_first + v + 1)
                            take(0, u, kind, j)
                    return
                for v, (kind, u, ada) in enumerate(plan(i)):
                    if kind == "ada":
                        ada_value(act, lin(i, per, s0 + v), lin(i, 4, q0 + ada), 6 + ada % 2)
                        continue
                    for j in range(NJ):
                        if kind == "gate":
                            if j < 2:
                                act.wait_ge(S("group"), lin(i, 8, g0 + 4 * u + j + 1))
                            else:
                                act.wait_ge(slab_used, lin(i, per, s0 + v + 1))
                        take(i, u, kind, j)

            looped(act, pair_of_chunks, NIT, first=1)
            act.sem_inc(S("ysq"), 6)

        def take_y(act, i, u, j):
            if j < 2:
                act.wait_ge(S("group"), lin(i, 4, g0 + 4 * KF + 2 * u + j + 1))
            else:
                act.wait_ge(slab_used, lin(i, 4, s1 + 2 * u + 2))
            y_chunk(act, post, vec, lin(i, 2, u), j, bank[3 * u + j])
            act.wait_ge(S("acc_done"), lin(i, 6, acc0 + 3 * u + j + 1))
            act.activation(sq[:, j, :], bank[3 * u + j][:, 0:TJ], ACT.Square, scale=IWS).then_inc(S("ysq"), 1)

        def add_square(dve, i, u, j):
            m = 3 * u + j
            dve.wait_ge(S("ysq"), lin(i, 6, ysq0 + 6 + m + 1))
            dve.wait_ge(S("acc_done"), lin(i, 6, acc0 + m + 1))
            dve.tensor_tensor(acc[:, j, :], acc[:, j, :], sq[:, j, :], ALU.add).then_inc(S("acc_done"), 1)

        @block.vector
        def _(dve):
            dve.sem_inc(S("h"), 3)
            dve.sem_inc(S("h_lo"), 3)

            def multiply(i, u, j):
                m = place_of(i, u, j)
                dve.wait_ge(S("silu"), lin(i, 6, silu0 + 3 + m + 1))
                dve.wait_ge(S("h_lo"), lin(i, 6, hl0 + m + 1))
                dve.scalar_tensor_tensor(out=h32[:, m % 3, :], in0=bank[3 + m % 3][:, 0:TJ], scalar=IWS,
                                         in1=sg[:, m % 3, :], op0=ALU.mult, op1=ALU.mult).then_inc(S("h"), 1)

            def low(i, u, j):
                a, b = third(j)
                m = place_of(i, u, j)
                dve.wait_ge(S("h_hi"), lin(i, 6, hh0 + m + 1))
                dve.tensor_tensor(hlo[:, bass.ds(lin(i, 2, u), 1), a:b], h32[:, m % 3, :].unsqueeze(1),
                                  hhi[:, bass.ds(lin(i, 2, u), 1), a:b], ALU.subtract).then_inc(S("h_lo"), 1)

            def pair_of_chunks(i):
                if i == 0:
                    for j in range(NJ):
                        for v, (kind, u, ada) in enumerate(plan(0)):
                            if kind == "up":
                                dve.wait_ge(S("group") if j < 2 else slab_used, g0 + 4 * j + v + 1 if j < 2
                                            else s_first + v + 1)
                                multiply(0, u, j)
                                low(0, u, j)
                    return
                for v, (kind, u, ada) in enumerate(plan(i)):
                    if kind != "up":
                        continue
                    for j in range(NJ):
                        if j < 2:
                            dve.wait_ge(S("group"), lin(i, 8, g0 + 4 * u + 2 + j + 1))
                        else:
                            dve.wait_ge(slab_used, lin(i, per, s0 + v + 1))
                        multiply(i, u, j)
                    for j in range(NJ):
                        low(i, u, j)

            looped(dve, pair_of_chunks, NIT, first=1)
            dve.wait_ge(S("h_lo"), hl0 + 3 + NJ * KF)
            for j in range(NJ):
                dve.memset(acc[:, j, :], 0.0).then_inc(S("acc_done"), 1)

        vec = gate_values(post)

        @block.scalar
        def _(act):
            def output_chunks(i):
                for u in range(2):
                    for j in range(NJ):
                        if not (i == KD // 2 - 1 and u == 1 and j == 2):
                            take_y(act, i, u, j)

            looped(act, output_chunks, KD // 2, last=1)

        @block.vector
        def _(dve):
            def output_chunks(i):
                for u in range(2):
                    for j in range(NJ):
                        if not (i == KD // 2 - 1 and u == 1 and j == 2):
                            add_square(dve, i, u, j)

            looped(dve, output_chunks, KD // 2, last=1)

        count("slab", NIT * per - (per - 4) + 2 * KD)
        count("silu", 3 + NJ * KF)
        count("h", 3 + NJ * KF)
        count("h_hi", NJ * KF)
        count("h_lo", 3 + NJ * KF)
        count("group", 4 * KF + 2 * KD)
        count("ysq", 6 + NJ * KD)
        count("y", NJ * KD)
        count("acc_done", NJ + NJ * KD)
        if with_ada:
            count("mod_done", 4 * (NIT - 1))
        return {"acc": at("acc_done"), "act": lambda act: take_y(act, KD // 2 - 1, 1, 2),
                "dve": lambda dve: add_square(dve, KD // 2 - 1, 1, 2)}

    def write_out():
        EARLY_ROWS = 2 * TJ // P

        def rows_first_half(eng, t):
            n = P if t < TT else NDEC
            eng.wait_ge(S("rows_mm"), 2 * (TT + 1) + 2 * t + 1)
            if t >= 4:
                eng.wait_ge(S(f"rows_dma{t % 4}"), 16 * (t // 4) + moved(t % 4))
            return xrow[0:n, t % 4, 0:512], bank[2 * (t % 2)][0:n, :]

        def moved(q):
            return 16 * (3 if q == 0 else 2)

        o_prompt, o_sample = O["y_prompt"][0], O["y_sample"].rearrange("b o d -> (b o) d")

        @block.tensor
        def _(pe):
            pe.wait_ge(S("ysq"), at("ysq"))
            for t in range(TT + 1):
                n = P if t < TT else NDEC
                j = (min(T, (t + 1) * P) - 1) // TJ
                pe.wait_ge(S("x_new"), at("x_new") - 2 + j)
                pe.wait_ge(S("x_new_b"), at("x_new_b") - 2 + j)
                if t >= 2:
                    pe.wait_ge(S("rows_a"), TT + 1 + t - 1)
                    pe.wait_ge(S("rows_b"), TT + 1 + t - 1)
                for half in range(2):
                    for c in range(4):
                        last = pe.transpose(bank[2 * (t % 2) + half][0:n, c * P:(c + 1) * P],
                                            x[:, 4 * half + c, t * P:t * P + n], const("ident"))
                    last.then_inc(S("rows_mm"), 1)

        @block.vector
        def _(dve):
            dve.wait_ge(S("rows_a"), TT + 1 + EARLY_ROWS)
            for t in range(EARLY_ROWS, TT + 1):
                rows, values = rows_first_half(dve, t)
                dve.tensor_copy(rows, values).then_inc(S("rows_a"), 1)

        @block.scalar
        def _(act):
            for t in range(TT + 1):
                n = P if t < TT else NDEC
                if t < EARLY_ROWS:
                    rows, values = rows_first_half(act, t)
                    act.activation(rows, values, ACT.Copy).then_inc(S("rows_a"), 1)
                act.wait_ge(S("rows_mm"), 2 * (TT + 1) + 2 * t + 2)
                if t >= 4:
                    act.wait_ge(S(f"rows_dma{t % 4}"), 16 * (t // 4) + moved(t % 4))
                act.activation(xrow[0:n, t % 4, 512:D], bank[2 * (t % 2) + 1][0:n, :], ACT.Copy).then_inc(S("rows_b"), 1)

        @block.sync
        def _(sp):
            for t in range(TT + 1):
                sp.wait_ge(S("rows_a"), TT + 1 + t + 1)
                sp.wait_ge(S("rows_b"), TT + 1 + t + 1)
                if t < TT:
                    sp.dma_start(o_prompt[t * P:(t + 1) * P, :], xrow[:, t % 4, :]).then_inc(S(f"rows_dma{t % 4}"), 16)
                else:
                    sp.dma_start(o_sample, xrow[0:NDEC, t % 4, :]).then_inc(S(f"rows_dma{t % 4}"), 16)
            for q in range(4):
                sp.wait_ge(S(f"rows_dma{q}"), 2 * moved(q))

    def mixer(a_ready):
        w_in = I["w_in"][0]
        a_ready, late = a_ready
        sa = at("slab")
        sphi = sa + 11
        sw2 = sphi + 8
        sconv = sw2 + 1
        LATE = NMOD - NSTART - 4 * (KF // 2 - 1)
        smerge = sconv + 3 * KC + LATE
        sout = smerge + 4 * KD
        assert sa % 4 == 0 and smerge % 4 == 0 and (sout + KD) % 4 == 0
        count("slab", sout + KD - sa)
        R = NDEC * NH

        cursor[0] = free_at
        oahi = place("oahi", [P, KC, T], F16)
        oalo = place("oalo", [P, KC, T], F16)
        mix_at = cursor[0]
        gs = place("gs", [P, TT + 1, GC], F32)
        qst_at = cursor[0]
        qst = place("qst", [P, NH, SEQ], F16)
        kst = place("kst", [P, 2, NG, 2, SEQ], F16)
        vst_at = cursor[0]
        vst = place("vst", [P, 2, TT + 1, P], F32)
        zd = place("zd", [NDEC, 6, P], F32)
        qd = place("qd", [P, NDEC, NH], F32)
        knt = place("knt", [P, 2, NDEC], F32)
        vbd = place("vbd", [P, NH, HD], F32)
        kcst = place("kcst", [P, NG, 2, NB], F16)
        kcd = place("kcd", [P, NDEC * NB], F32)
        vcd = place("vcd", [P, P], F32)
        gdec = place("gdec", [R, 3], F32)
        ptf = place("ptf", [P, 1], F32)
        pti = place("pti", [P, 1], I32)
        rowid = place("rowid", [P, 16], I32)
        mixwork = cursor[0]
        zs = place("zs", [P, 2, TT + 1, P], F32)
        rot = place("rot", [P, 4, (TT + 1) * 16], F32)

        def split_const(pool, s, n):
            split_slab(pool, s - s % 4, 0, s % 4, n)

        def load_const(sp, s, src, kk, w=P):
            load_slab(sp, s, s % 4, src, kk, w)

        def cols(c0, w):
            return w_in[:, c0:c0 + w].rearrange("(k p) n -> p k n", p=P)

        NL = 4

        KINDS = ["q", "q", "q", "q", "cmp_k", "cmp_v", "slc_k", "slc_v", "win_k", "win_v", "gate"]
        DEST = {0: 0, 1: 1, 2: 0, 3: 1, 4: 0, 5: 1, 6: 0, 8: 1}
        width = [GC if kind == "gate" else P for kind in KINDS]
        outs = {4: ("cmp", 0), 5: ("cmp", 1), 6: ("slc", 0), 7: ("slc", 1), 8: ("win", 0), 9: ("win", 1)}

        @block.sync
        def _(sp):
            for n in range(11):
                load_const(sp, sa + n, cols(n * P, width[n]), KD, width[n])
                if n == 4:
                    sp.wait_ge(slab_used, sa + 1)
                    for half in range(2):
                        sp.dma_start(pti[half:P:2, :], I["page_table"].rearrange("b (n o) -> (b n) o", o=1))\
                          .then_inc(S("pages_in"), 16)
            sp.dma_start(O["win_kv_sample"][0][:, 0:WIN - 1], I["state_win_kv"][0][:, 1:WIN]).then_inc(S("shifts"), 16)

        @block.gpsimd
        def _(pool):
            for n in range(4, 11):
                split_const(pool, sa + n, KD * width[n])

        @block.vector
        def _(dve):
            dve.memset(zs[:, :, TT, :], 0.0).then_inc(S("z_clear"), 1)
            dve.memset(qd[:], 0.0).then_inc(S("z_clear"), 1)

        @block.tensor
        def _(pe):
            pe.wait_ge(S("ysq"), at("ysq"))

        @block.vector
        def _(dve):
            dve.wait_ge(S("pages_in"), 32)
            dve.tensor_copy(ptf[:], pti[:]).then_inc(S("rowid"), 1)
            dve.wait_ge(S("rowid"), 1)
            dve.tensor_scalar(ptf[:], ptf[:], 2.0 * BLK / NL, None, ALU.mult).then_inc(S("rowid"), 1)
            dve.wait_ge(S("rowid"), 2)
            dve.tensor_scalar(rowid[:], const("blockrow"), ptf[:, 0:1], None, ALU.add).then_inc(S("rowid"), 1)

        roped, evac, zdec, out_sems = {}, {}, {}, []

        def dest(n, ts):
            if n in (7, 9):
                return vst[:, (n - 7) // 2, ts, :]
            return gs[:, ts, :] if n == 10 else zs[:, DEST[n], ts, :]

        def project(n):
            s, w = sa + n, width[n]

            @block.tensor
            def _(pe):
                w1, w2 = slab_parts(s % 4, KD, w)
                pe.wait_ge(slab_split, s + 1)
                if n == 1:
                    pe.wait_ge(S("rms_sqrt"), at("rms_sqrt"))
                if n >= 2:
                    pe.wait_ge(S("z_row"), evac[n - 2])
                for part, tiles in enumerate((range(0, 4), range(4, 8), range(8, 9))):
                    for t in tiles:
                        a, b = t * P, min(T, (t + 1) * P)
                        if n == 0:
                            if t == 2:
                                late(pe)
                            if t > 0:
                                pe.wait_ge(S("a_lo"), a_ready[(b - 1) // TJ])
                        o = bank[3 * (n % 2) + part][0:b - a, (t % 4) * P:(t % 4) * P + w]
                        for k in range(KD):
                            if n == 0 and t == 0:
                                pe.wait_ge(S("a_lo"), a_ready[0] - KD // 2 + k // 2 + 1)
                            last = product(pe, o, ahi[:, k, a:b], alo[:, k, a:b], w1[:, k, :], w2[:, k, :],
                                           k == 0, k == KD - 1)
                    if part < 2:
                        last.then_inc(S("z_mm"), 1)
                        count("z_mm")
                    else:
                        last.then_inc(slab_used, 1)

            @block.scalar
            def _(act):
                for part in range(3):
                    rows = NDEC if part == 2 else P
                    ts = slice(4 * part, 4 * part + 4) if part < 2 else slice(8, 9)
                    if part == 0:
                        if n in DEST:
                            if n - 2 in DEST:
                                act.wait_ge(S("z_used"), used[n - 2])
                            if n - 2 in zdec:
                                act.wait_ge(S("z_dec"), zdec[n - 2])
                            for name in slot_out.get(DEST[n], []):
                                act.wait_ge(S(name), 32)
                            act.wait_ge(S("z_clear"), 2)
                    if part < 2:
                        act.wait_ge(S("z_mm"), at("z_mm") - 1 + part)
                    else:
                        act.wait_ge(slab_used, s + 1)
                    nt = 4 if part < 2 else 1
                    src = bank[3 * (n % 2) + part][0:rows, 0:nt * P].rearrange("p (t n) -> p t n", n=P)[:, :, 0:w]
                    act.activation(dest(n, ts)[0:rows], src, ACT.Sigmoid if n == 10 else ACT.Copy,
                                   scale=IWS / 8 if KINDS[n] == "q" else IWS).then_inc(S("z_row"), 1)
                    evac[n] = count("z_row")

            if n in DEST and n != 5:
                z = zs[:, DEST[n]].rearrange("p t (h d) -> p t h d", h=2)
                x1, x2 = z[:, :, :, 0:8], z[:, :, :, 8:16]
                cosb, sinb = (const(m).rearrange("p (t r) -> p t r", t=TT + 1).unsqueeze(2)
                              .to_broadcast([P, TT + 1, 2, 8]) for m in ("cos", "sin"))
                r = [rot[:, m, :].rearrange("p (t h r) -> p t h r", t=TT + 1, h=2) for m in range(4)]

                @block.vector
                def _(dve):
                    dve.wait_ge(S("z_row"), evac[n])
                    if at("rope"):
                        dve.wait_ge(S("rope"), at("rope"))
                    for m, (xx, cs) in enumerate(((x1, cosb), (x2, sinb), (x2, cosb), (x1, sinb))):
                        dve.tensor_tensor(r[m], xx, cs, ALU.mult).then_inc(S("rope"), 1)
                        count("rope")
                    dve.wait_ge(S("rope"), at("rope"))
                    dve.tensor_tensor(x1, r[0], r[1], ALU.subtract).then_inc(S("rope"), 1)
                    dve.tensor_tensor(x2, r[2], r[3], ALU.add).then_inc(S("rope"), 1)
                    roped[n] = count("rope", 2)
                    if n in ZD:
                        dve.wait_ge(S("rope"), roped[n])
                        dve.tensor_copy(zd[:, ZD[n], :], zs[0:NDEC, DEST[n], TT, :]).then_inc(S("z_dec"), 1)
                        zdec[n] = count("z_dec")
            if n in outs:
                name, kv = outs[n]

                @block.scalar
                def _(act):
                    if n in roped:
                        act.wait_ge(S("rope"), roped[n])
                    else:
                        act.wait_ge(S("z_row"), evac[n])
                    t0 = 4 if name == "win" else 0
                    o = O[f"{name}_kv_prompt"][0, 0].rearrange("(t p) v g d -> p t v (g d)", p=P)
                    act.dma_start(o[:, :, kv, :], dest(n, slice(t0, TT))).then_inc(S(f"out{n}"), 16)
                    o = O[f"{name}_kv_sample"][0][:, WIN - 1 if name == "win" else 0, kv].rearrange("b g d -> b (g d)")
                    act.dma_start(o, dest(n, slice(TT, TT + 1))[0:NDEC, 0, :]).then_inc(S(f"out{n}"), 16)
                    out_sems.append((f"out{n}", 32))
                    if n in DEST:
                        slot_out[DEST[n]] = [f"out{n}"]

        ZD = {0: 0, 1: 1, 2: 2, 3: 3, 6: 4, 8: 5}
        used, slot_out, tsplit = {}, {}, {}

        def transposed(n):
            if n not in DEST:
                return
            if n in (4, 5):
                used[n] = at("z_used")
                return
            for half in range(2):
                b = bank[6 + half]
                sl = slice(half * 512, half * 512 + 512)

                @block.tensor
                def _(pe):
                    pe.wait_ge(S("rope"), roped[n])
                    if tsplit.get(half):
                        pe.wait_ge(S("zT_lo"), tsplit[half])
                    for t in range(4):
                        last = pe.transpose(b[:, t * P:(t + 1) * P], zs[:, DEST[n], 4 * half + t, :], const("ident"))
                    last.then_inc(S("z_used"), 1)
                    used[n] = count("z_used")
                for r in range(2):
                    rows, other = slice(64 * r, 64 * r + 64), slice(64 - 64 * r, 128 - 64 * r)
                    if n < 4:
                        hi, lo = qst[rows, 2 * n + r, sl], qst[other, 2 * n + r, sl]
                    else:
                        hi, lo = kst[rows, (n - 6) // 2, r, 0, sl], kst[rows, (n - 6) // 2, r, 1, sl]

                    @block.scalar
                    def _(act):
                        act.wait_ge(S("z_used"), used[n])
                        act.activation(hi, b[rows, :], ACT.Copy).then_inc(S("zT_hi"), 1)
                        count("zT_hi")

                    @block.vector
                    def _(dve):
                        dve.wait_ge(S("zT_hi"), at("zT_hi"))
                        dve.tensor_tensor(lo, b[rows, :], hi, ALU.subtract).then_inc(S("zT_lo"), 1)
                        tsplit[half] = count("zT_lo")
            if n >= 6:
                @block.vector
                def _(dve):
                    dve.wait_ge(S("zT_lo"), at("zT_lo"))
                    for r in range(2):
                        rows, other = slice(64 * r, 64 * r + 64), slice(64 - 64 * r, 128 - 64 * r)
                        for part in range(2):
                            dve.tensor_copy(kst[other, (n - 6) // 2, r, part, :], kst[rows, (n - 6) // 2, r, part, :])\
                               .then_inc(S("k_twice"), 1)
                            count("k_twice")

        for n in range(12):
            if n < 11:
                project(n)
            if n >= 1:
                transposed(n - 1)
        z_end = {m: at(m) for m in ("z_row", "zT_lo", "zT_hi", "k_twice", "z_used", "rope", "z_dec")}

        @block.tensor
        def _(pe):
            pe.wait_ge(S("z_dec"), at("z_dec"))
            pe.wait_ge(S("zT_lo"), at("zT_lo"))
            pe.wait_ge(S("z_row"), at("z_row"))
            for m in range(6):
                last = pe.transpose(bank[6][:, 16 * m:16 * m + NDEC], zd[:, m, :], const("ident", NDEC)[:, 0:NDEC])
            last.then_inc(S("dT_mm"), 1)
            pe.matmul(bank[7][0:R, 0:GC], const("seqrep", NDEC)[:, 0:R], gs[0:NDEC, TT, :], start=True, stop=True)\
              .then_inc(S("dT_mm"), 1)

        @block.vector
        def _(dve):
            dve.wait_ge(S("dT_mm"), 2)
            for h in range(NH):
                src = bank[6][64 * (h % 2):64 * (h % 2) + 64, 16 * (h // 2):16 * (h // 2) + NDEC]
                g = h // HPG
                dve.tensor_copy(qd[64 * g:64 * g + 64, :, h], src).then_inc(S("dec_q"), 1)
            for br in range(2):
                dve.tensor_copy(knt[:, br, :], bank[6][:, 64 + 16 * br:64 + 16 * br + NDEC]).then_inc(S("dec_q"), 1)
            g3 = rot[0:R, 0, 0:GC].rearrange("p (b h) -> p b h", h=NH)
            dve.wait_ge(S("rope"), at("rope"))
            dve.tensor_tensor(g3, bank[7][0:R, 0:GC].rearrange("p (b h) -> p b h", h=NH),
                              const("ownhead", R).unsqueeze(1).to_broadcast([R, 3, NH]), ALU.mult)\
               .then_inc(S("dec_q"), 1)
            dve.wait_ge(S("dec_q"), 11)
            dve.reduce_sum(gdec[:], g3, AX_X).then_inc(S("dec_q"), 1)
            dve.wait_ge(S("dec_q"), 12)
        count("dec_q", 12)

        NBK = NDEC * NB + NB
        NL = 4
        NLC = BLK // NL
        cx = nc.alloc_sbuf_tensor_at("cx", [P, 2, NL * 2 * P], F32, offset=free_at)
        cxs = nc.alloc_sbuf_tensor_at("cxs", [P, 2, NL * 2 * P], F32, offset=free_at + 2 * NL * 2 * P * 4)
        cursor[0] = mixwork
        cxp = place("cxp", [NB, 2, NL * 2 * P], F32)
        cxps = place("cxps", [NB, 2, NL * 2 * P], F32)
        xth = place("xth", [P, 3, NG * NBK], F16)
        xtl = place("xtl", [P, 3, NG * NBK], F16)
        hid = place("hid", [P, 2, NG * NBK], F32)
        hidh = place("hidh", [P, 2, NG * NBK], F16)
        hidl = place("hidl", [P, 2, NG * NBK], F16)
        vcp = place("vcp", [NB, P], F32)

        @block.sync
        def _(sp):
            for n in range(8):
                v, m = n % 2, n // 2
                load_const(sp, sphi + n,
                           I["phi_w1"][0, v, m * 8 * P:(m + 1) * 8 * P, :].rearrange("(k p) n -> p k n", p=P), 8)
            load_const(sp, sw2, I["phi_w2"][0].rearrange("v p d -> p v d"), 2, HD)

        cache_rows = I["cache_cmp_kv"][0].rearrange("r (a l) v g d -> (r a) (l v g d)", l=NL)
        new_rows = O["cmp_kv_prompt"][0, 0].rearrange("(n a l) v g d -> n a (l v g d)", a=NLC, l=NL)
        xbank = [bank[0], bank[1], bank[4]]
        chunks = [(lc, v, m) for lc in range(NLC) for v in range(2) for m in range(2)]

        def gather(lc):
            @block.gpsimd
            def _(pool):
                if lc == 0:
                    pool.wait_ge(S("rowid"), 3)
                    pool.wait_ge(slab_used, sa + 1)
                if lc >= 2:
                    pool.wait_ge(S("cx_used"), lc - 1)
                pool.indirect_dma_start(cx[:, lc % 2, :], None, cache_rows,
                                        bass.IndirectOffsetOnAxis(ap=rowid[:, lc:lc + 1], axis=0))\
                    .then_inc(S(f"gathered{lc % 2}"), 16)

            @block.scalar
            def _(act):
                if lc == 0:
                    for n in (4, 5, 6, 8):
                        act.wait_ge(S(f"out{n}"), 32)
                    act.wait_ge(S("dec_q"), 12)
                if lc >= 2:
                    act.wait_ge(S("cxp_used"), lc - 1)
                act.dma_start(cxp[:, lc % 2, :], new_rows[:, lc, :]).then_inc(S(f"cxp_in{lc % 2}"), 16)

        def permute(lc):
            for src, dst, eng, n, full, used_sem, ready_sem in (
                    (cx, cxs, block.vector, P, "gathered", "cx_used", "cx_side"),
                    (cxp, cxps, block.scalar, NB, "cxp_in", "cxp_used", "cxp_side")):
                a = src[:, lc % 2, :].rearrange("p (m l x d) -> p m x l d", m=NL // 2, l=2, d=HD)
                b = dst[:, lc % 2, :].rearrange("p (m x l d) -> p m x l d", m=NL // 2, l=2, d=HD)

                @eng
                def _(e):
                    e.wait_ge(S(f"{full}{lc % 2}"), 16 * (lc // 2 + 1))
                    if lc >= 2:
                        e.wait_ge(S("xt_mm"), 4 * (lc - 1))
                    for m in range(NL // 2):
                        op = e.tensor_copy(b[:, m], a[:, m]) if n == P else \
                            e.activation(b[:, m], a[:, m], ACT.Copy)
                        op.then_inc(S(used_sem if m else ready_sem), 1)

        for lc in range(2):
            gather(lc)
        permute(0)

        @block.gpsimd
        def _(pool):
            for n in range(4):
                split_const(pool, sphi + n, KD * P)

        @block.tensor
        def _(pe):
            pe.wait_ge(S("dec_q"), 12)

        for u in range(len(chunks) + 2):
            if u < len(chunks):
                lc, v, m = chunks[u]
                if v == 0 and m == 0 and lc + 1 < NLC:
                    permute(lc + 1)
                    if lc + 2 < NLC:
                        gather(lc + 2)
                    if lc in (4, 5, 8, 9):
                        @block.gpsimd
                        def _(pool):
                            split_const(pool, sphi + 4 + lc // 4 * 2 - 2 + lc % 4, KD * P)

                @block.tensor
                def _(pe):
                    if v == 0 and m == 0:
                        pe.wait_ge(S("cx_used"), lc + 1)
                        pe.wait_ge(S("cxp_used"), lc + 1)
                    if u >= 3:
                        pe.wait_ge(S("xt_lo"), u - 2)
                    for g in range(NG):
                        for src, n, c0 in ((cxs, P, 0), (cxps, NB, P)):
                            at_ = ((m * 2 + v) * NG + g) * P
                            last = pe.transpose(xbank[u % 3][:, g * NBK + c0:g * NBK + c0 + n],
                                                src[:, lc % 2, at_:at_ + P], const("ident", n)[:, 0:n])
                    last.then_inc(S("xt_mm"), 1)
                bias = par2[:, 12 + 32 * v + 2 * lc + m:13 + 32 * v + 2 * lc + m]

                @block.scalar
                def _(act):
                    act.wait_ge(S("xt_mm"), u + 1)
                    if u >= 3:
                        act.wait_ge(S("x_mm"), u - 2)
                    act.activation(xth[:, u % 3, :], xbank[u % 3][:, 0:NG * NBK], ACT.Identity, bias=bias)\
                       .then_inc(S("xt_hi"), 1)

                @block.vector
                def _(dve):
                    dve.wait_ge(S("xt_hi"), u + 1)
                    dve.scalar_tensor_tensor(out=xtl[:, u % 3, :], in0=xbank[u % 3][:, 0:NG * NBK], scalar=bias,
                                             in1=xth[:, u % 3, :], op0=ALU.add, op1=ALU.subtract)\
                       .then_inc(S("xt_lo"), 1)
            if u >= 2:
                lc, v, m = chunks[u - 2]

                @block.tensor
                def _(pe):
                    s = sphi + 2 * (lc // 4) + v
                    kc = 2 * (lc % 4) + m
                    w1, w2 = slab_parts(s % 4, KD)
                    pe.wait_ge(slab_split, s + 1)
                    pe.wait_ge(S("xt_lo"), u - 1)
                    last = product(pe, bank[2 + v][:, 0:NG * NBK], w1[:, kc, :], w2[:, kc, :], xth[:, (u - 2) % 3, :],
                                   xtl[:, (u - 2) % 3, :], lc == 0 and m == 0, lc == NLC - 1 and m == 1)
                    last.then_inc(S("x_mm"), 1)
                    if kc == 7:
                        pe.wait_ge(S("x_mm"), u - 1)
                        pe.sem_inc(slab_used, 1)

        @block.gpsimd
        def _(pool):
            split_const(pool, sw2, P)

        @block.scalar
        def _(act):
            act.wait_ge(S("x_mm"), 64)
            for v in range(2):
                act.activation(hid[:, v, :], bank[2 + v][:, 0:NG * NBK], ACT.Silu, bias=par2[:, 76 + v:77 + v],
                               scale=IWS).then_inc(S("hid"), 1)
            act.wait_ge(S("hid"), 2)
            act.activation(hidh[:], hid[:], ACT.Copy).then_inc(S("hid_hi"), 1)

        @block.vector
        def _(dve):
            dve.wait_ge(S("hid_hi"), 1)
            dve.tensor_tensor(hidl[:], hid[:], hidh[:], ALU.subtract).then_inc(S("hid_lo"), 1)

        @block.tensor
        def _(pe):
            w1, w2 = slab_parts(sw2 % 4, 2, HD)
            pe.wait_ge(slab_split, sw2 + 1)
            pe.wait_ge(S("hid_lo"), 1)
            product(pe, bank[4][0:HD, 0:NG * NBK], w1[:, 0, :], w2[:, 0, :], hidh[:, 0, :], hidl[:, 0, :], True, True)\
                .then_inc(S("kc_mm"), 1)
            for g in range(NG):
                for n, c0, o in ((P, g * NBK, 0), (NB, g * NBK + P, 256)):
                    last = product(pe, bank[5][0:n, o + g * HD:o + (g + 1) * HD], hidh[:, 1, c0:c0 + n],
                                   hidl[:, 1, c0:c0 + n], w1[:, 1, :], w2[:, 1, :], True, True)
            last.then_inc(slab_used, 1)

        @block.scalar
        def _(act):
            act.wait_ge(S("kc_mm"), 1)
            for g in range(NG):
                act.activation(kcst[0:HD, g, 0, :], bank[4][0:HD, g * NBK + P:(g + 1) * NBK], ACT.Copy, scale=IWS)\
                   .then_inc(S("kc_hi"), 1)
            for g in range(NG):
                act.activation(kcd[64 * g:64 * g + 64, :], bank[4][0:HD, g * NBK:g * NBK + P], ACT.Copy, scale=IWS)\
                   .then_inc(S("kc_hi"), 1)

        @block.vector
        def _(dve):
            dve.wait_ge(S("kc_hi"), 4)
            for g in range(NG):
                dve.scalar_tensor_tensor(out=kcst[0:HD, g, 1, :], in0=bank[4][0:HD, g * NBK + P:(g + 1) * NBK],
                                         scalar=IWS, in1=kcst[0:HD, g, 0, :], op0=ALU.mult, op1=ALU.subtract)\
                   .then_inc(S("kc_lo"), 1)
            dve.wait_ge(slab_used, sw2 + 1)
            dve.tensor_scalar(vcd[:], bank[5][:, 0:P], IWS, None, ALU.mult).then_inc(S("kc_lo"), 1)
            dve.tensor_scalar(vcp[:], bank[5][0:NB, 256:256 + P], IWS, None, ALU.mult).then_inc(S("kc_lo"), 1)
            dve.wait_ge(S("kc_lo"), 4)
            dve.tensor_copy(kcst[HD:P], kcst[0:HD]).then_inc(S("kc_lo"), 1)

        @block.tensor
        def _(pe):
            pe.wait_ge(S("kc_lo"), 4)
            pe.matmul(bank[0][:, 0:P], const("spread", NB), vcp[:], start=True, stop=True).then_inc(S("vbd_mm"), 1)

        @block.vector
        def _(dve):
            dve.wait_ge(S("vbd_mm"), 1)
            for h in range(NH):
                g = h // HPG
                dve.tensor_scalar(vbd[:, h, :], bank[0][:, g * HD:(g + 1) * HD], const("headmask")[:, h:h + 1], None,
                                  ALU.mult).then_inc(S("vbd"), 1)
        pe_after = {}

        cursor[0] = mixwork
        prob = {"slc": place("prs", [P, 2, SEQ], F32), "win": place("prw", [P, 2, WIN + P], F32),
                "cmp": place("prc", [P, 2, NH * NB], F32)}
        pt = place("pt", [P, 2, TT, P], F32)
        pct = place("pct", [P, 2, P], F32)
        cneg = place("cneg", [P, TT, NB], F32)
        stat = place("stat", [P, 4, 2], F32)
        cstat = place("cstat", [P, 2, NH], F32)
        cp = nc.alloc_sbuf_tensor_at("cp", [P, NH, NB], F32, offset=cursor[0])
        cursor[0] += NH * NB * 4
        dwork_at = cursor[0]
        units = []
        for t in range(TT):
            units.append(("cmp", t, 0))
            for h in range(NH):
                units += [("slc", t, h), ("win", t, h)]
        U = len(units)
        probs, slot_before = [], []
        for u, (kind, t, h) in enumerate(units):
            turn = t if kind == "cmp" else h
            probs.append(prob[kind][:, turn % 2, :])
            before = [w for w in range(u) if units[w][0] == kind and (units[w][1] if kind == "cmp" else units[w][2]) % 2 == turn % 2]
            slot_before.append(before[-1] if before else None)
        psum = banks8[:].rearrange("p b n -> p (b n)")

        def blocks(kind, t):
            return list(range(t + 1)) if kind == "slc" else list(range(max(0, t - WIN // P), t + 1))

        @block.vector
        def _(dve):
            dve.tensor_scalar(cneg[:].rearrange("p t n -> p (t n)"), const("cmpok"), -NEG, NEG, ALU.mult, ALU.add)\
               .then_inc(S("cneg"), 1)
            dve.wait_ge(S("cneg"), 1)

        @block.tensor
        def _(pe):
            for name in ("vbd", "kc_lo", "kc_hi", "zT_lo", "k_twice"):
                pe.wait_ge(S(name), {"vbd": NH, "kc_lo": 5, "kc_hi": 4}.get(name, at(name)))
            for name, v in pe_after.items():
                pe.wait_ge(S(name), v)

        def wide(v):
            return v.unsqueeze(2).to_broadcast([P, NH, NB])

        s_free, exp_done, scaled, t_mm, t_ev, t_ev_b, pv = {}, {}, {}, {}, {}, {}, {}
        bank_ev = {4: 0, 5: 0, 7: 0}
        TL = 3
        PL = 5
        EV = 4

        for u in range(U + PL + 1):
            if u > PL and units[u - PL - 1][0] == "win" and units[u - PL - 1][2] % 2 == 1:
                _, t, h = units[u - PL - 1]
                pair = t * NH // 2 + h // 2

                @block.scalar
                def _(act):
                    act.wait_ge(S("o_mm"), pair + 1)
                    act.activation(oahi[:, h // 2, t * P:(t + 1) * P], bank[6][:, 0:P], ACT.Copy)\
                       .then_inc(S("o_hi"), 1)

                @block.vector
                def _(dve):
                    dve.wait_ge(S("o_hi"), pair + 1)
                    dve.tensor_tensor(oalo[:, h // 2, t * P:(t + 1) * P], bank[6][:, 0:P],
                                      oahi[:, h // 2, t * P:(t + 1) * P], ALU.subtract).then_inc(S("o_lo"), 1)

            if EV <= u <= U + EV - 1:
                v = u - EV
                kind, t, h = units[v]
                nblk = 1 if kind == "cmp" else len(blocks(kind, t))

                @block.scalar
                def _(act):
                    act.wait_ge(S("t_mm"), t_mm[v] - (nblk > 4))
                    if kind == "cmp":
                        if t >= 2:
                            act.wait_ge(S("o_mm"), (t - 1) * NH // 2)
                        act.activation(pct[:, t % 2, :], bank[4 + v % 2][:, 0:P], ACT.Copy).then_inc(S("t_ev_a"), 1)
                    else:
                        if v - 2 in pv:
                            act.wait_ge(S("pv"), pv[v - 2])
                        m = min(4, nblk)
                        act.activation(pt[:, v % 2, 0:m, :].rearrange("p m q -> p (m q)"), bank[4 + v % 2][:, 0:m * P],
                                       ACT.Copy).then_inc(S("t_ev_a"), 1)
                    t_ev[v] = count("t_ev_a")
                    bank_ev[4 + v % 2] = t_ev[v]

                if nblk > 4:
                    @block.vector
                    def _(dve):
                        dve.wait_ge(S("t_mm"), t_mm[v])
                        if v - 2 in pv:
                            dve.wait_ge(S("pv"), pv[v - 2])
                        m = nblk - 4
                        dve.tensor_copy(pt[:, v % 2, 4:nblk, :].rearrange("p m q -> p (m q)"), bank[7][:, 0:m * P])\
                           .then_inc(S("t_ev_b"), 1)
                        bank_ev[7] = t_ev_b[v] = count("t_ev_b")

            if u < U:
                kind, t, h = units[u]
                sl = u % 4
                q0 = t * P
                base_col = u % 2 * 1024
                g, br = h // HPG, 0 if kind == "slc" else 1
                ks = blocks(kind, t)
                n = len(ks) * P

                @block.tensor
                def _(pe):
                    if u >= 2:
                        pe.wait_ge(S(s_free[u - 2][0]), s_free[u - 2][1])
                    if kind == "cmp":
                        for hh in range(NH):
                            o = psum[:, base_col + hh * NB:base_col + (hh + 1) * NB]
                            for part in range(2):
                                last = pe.matmul(o, qst[:, hh, q0:q0 + P], kcst[:, hh // HPG, part, :],
                                                 start=part == 0, stop=part == 1)
                    else:
                        for c in range(0, len(ks), 4):
                            kk = ks[c:c + 4]
                            o = psum[:, base_col + c * P:base_col + c * P + len(kk) * P]
                            masks = [(i, 0) for i, k in enumerate(kk) if k == t] + \
                                    [(i, 1) for i, k in enumerate(kk) if kind == "win" and k == t - WIN // P]
                            for part in range(2):
                                last = pe.matmul(o, qst[:, h, q0:q0 + P],
                                                 kst[:, br, g, part, kk[0] * P:(kk[-1] + 1) * P],
                                                 start=part == 0, stop=part == 1 and not masks)
                            for i, m in masks:
                                last = pe.matmul(o[:, i * P:(i + 1) * P], identb[:], maskb[:, m, :], start=False,
                                                 stop=(i, m) == masks[-1])
                    last.then_inc(S("s_mm"), 1)

                if kind == "cmp":
                    neg = cneg[:, t, :].unsqueeze(1).to_broadcast([P, NH, NB])
                    s3 = psum[:, base_col:base_col + NH * NB].rearrange("p (h n) -> p h n", n=NB)

                    @block.vector
                    def _(dve):
                        dve.wait_ge(S("s_mm"), u + 1)
                        dve.wait_ge(S("cm"), at("cm"))
                        dve.tensor_tensor(cp[:], s3, neg, ALU.add).then_inc(S("s_read"), 1)
                        dve.wait_ge(S("s_read"), at("s_read") + 1)
                        dve.reduce_max(cstat[:, 0, :], cp[:], AX_X).then_inc(S("cm"), 1)
                        dve.wait_ge(S("cm"), count("cm"))
                        dve.tensor_tensor(cp[:], cp[:], wide(cstat[:, 0, :]), ALU.subtract).then_inc(S("cm"), 1)
                    s_free[u] = ("s_read", count("s_read"))
                    cm1 = count("cm")

                    @block.scalar
                    def _(act):
                        act.wait_ge(S("cm"), cm1)
                        act.activation(cp[:], cp[:], ACT.Exp).then_inc(S("c_exp"), 1)
                else:
                    @block.vector
                    def _(dve):
                        dve.wait_ge(S("s_mm"), u + 1)
                        if u >= 4:
                            dve.wait_ge(S(scaled[u - 4][0]), scaled[u - 4][1])
                        dve.reduce_max(stat[:, sl, 0:1], psum[:, base_col:base_col + n], AX_X, negate=True)\
                           .then_inc(S("s_max"), 1)
                        count("s_max")

                    @block.scalar
                    def _(act):
                        act.wait_ge(S("s_max"), at("s_max"))
                        if slot_before[u] is not None:
                            act.wait_ge(S("t_mm"), t_mm[slot_before[u]])
                        act.activation(probs[u][:, 0:n], psum[:, base_col:base_col + n], ACT.Exp, bias=stat[:, sl, 0:1],
                                       accum_out=stat[:, sl, 1:2]).then_inc(S("p_exp"), 1)
                        exp_done[u] = count("p_exp")
                        s_free[u] = ("p_exp", exp_done[u])

            if 1 <= u <= U:
                v = u - 1
                kind, t, h = units[v]
                sl, br = v % 4, 0 if kind == "slc" else 1
                if kind == "cmp":
                    p3 = probs[v].rearrange("p (h n) -> p h n", n=NB)
                    okt = const("cmpok").rearrange("p (t n) -> p t n", n=NB)[:, t, :].unsqueeze(1).to_broadcast([P, NH, NB])
                    @block.vector
                    def _(dve):
                        dve.wait_ge(S("c_exp"), t + 1)
                        if slot_before[v] is not None:
                            dve.wait_ge(S("t_mm"), t_mm[slot_before[v]])
                        dve.tensor_tensor(cp[:], cp[:], okt, ALU.mult).then_inc(S("cm"), 1)
                        dve.wait_ge(S("cm"), count("cm"))
                        dve.reduce_sum(cstat[:, 1, :], cp[:], AX_X).then_inc(S("cm"), 1)
                        dve.wait_ge(S("cm"), count("cm"))
                        dve.tensor_scalar(cstat[:, 1, :], cstat[:, 1, :], 1e-30, None, ALU.max).then_inc(S("cm"), 1)
                        dve.wait_ge(S("cm"), count("cm"))
                        dve.reciprocal(cstat[:, 1, :], cstat[:, 1, :]).then_inc(S("cm"), 1)
                        dve.wait_ge(S("cm"), count("cm"))
                        dve.tensor_tensor(cstat[:, 1, :], cstat[:, 1, :], gs[:, t, 0:NH], ALU.mult).then_inc(S("cm"), 1)
                        dve.wait_ge(S("cm"), count("cm"))
                        dve.tensor_tensor(p3, cp[:], wide(cstat[:, 1, :]), ALU.mult).then_inc(S("pc_scaled"), 1)
                        scaled[v] = ("pc_scaled", count("pc_scaled"))
                        dve.wait_ge(S("pc_scaled"), scaled[v][1])
                else:
                    n = len(blocks(kind, t)) * P

                    @block.vector
                    def _(dve):
                        dve.wait_ge(S("p_exp"), exp_done[v])
                        dve.reciprocal(stat[:, sl, 1:2], stat[:, sl, 1:2]).then_inc(S("p_inv"), 1)
                        count("p_inv")

                    @block.gpsimd
                    def _(pool):
                        pool.wait_ge(S("p_inv"), at("p_inv"))
                        col = (1 + br) * NH + h
                        pool.tensor_scalar(probs[v][:, 0:n], probs[v][:, 0:n], stat[:, sl, 1:2], gs[:, t, col:col + 1],
                                           ALU.mult, ALU.mult).then_inc(S("p_scaled"), 1)
                        scaled[v] = ("p_scaled", count("p_scaled"))

            if TL <= u <= U + TL - 1:
                v = u - TL
                kind, t, h = units[v]
                sl = v % 2
                nblk = 1 if kind == "cmp" else len(blocks(kind, t))
                for c in range(0, nblk, 4):
                    m = min(4, nblk - c)
                    b = 4 + v % 2 if c == 0 else 7

                    @block.tensor
                    def _(pe):
                        pe.wait_ge(S(scaled[v][0]), scaled[v][1])
                        if bank_ev[b]:
                            pe.wait_ge(S("t_ev_b" if b == 7 else "t_ev_a"), bank_ev[b])
                        for i in range(m):
                            last = pe.transpose(bank[b][:, i * P:(i + 1) * P], probs[v][:, (c + i) * P:(c + i + 1) * P],
                                                const("ident"))
                        last.then_inc(S("t_mm"), 1)
                        t_mm[v] = count("t_mm")

            if PL <= u <= U + PL - 1:
                v = u - PL
                kind, t, h = units[v]
                sl = v % 2
                if kind != "cmp":
                    g, br = h // HPG, 0 if kind == "slc" else 1
                    ks = blocks(kind, t)
                    pair = t * NH // 2 + h // 2
                    o = bank[6][64 * (h % 2):64 * (h % 2) + 64, 0:P]

                    @block.tensor
                    def _(pe):
                        pe.wait_ge(S("t_ev_a"), t_ev[v])
                        if len(ks) > 4:
                            pe.wait_ge(S("t_ev_b"), t_ev_b[v])
                        if kind == "slc":
                            if h % 2 == 0 and pair >= 1:
                                pe.wait_ge(S("o_lo"), pair)
                            pe.matmul(o, vbd[:, h, :], pct[:, t % 2, :], start=True, stop=False)
                        for i, k in enumerate(ks):
                            last = pe.matmul(o, vst[:, br, k, g * HD:(g + 1) * HD], pt[:, sl, i, :], start=False,
                                             stop=kind == "win" and i == len(ks) - 1)
                        pv_end = kind == "win" and h % 2 == 1
                        last.then_inc(S("o_mm" if pv_end else "pv"), 1)
                        if not pv_end:
                            pv[v] = count("pv")
                        else:
                            pv[v] = at("pv")

        at_s_mm = U

        cursor[0] = qst_at
        NKB = NPAGE + WIN // P
        ring = place("ring", [P, 2, NKB, P], F32)
        ktr = place("ktr", [P, 2, NKB, P], F32)
        qpad = place("qpad", [P, NDEC, R], F32)
        dprod = place("dprod", [P, R], F32)
        assert cursor[0] <= vst_at
        cursor[0] = dwork_at
        ptrow = place("ptrow", [1, NDEC * NPAGE], I32)
        cursor[0] = mixwork
        sds = place("sds", [R, PAST + 1], F32)
        sdw = place("sdw", [R, WIN + 1], F32)
        sdc = place("sdc", [R, 4, NB], F32)
        dst = place("dst", [R, 16], F32)
        pdiag = place("pdiag", [R, NDEC, NB], F32)
        ptd = place("ptd", [P, NKB + 1, R], F32)
        osb = place("osb", [NH, NDEC, P], F32)
        newp = place("newp", [R, 2, R], F32)
        newr = place("newr", [NDEC, 2, R], F32)
        ot = place("ot", [P, R], F32)
        oth = place("oth", [P, R], F16)
        otl = place("otl", [P, R], F16)
        assert cursor[0] <= dwork_at
        rounds = 2 * NDEC
        s_mm_end, o_end = at_s_mm, TT * NH // 2

        def load_pages(eng, r, pages, sem_name="ring_in"):
            kv, b = r // NDEC, r % NDEC
            if r == 0:
                eng.wait_ge(S("ptrow_in"), 16)
                eng.wait_ge(S("s_mm"), s_mm_end)
            if r >= 2:
                eng.wait_ge(S("ring_used"), r - 1)
            for n in pages:
                page = eng.value_load(ptrow[0:1, b * NPAGE + n:b * NPAGE + n + 1], min_val=0, max_val=NPHYS - 1)
                eng.dma_start(ring[:, r % 2, n:n + 1, :],
                              I["cache_slc_kv"][0][bass.ds(page, 1), :, kv].rearrange("a p g d -> p a (g d)"))\
                   .then_inc(S(f"{sem_name}{r % 2}"), 16)

        def loaded(pe, r):
            pe.wait_ge(S(f"ring_in{r % 2}"), 16 * (NPAGE - 3 + 1) * (r // 2 + 1))
            pe.wait_ge(S(f"gathered{r % 2}"), 16 * NLC // 2 + 16 * 3 * (r // 2 + 1))

        @block.gpsimd
        def _(pool):
            for r in range(rounds):
                load_pages(pool, r, range(3, 6), "gathered")

        @block.scalar
        def _(act):
            load_pages(act, 0, range(6, NPAGE))
            load_pages(act, 1, range(6, NPAGE))

        @block.sync
        def _(sp):
            sp.wait_ge(S("s_mm"), 1)
            sp.dma_start(ptrow[:], I["page_table"].rearrange("(o b) n -> o (b n)", o=1)).then_inc(S("ptrow_in"), 16)
            sp.wait_ge(S("ptrow_in"), 16)
            for r in range(rounds):
                kv, b = r // NDEC, r % NDEC
                load_pages(sp, r, range(0, 3))
                sp.dma_start(ring[:, r % 2, NPAGE:NKB, :],
                             I["state_win_kv"][0][b, :, kv].rearrange("(c p) g d -> p c (g d)", p=P))\
                  .then_inc(S(f"ring_in{r % 2}"), 16)

        @block.vector
        def _(dve):
            dve.wait_ge(S("s_mm"), s_mm_end)
            dve.wait_ge(S("p_scaled"), at("p_scaled"))
            dve.wait_ge(S("o_lo"), o_end)
            dve.wait_ge(S("pv"), at("pv"))
            dve.wait_ge(S("t_ev_a"), at("t_ev_a"))
            dve.memset(qpad[:], 0.0).then_inc(S("dq"), 1)
            dve.wait_ge(S("dq"), 1)
            for b in range(NDEC):
                dve.tensor_copy(qpad[:, b, b * NH:(b + 1) * NH], qd[:, b, :]).then_inc(S("dq"), 1)
            dve.tensor_tensor(dprod[:].rearrange("p (b h) -> p b h", h=NH), qd[:],
                              knt[:, 0, :].unsqueeze(2).to_broadcast([P, NDEC, NH]), ALU.mult).then_inc(S("dq"), 1)

        @block.tensor
        def _(pe):
            pe.wait_ge(S("o_lo"), o_end)
            pe.wait_ge(S("t_ev_a"), at("t_ev_a"))
            pe.wait_ge(S("t_ev_b"), at("t_ev_b"))
            pe.wait_ge(S("s_read"), at("s_read"))
            pe.wait_ge(S("p_exp"), at("p_exp"))
            pe.wait_ge(S("dq"), 10)
            for b in range(NDEC):
                last = pe.matmul(bank[6][0:R, 0:NB], qpad[:, b, :], kcd[:, b * NB:(b + 1) * NB], start=b == 0,
                                 stop=b == NDEC - 1)
            last.then_inc(S("dc_mm"), 1)
            pe.matmul(bank[7][0:R, 0:1], dprod[:], const("mean")[:, 0:1], start=True, stop=True).then_inc(S("dn_mm"), 1)

        def d(i, n=1):
            return dst[:, i:i + n]

        @block.vector
        def _(dve):
            dve.wait_ge(S("dn_mm"), 1)
            dve.tensor_scalar(sds[:, PAST:PAST + 1], bank[7][0:R, 0:1], float(D), None, ALU.mult).then_inc(S("dq"), 1)
            dve.tensor_tensor(dprod[:].rearrange("p (b h) -> p b h", h=NH), qd[:],
                              knt[:, 1, :].unsqueeze(2).to_broadcast([P, NDEC, NH]), ALU.mult).then_inc(S("dq"), 1)
            dve.wait_ge(S("dc_mm"), 1)
            dve.tensor_copy(sdc[:, 0, :], bank[6][0:R, 0:NB]).then_inc(S("dc"), 1)
            dve.wait_ge(S("dc"), 1)
            dve.reduce_max(d(0), sdc[:, 0, :], AX_X, negate=True).then_inc(S("dc"), 1)

        @block.tensor
        def _(pe):
            pe.wait_ge(S("dq"), 12)
            pe.matmul(bank[7][0:R, 0:1], dprod[:], const("mean")[:, 0:1], start=True, stop=True).then_inc(S("dn_mm"), 1)

        @block.scalar
        def _(act):
            act.wait_ge(S("dc"), 2)
            act.activation(sdc[:, 1, :], sdc[:, 0, :], ACT.Exp, bias=d(0), accum_out=d(1)).then_inc(S("dc_exp"), 1)

        @block.vector
        def _(dve):
            dve.wait_ge(S("dn_mm"), 2)
            dve.tensor_scalar(sdw[:, WIN:WIN + 1], bank[7][0:R, 0:1], float(D), None, ALU.mult).then_inc(S("dq"), 1)
            dve.wait_ge(S("dc_exp"), 1)
            dve.reciprocal(d(1), d(1)).then_inc(S("dc"), 1)
            dve.wait_ge(S("dc"), 3)
            dve.tensor_scalar(sdc[:, 1, :], sdc[:, 1, :], d(1), None, ALU.mult).then_inc(S("dc"), 1)

        @block.tensor
        def _(pe):
            pe.wait_ge(S("dc"), 4)
            pe.wait_ge(S("dq"), 13)
            pe.matmul(bank[7][0:R, 0:NB], const("group", R)[:, 0:R], sdc[:, 1, :], start=True, stop=True)\
              .then_inc(S("imp_mm"), 1)

        @block.vector
        def _(dve):
            order = const("order", R)
            other = slice(1, NB - 1)
            dve.wait_ge(S("imp_mm"), 1)
            dve.tensor_copy(sdc[:, 2, :], bank[7][0:R, 0:NB]).then_inc(S("dc"), 1)
            dve.wait_ge(S("dc"), 5)
            dve.tensor_reduce(d(2), sdc[:, 2, other], AX_X, ALU.min).then_inc(S("dc"), 1)
            dve.wait_ge(S("dc"), 6)
            dve.tensor_scalar(sdc[:, 3, other], sdc[:, 2, other], d(2), None, ALU.is_le).then_inc(S("dc"), 1)
            dve.wait_ge(S("dc"), 7)
            dve.tensor_tensor(sdc[:, 3, other], sdc[:, 3, other], order, ALU.mult).then_inc(S("dc"), 1)
            dve.wait_ge(S("dc"), 8)
            dve.reduce_max(d(3), sdc[:, 3, other], AX_X).then_inc(S("dc"), 1)
            dve.wait_ge(S("dc"), 9)
            dve.tensor_scalar(sdc[:, 3, other], order, d(3), NEG, ALU.is_equal, ALU.mult).then_inc(S("dc"), 1)
            dve.tensor_scalar(sdc[:, 1, :], sdc[:, 1, :], gdec[:, 0:1], None, ALU.mult).then_inc(S("dc"), 1)
            dve.wait_ge(S("dc"), 11)
            dve.tensor_tensor(pdiag[:], sdc[:, 1, :].unsqueeze(1).to_broadcast([R, NDEC, NB]),
                              const("seqmask", R).unsqueeze(2).to_broadcast([R, NDEC, NB]), ALU.mult)\
               .then_inc(S("dc"), 1)

        for r in range(NDEC + 1):
            if r < NDEC:
                @block.tensor
                def _(pe):
                    loaded(pe, r)
                    for c in range(3):
                        if r >= 1:
                            pe.wait_ge(S("kt_b") if c == 2 else S("kt_a"), r if c == 2 else 2 * r - 1 + c)
                        for i in range(4):
                            last = pe.transpose(bank[3 + c][:, i * P:(i + 1) * P], ring[:, r % 2, 4 * c + i, :],
                                                const("ident"))
                        last.then_inc(S("ring_used" if c == 2 else "kt_mm"), 1)

                @block.scalar
                def _(act):
                    for c in range(2):
                        act.wait_ge(S("kt_mm"), 2 * r + c + 1)
                        if r >= 2:
                            act.wait_ge(S("ds_mm"), r - 1)
                        act.activation(ktr[:, r % 2, 4 * c:4 * c + 4, :].rearrange("p c n -> p (c n)"), bank[3 + c],
                                       ACT.Copy).then_inc(S("kt_a"), 1)
                    load_pages(act, r + 2, range(6, NPAGE))

                @block.vector
                def _(dve):
                    dve.wait_ge(S("ring_used"), r + 1)
                    if r >= 2:
                        dve.wait_ge(S("ds_mm"), r - 1)
                    dve.tensor_copy(ktr[:, r % 2, 8:12, :].rearrange("p c n -> p (c n)"), bank[5]).then_inc(S("kt_b"), 1)
            if r >= 1:
                @block.tensor
                def _(pe):
                    b = r - 1
                    pe.wait_ge(S("kt_a"), 2 * b + 2)
                    pe.wait_ge(S("kt_b"), b + 1)
                    for c in range(3):
                        last = pe.matmul(bank[c][0:R, :], qpad[:, b, :],
                                         ktr[:, b % 2, 4 * c:4 * c + 4, :].rearrange("p c n -> p (c n)"),
                                         start=b == 0, stop=b == NDEC - 1)
                    last.then_inc(S("ds_mm"), 1)

        @block.vector
        def _(dve):
            dve.wait_ge(S("ds_mm"), NDEC)
            dve.wait_ge(S("dc"), 12)
            dve.tensor_copy(sds[:, 0:PAST], psum[0:R, 0:PAST]).then_inc(S("dx"), 1)
            dve.tensor_copy(sdw[:, 0:WIN], bank[2][0:R, :]).then_inc(S("dx"), 1)
            dve.wait_ge(S("dx"), 2)
            kept = sds[:, BLK:BLK * (NB - 1)].rearrange("p (n l) -> p n l", l=BLK)
            dve.tensor_tensor(kept, kept, sdc[:, 3, 1:NB - 1].unsqueeze(2).to_broadcast([R, NB - 2, BLK]), ALU.add)\
               .then_inc(S("dx"), 1)
            dve.memset(sdw[:, 0:1], NEG).then_inc(S("dx"), 1)
            dve.wait_ge(S("dx"), 4)
            dve.reduce_max(d(4), sds[:], AX_X, negate=True).then_inc(S("dx"), 1)
            dve.reduce_max(d(5), sdw[:], AX_X, negate=True).then_inc(S("dx"), 1)

        @block.scalar
        def _(act):
            act.wait_ge(S("dx"), 6)
            act.activation(sds[:], sds[:], ACT.Exp, bias=d(4), accum_out=d(6)).then_inc(S("dx_exp"), 1)
            act.activation(sdw[:], sdw[:], ACT.Exp, bias=d(5), accum_out=d(7)).then_inc(S("dx_exp"), 1)
            for r in range(NDEC + 2, rounds):
                load_pages(act, r, range(6, NPAGE))

        @block.vector
        def _(dve):
            dve.wait_ge(S("dx_exp"), 2)
            dve.reciprocal(d(6, 2), d(6, 2)).then_inc(S("dx"), 1)
            dve.wait_ge(S("dx"), 7)
            dve.tensor_scalar(sds[:], sds[:], d(6), gdec[:, 1:2], ALU.mult, ALU.mult).then_inc(S("dx"), 1)
            dve.tensor_scalar(sdw[:], sdw[:], d(7), gdec[:, 2:3], ALU.mult, ALU.mult).then_inc(S("dx"), 1)
            dve.wait_ge(S("dx"), 9)
            for br, col in ((0, sds[:, PAST:PAST + 1]), (1, sdw[:, WIN:WIN + 1])):
                dve.tensor_scalar(newp[:, br, :], const("ident", R)[:, 0:R], col, None, ALU.mult).then_inc(S("dx"), 1)

        @block.tensor
        def _(pe):
            pe.wait_ge(S("dx"), 9)
            pe.wait_ge(S("kt_a"), 2 * NDEC)
            pe.wait_ge(S("kt_b"), NDEC)
            for i in range(NPAGE):
                last = pe.transpose(bank[3][:, i * R:(i + 1) * R], sds[:, i * P:(i + 1) * P], const("ident", R)[:, 0:R])
            last.then_inc(S("dp_mm"), 1)
            for i in range(WIN // P):
                pe.transpose(bank[4][:, i * R:(i + 1) * R], sdw[:, i * P:(i + 1) * P], const("ident", R)[:, 0:R])
            pe.transpose(bank[4][:, 4 * R:5 * R], pdiag[:].rearrange("p b n -> p (b n)"), const("ident", R)[:, 0:R])\
              .then_inc(S("dp_mm"), 1)
            pe.wait_ge(S("dx"), 11)
            for br in range(2):
                last = pe.matmul(bank[5][0:NDEC, br * R:(br + 1) * R], const("seqmask", R), newp[:, br, :],
                                 start=True, stop=True)
            last.then_inc(S("dp_mm"), 1)

        @block.vector
        def _(dve):
            dve.wait_ge(S("dp_mm"), 1)
            dve.tensor_copy(ptd[:, 0:NPAGE, :].rearrange("p c n -> p (c n)"), bank[3]).then_inc(S("dp"), 1)
            dve.wait_ge(S("dp_mm"), 2)
            dve.tensor_copy(ptd[:, NPAGE:NKB + 1, :].rearrange("p c n -> p (c n)"), bank[4][:, 0:5 * R])\
               .then_inc(S("dp"), 1)
            dve.wait_ge(S("dp_mm"), 3)
            dve.tensor_copy(newr[:].rearrange("p c n -> p (c n)"), bank[5][0:NDEC, 0:2 * R]).then_inc(S("dp"), 1)

        @block.tensor
        def _(pe):
            pe.wait_ge(S("dp"), 3)
            for r in range(NDEC, rounds):
                b = r - NDEC
                loaded(pe, r)
                for i in range(NKB):
                    last = pe.matmul(psum[0:NH, b * P:(b + 1) * P], ptd[:, i, b * NH:(b + 1) * NH], ring[:, r % 2, i, :],
                                     start=i == 0, stop=i == NKB - 1)
                last.then_inc(S("ring_used"), 1)

        @block.vector
        def _(dve):
            dve.wait_ge(S("ring_used"), rounds)
            dve.tensor_copy(osb[:].rearrange("p b n -> p (b n)"), psum[0:NH, 0:NDEC * P]).then_inc(S("dp"), 1)

        @block.tensor
        def _(pe):
            o = bank[2][:, 0:R]
            pe.matmul(o, vcd[:], ptd[:, NKB, :], start=True, stop=False)
            for br in range(2):
                pe.matmul(o, vst[0:NDEC, br, TT, :], newr[:, br, :], start=False, stop=False)
            pe.wait_ge(S("dp"), 4)
            for b in range(NDEC):
                last = pe.matmul(o[:, b * NH:(b + 1) * NH], osb[:, b, :], const("ident", NH)[:, 0:NH], start=False,
                                 stop=b == NDEC - 1)
            last.then_inc(S("dp_mm"), 1)

        @block.vector
        def _(dve):
            dve.wait_ge(S("dp_mm"), 4)
            dve.tensor_copy(oth[:], bank[2][:, 0:R]).then_inc(S("dp"), 1)
            dve.wait_ge(S("dp"), 5)
            dve.tensor_tensor(otl[:], bank[2][:, 0:R], oth[:], ALU.subtract).then_inc(S("dp"), 1)
            dve.wait_ge(S("dp"), 6)
            for dst_, src in ((oahi, oth), (oalo, otl)):
                for h in range(NH):
                    g, to = h // HPG, 64 * (h % 2)
                    dve.tensor_copy(dst_[to:to + 64, h // 2, SEQ:T],
                                    src[64 * g:64 * g + 64, :].rearrange("p (b h) -> p b h", h=NH)[:, :, h])\
                       .then_inc(S("dp"), 1)

        cursor[0] = qst_at
        cihi = place("cihi", [P, KC, T], F16)
        cilo = place("cilo", [P, KC, T], F16)
        mhi = place("mhi", [P, KD, T], F16)
        mlo = place("mlo", [P, KD, T], F16)
        late_at = cursor[0]
        hc = place("hc", [P, T], F32)
        uc = place("uc", [P, 2, T + 2], F32)
        yc = place("yc", [P, T], F32)
        ci = hc
        srow = place("srow", [2 * NDEC, DCONV], F32)
        stc = place("stc", [P, KC, 2 * NDEC], F32)
        tail = place("tail", [2 + NDEC, DCONV], F32)
        o_ready = at("o_lo")
        STREAM = []
        for c in range(KC):
            STREAM += [(0, c), ("ada", 4 * c), (1, c), ("ada", 4 * c + 1), (2, c), ("ada", 4 * c + 2), ("ada", 4 * c + 3)]
        assert 4 * KC == LATE

        @block.sync
        def _(sp):
            for v, (kind, c) in enumerate(STREAM):
                if kind == "ada":
                    load_const(sp, sconv + v, ada_src(NMOD - LATE + c), KD)
                else:
                    load_const(sp, sconv + v, cols(CONV0 + (0, 2 * DCONV, DCONV)[kind] + c * P, P), KD)
                if v == 1:
                    sp.wait_ge(S("dp"), 22)
                    sp.dma_start(srow[:], I["state_conv"][0].rearrange("b j n -> (b j) n")).then_inc(S("srow_in"), 16)
                    sp.dma_start(O["conv_sample"][0][:, 0, :], I["state_conv"][0][:, 1, :]).then_inc(S("shifts"), 16)

        @block.gpsimd
        def _(pool):
            for v in range(len(STREAM)):
                split_const(pool, sconv + v, KD * P)

        @block.vector
        def _(dve):
            dve.wait_ge(S("dp"), 22)
            dve.memset(uc[:, :, 0:2], 0.0).then_inc(S("u_clear"), 1)

        @block.tensor
        def _(pe):
            pe.wait_ge(S("dp"), 6)
            pe.wait_ge(S("srow_in"), 16)
            for c in range(KC):
                last = pe.transpose(bank[7][:, c * 2 * NDEC:(c + 1) * 2 * NDEC], srow[:, c * P:(c + 1) * P],
                                    const("ident", 2 * NDEC)[:, 0:2 * NDEC])
            last.then_inc(S("stc_mm"), 1)

        @block.vector
        def _(dve):
            dve.wait_ge(S("stc_mm"), 1)
            dve.tensor_copy(stc[:].rearrange("p c n -> p (c n)"), bank[7][:, 0:KC * 2 * NDEC]).then_inc(S("stc"), 1)
            dve.wait_ge(S("stc"), 1)

        W = par2[:, 0:3 * KC].rearrange("p (j c) -> p j c", j=3)
        for v, (kind, c) in enumerate(STREAM):
            s = sconv + v
            if kind == "ada":
                q = NMOD - LATE + c

                @block.tensor
                def _(pe):
                    if c == 0:
                        pe.wait_ge(S("stc"), 1)
                    pe.wait_ge(slab_split, s + 1)
                    ada_product(pe, s % 4, q, 7, 1)

                @block.scalar
                def _(act):
                    ada_value(act, s, q, 7)
                continue
            n = 3 * c + kind

            @block.tensor
            def _(pe):
                w1, w2 = slab_parts(s % 4, KD)
                pe.wait_ge(slab_split, s + 1)
                for j in range(NJ):
                    a, b = third(j)
                    if n >= 2:
                        m = n - 2
                        name, v = {0: ("hc", m // 3 * 3 + j + 1), 1: ("uc", m // 3 * 3 + j + 1),
                                   2: ("ci", m // 3 * 3 + j + 1)}[m % 3]
                        pe.wait_ge(S(name), v)
                    for k in range(KD):
                        last = product(pe, bank[3 * (n % 2) + j][:, 0:TJ], w1[:, k, :], w2[:, k, :], ahi[:, k, a:b],
                                       alo[:, k, a:b], k == 0, k == KD - 1)
                    last.then_inc(S("cv_mm") if j < 2 else slab_used, 1)

            def arrived_third(eng, j):
                eng.wait_ge(S("cv_mm") if j < 2 else slab_used, 2 * n + j + 1 if j < 2 else s + 1)

            if kind == 0:
                @block.scalar
                def _(act):
                    for j in range(NJ):
                        a, b = third(j)
                        arrived_third(act, j)
                        if c == 0:
                            act.wait_ge(S("u_clear"), 1)
                        if c >= 1:
                            act.wait_ge(S("ci_lo"), (c - 1) * 3 + j + 1)
                        act.activation(hc[:, a:b], bank[3 * (n % 2) + j][:, 0:TJ], ACT.Copy, scale=IWS)\
                           .then_inc(S("hc"), 1)
            elif kind == 1:
                @block.vector
                def _(dve):
                    for j in range(NJ):
                        a, b = third(j)
                        arrived_third(dve, j)
                        dve.wait_ge(S("hc"), 3 * c + j + 1)
                        if c >= 2:
                            dve.wait_ge(S("tail_mm"), c - 1)
                        dve.scalar_tensor_tensor(out=uc[:, c % 2, 2 + a:2 + b], in0=bank[3 * (n % 2) + j][:, 0:TJ],
                                                 scalar=IWS, in1=hc[:, a:b], op0=ALU.mult, op1=ALU.mult)\
                           .then_inc(S("uc"), 1)
                    dve.wait_ge(S("uc"), 3 * c + 3)
                    if c >= 1:
                        dve.wait_ge(S("ci"), 3 * c)
                    sd = stc[:, c, :].rearrange("p (b j) -> p j b", j=2)
                    u = uc[:, c % 2, :]
                    dve.tensor_scalar(yc[:, 0:SEQ], u[:, 2:2 + SEQ], W[:, 2, c:c + 1], None, ALU.mult)\
                       .then_inc(S("taps"), 1)
                    dve.tensor_scalar(yc[:, SEQ:T], u[:, 2 + SEQ:2 + T], W[:, 2, c:c + 1], None, ALU.mult)\
                       .then_inc(S("taps"), 1)
                    dve.wait_ge(S("taps"), 6 * c + 2)
                    dve.scalar_tensor_tensor(out=yc[:, 0:SEQ], in0=u[:, 1:1 + SEQ], scalar=W[:, 1, c:c + 1],
                                             in1=yc[:, 0:SEQ], op0=ALU.mult, op1=ALU.add).then_inc(S("taps"), 1)
                    dve.scalar_tensor_tensor(out=yc[:, SEQ:T], in0=sd[:, 1, :], scalar=W[:, 1, c:c + 1],
                                             in1=yc[:, SEQ:T], op0=ALU.mult, op1=ALU.add).then_inc(S("taps"), 1)
                    dve.wait_ge(S("taps"), 6 * c + 4)
                    dve.scalar_tensor_tensor(out=yc[:, 0:SEQ], in0=u[:, 0:SEQ], scalar=W[:, 0, c:c + 1],
                                             in1=yc[:, 0:SEQ], op0=ALU.mult, op1=ALU.add).then_inc(S("taps"), 1)
                    dve.scalar_tensor_tensor(out=yc[:, SEQ:T], in0=sd[:, 0, :], scalar=W[:, 0, c:c + 1],
                                             in1=yc[:, SEQ:T], op0=ALU.mult, op1=ALU.add).then_inc(S("taps"), 1)
                    dve.wait_ge(S("taps"), 6 * c + 6)
            else:
                @block.tensor
                def _(pe):
                    pe.wait_ge(S("uc"), 3 * c + 3)
                    pe.transpose(bank[6][0:2 + NDEC, c * P:(c + 1) * P], uc[:, c % 2, SEQ:2 + T], const("ident"))\
                      .then_inc(S("tail_mm"), 1)

                @block.vector
                def _(dve):
                    for j in range(NJ):
                        a, b = third(j)
                        arrived_third(dve, j)
                        if c >= 1:
                            dve.wait_ge(S("ci_lo"), 3 * c - 2 + j)
                        dve.scalar_tensor_tensor(out=ci[:, a:b], in0=bank[3 * (n % 2) + j][:, 0:TJ], scalar=IWS,
                                                 in1=yc[:, a:b], op0=ALU.mult, op1=ALU.mult).then_inc(S("ci"), 1)

                @block.scalar
                def _(act):
                    for j in range(NJ):
                        a, b = third(j)
                        act.wait_ge(S("ci"), 3 * c + j + 1)
                        act.activation(cihi[:, c, a:b], ci[:, a:b], ACT.Copy).then_inc(S("ci_hi"), 1)

                @block.vector
                def _(dve):
                    for j in range(NJ):
                        a, b = third(j)
                        dve.wait_ge(S("ci_hi"), 3 * c + j + 1)
                        dve.tensor_tensor(cilo[:, c, a:b], ci[:, a:b], cihi[:, c, a:b], ALU.subtract)\
                           .then_inc(S("ci_lo"), 1)

        @block.vector
        def _(dve):
            dve.wait_ge(S("tail_mm"), KC)
            dve.tensor_copy(tail[:], bank[6][0:2 + NDEC, :]).then_inc(S("tail"), 1)

        @block.scalar
        def _(act):
            act.wait_ge(S("tail"), 1)
            act.dma_start(O["conv_prompt"][0, 0], tail[0:2]).then_inc(S("conv_out"), 16)
            act.dma_start(O["conv_sample"][0][:, 1, :], tail[2:2 + NDEC]).then_inc(S("conv_out"), 16)
        count("mod_done", LATE)
        out_sems.extend([("shifts", 32), ("conv_out", 32)])

        cursor[0] = late_at + 0
        sgm = place("sgm", [P, NJ, TJ], F32)
        mm = place("mm", [P, 2, NJ, TJ], F32)
        assert cursor[0] <= late_at + 4 * (4 * T + 4)

        @block.sync
        def _(sp):
            with sp.Fori(0, KD) as i:
                for v in range(4):
                    if v % 2 == 0:
                        src = w_in[:, bass.ds(i * P + (MERGE0 + v // 2 * D), P)].rearrange("(k p) n -> p k n", p=P)
                        load_slab(sp, i * 4 + (smerge + v), v, src, KD)
                    else:
                        w = (I["w_attn_up"] if v == 1 else I["w_conv_out"])[0]
                        load_slab(sp, i * 4 + (smerge + v), v,
                                  w[:, bass.ds(i * P, P)].rearrange("(k p) n -> p k n", p=P), KC)
            with sp.Fori(0, KD // 4) as i:
                for v in range(4):
                    load_slab(sp, i * 4 + (sout + v), v,
                              I["w_out"][0][:, bass.ds(i * (4 * P) + v * P, P)].rearrange("(k p) n -> p k n", p=P), KD)

        @block.gpsimd
        def _(pool):
            with pool.Fori(0, KD) as i:
                for v in range(4):
                    split_slab(pool, smerge, i * 4, v, (KD if v % 2 == 0 else KC) * P)
            with pool.Fori(0, KD // 4) as i:
                for v in range(4):
                    split_slab(pool, sout, i * 4, v, KD * P)

        ysq0, y0, acc0, group0 = at("ysq"), at("y"), at("acc_done"), at("group")

        @block.tensor
        def _(pe):
            pe.wait_ge(S("uc"), 3 * KC)
            pe.wait_ge(S("dp"), 22)
            pe.wait_ge(S("o_lo"), o_ready)
            pe.wait_ge(S("ci_lo"), 3 * KC)
            with pe.Fori(0, KD) as i:
                for v in range(4):
                    s = i * 4 + (smerge + v)
                    nk = KD if v % 2 == 0 else KC
                    x1, x2 = ((ahi, alo), (oahi, oalo), (ahi, alo), (cihi, cilo))[v]
                    w1, w2 = slab_parts(v, nk)
                    pe.wait_ge(slab_split, s + 1)
                    for j in range(NJ):
                        a, b = third(j)
                        pe.wait_ge(S("mg_sig" if v % 2 == 0 else "mg_mul"), i * 6 + (v // 2 * 3 + j + 1))
                        for k in range(nk):
                            last = product(pe, bank[j + 3 * (v % 2)][:, 0:TJ], w1[:, k, :], w2[:, k, :], x1[:, k, a:b],
                                           x2[:, k, a:b], k == 0, k == nk - 1)
                        last.then_inc(S("mg_mm") if j < 2 else slab_used, 1)
            pe.wait_ge(S("mg_sig"), 3 + 6 * KD)
            pe.wait_ge(S("mg_mul"), 3 + 6 * KD)

            def output_chunks(i):
                for v in range(4):
                    w1, w2 = slab_parts(v, KD)
                    tail_ = i == KD // 4 - 1 and v == 3
                    pe.wait_ge(slab_split, lin(i, 4, sout + v + 1))
                    for j in range(NJ):
                        a, b = third(j)
                        pe.wait_ge(S("mg_lo"), 3 + NJ * (KD - 1) + j + 1)
                        pe.wait_ge(S("ysq"), lin(i, 12, ysq0 + 3 * v + j + 1))
                        for k in range(KD):
                            last = product(pe, bank[3 * (v % 2) + j][:, 0:TJ], w1[:, k, :], w2[:, k, :], mhi[:, k, a:b],
                                           mlo[:, k, a:b], k == 0, k == KD - 1)
                        last.then_inc(S("group") if j < 2 else slab_used, 1)
                        if tail_ and j >= 1:
                            y_mean(pe, j - 1, acc0 + NJ * KD + j)

            looped(pe, output_chunks, KD // 4, last=1)

        @block.scalar
        def _(act):
            act.wait_ge(S("ci_lo"), 3 * KC)
            act.sem_inc(S("mg_sig"), 3)
            with act.Fori(0, KD) as i:
                for half in range(2):
                    for j in range(NJ):
                        a, b = third(j)
                        if j < 2:
                            act.wait_ge(S("mg_mm"), i * 8 + (4 * half + j + 1))
                        else:
                            act.wait_ge(slab_used, i * 4 + (smerge + 2 * half + 1))
                        act.wait_ge(S("mg_mul"), i * 6 + (3 * half + j + 1))
                        act.activation(sgm[:, j, :], bank[j][:, 0:TJ], ACT.Sigmoid, scale=IWS).then_inc(S("mg_sig"), 1)
                for j in range(NJ):
                    a, b = third(j)
                    act.wait_ge(S("mg_add"), i * 3 + (j + 1))
                    act.activation(mhi[:, bass.ds(i, 1), a:b], mm[:, 0, j, :].unsqueeze(1), ACT.Copy)\
                       .then_inc(S("mg_hi"), 1)
            act.sem_inc(S("ysq"), 6)
        @block.vector
        def _(dve):
            dve.wait_ge(S("ci_lo"), 3 * KC)
            dve.sem_inc(S("mg_mul"), 3)
            dve.sem_inc(S("mg_lo"), 3)
            with dve.Fori(0, KD) as i:
                for half in range(2):
                    for j in range(NJ):
                        if j < 2:
                            dve.wait_ge(S("mg_mm"), i * 8 + (4 * half + 2 + j + 1))
                        else:
                            dve.wait_ge(slab_used, i * 4 + (smerge + 2 * half + 2))
                        dve.wait_ge(S("mg_sig"), i * 6 + (3 + 3 * half + j + 1))
                        dve.wait_ge(S("mg_lo"), i * 3 + (j + 1))
                        dve.scalar_tensor_tensor(out=mm[:, half, j, :], in0=bank[3 + j][:, 0:TJ], scalar=IWS,
                                                 in1=sgm[:, j, :], op0=ALU.mult, op1=ALU.mult).then_inc(S("mg_mul"), 1)
                for j in range(NJ):
                    dve.wait_ge(S("mg_mul"), i * 6 + (3 + 3 + j + 1))
                    dve.tensor_tensor(mm[:, 0, j, :], mm[:, 0, j, :], mm[:, 1, j, :], ALU.add).then_inc(S("mg_add"), 1)
                for j in range(NJ):
                    a, b = third(j)
                    dve.wait_ge(S("mg_hi"), i * 3 + (j + 1))
                    dve.tensor_tensor(mlo[:, bass.ds(i, 1), a:b], mm[:, 0, j, :].unsqueeze(1),
                                      mhi[:, bass.ds(i, 1), a:b], ALU.subtract).then_inc(S("mg_lo"), 1)
            dve.wait_ge(S("conv_out"), 32)
            for j in range(NJ):
                dve.memset(acc[:, j, :], 0.0).then_inc(S("acc_done"), 1)

        vec = gate_values(1)

        def take_y(act, i, v, j):
            if j < 2:
                act.wait_ge(S("group"), lin(i, 8, group0 + 2 * v + j + 1))
            else:
                act.wait_ge(slab_used, lin(i, 4, sout + v + 1))
            y_chunk(act, 1, vec, lin(i, 4, v), j, bank[3 * (v % 2) + j])
            act.wait_ge(S("acc_done"), lin(i, 12, acc0 + 3 * v + j + 1))
            act.activation(sq[:, j, :], bank[3 * (v % 2) + j][:, 0:TJ], ACT.Square, scale=IWS).then_inc(S("ysq"), 1)

        def add_square(dve, i, v, j):
            m = 3 * v + j
            dve.wait_ge(S("ysq"), lin(i, 12, ysq0 + 6 + m + 1))
            dve.wait_ge(S("acc_done"), lin(i, 12, acc0 + m + 1))
            dve.tensor_tensor(acc[:, j, :], acc[:, j, :], sq[:, j, :], ALU.add).then_inc(S("acc_done"), 1)

        @block.scalar
        def _(act):
            def output_chunks(i):
                for v in range(4):
                    for j in range(NJ):
                        if not (i == KD // 4 - 1 and v == 3 and j == 2):
                            take_y(act, i, v, j)

            looped(act, output_chunks, KD // 4, last=1)

        @block.vector
        def _(dve):
            def output_chunks(i):
                for v in range(4):
                    for j in range(NJ):
                        if not (i == KD // 4 - 1 and v == 3 and j == 2):
                            add_square(dve, i, v, j)

            looped(dve, output_chunks, KD // 4, last=1)

        count("group", 2 * KD)
        count("ysq", 6 + NJ * KD)
        count("y", NJ * KD)
        count("acc_done", NJ + NJ * KD)
        return out_sems, {"acc": at("acc_done"), "act": lambda act: take_y(act, KD // 4 - 1, 3, 2),
                          "dve": lambda dve: add_square(dve, KD // 4 - 1, 3, 2)}

    total["slab"] = NSTART

    def x_loaded(eng, j):
        eng.wait_ge(S("rows_a"), min(TT + 1, (third(j)[1] - 1) // P + 1))
        eng.wait_ge(S("rows_b"), min(TT + 1, (third(j)[1] - 1) // P + 1))

    a_ready = boundary(None, 0, x_loaded)
    tail = ffn(0, 0, a_ready, True)
    a_ready = boundary(0, 1, tail=tail)
    out_sems, tail = mixer(a_ready)
    a_ready = boundary(1, 2, tail=tail)
    tail = ffn(1, 2, a_ready, False)
    boundary(2, None, tail=tail)

    @block.sync
    def _(sp):
        for name, value in out_sems:
            sp.wait_ge(S(name), value)

    write_out()
    block_cm.__exit__(None, None, None)


_INS = ["x_prompt", "x_sample", "c_prompt", "c_sample", "cache_cmp_kv", "cache_slc_kv", "state_win_kv", "state_conv",
        "page_table", "w_ada", "b_ada", "g_norm", "w_ffn_gu", "w_ffn_down", "w_in", "phi_pe", "phi_w1", "phi_b1",
        "phi_w2", "w_attn_up", "conv_w", "w_conv_out", "w_out"]
_OUTS = [("y_prompt", (1, SEQ, D)), ("y_sample", (NDEC, 1, D)),
         ("cmp_kv_prompt", (1, 1, SEQ, 2, NG, HD)), ("slc_kv_prompt", (1, 1, SEQ, 2, NG, HD)),
         ("win_kv_prompt", (1, 1, WIN, 2, NG, HD)), ("conv_prompt", (1, 1, 2, DCONV)),
         ("cmp_kv_sample", (1, NDEC, 1, 2, NG, HD)), ("slc_kv_sample", (1, NDEC, 1, 2, NG, HD)),
         ("win_kv_sample", (1, NDEC, WIN, 2, NG, HD)), ("conv_sample", (1, NDEC, 2, DCONV))]


def kernel(**inputs):
    import numpy as _np
    import concourse.bacc as _bacc
    from concourse import mybir as _mybir
    from concourse.bass_utils import run_bass_kernel_spmd as _run

    nc = _bacc.Bacc("TRN2", target_bir_lowering=False, num_devices=1)
    arrays, ins, outs = {}, {}, {}
    made = {"consts": shape_constants()[0], "masks": mask_constants()}
    for name in _INS + list(made):
        a = made[name] if name in made else _np.ascontiguousarray(inputs[name])
        arrays[f"in_{name}_dram"] = a
        ins[name] = nc.dram_tensor(f"in_{name}_dram", a.shape, _mybir.dt.from_np(a.dtype), kind="ExternalInput").ap()
    for name, shape in _OUTS:
        outs[name] = nc.dram_tensor(f"out_{name}_dram", shape, _mybir.dt.float32, kind="ExternalOutput").ap()
    build_program(nc, ins, outs)
    r = _run(nc, [arrays], core_ids=[0])
    return tuple(r.results[0][f"out_{name}_dram"] for name, _ in _OUTS)
```
